# Optimizing a Trainium2 kernel written in Bass

```python
import jax, jax.numpy as jnp
from jax import lax
import numpy as np
import math

D_MODEL = 1024
BATCH = 1
SEQ = 512
DEPTH = 1

D_MIX = D_MODEL
D_RET = D_MIX // 2
D_POOL = D_MIX - D_RET
RET_HEADS = 8
RET_HEAD_DIM = D_RET // RET_HEADS
RET_CHUNK = 128
ROPE_BASE = 10000.0
POOL_WINDOWS = (2, 4, 8, 16)
POOL_GROUPS = len(POOL_WINDOWS)
POOL_GROUP_DIM = D_POOL // POOL_GROUPS
D_IN_PROJ = 4 * D_RET + D_POOL
N_EXPERTS = 32
TOP_K = 4
D_EXPERT = D_MODEL
SWIGLU_LIMIT = 7.0
SWIGLU_ALPHA = 1.702
PLE_DIM = 256
NORM_EPS = 1e-5
GN_EPS = 1e-5


def rms_norm(x, g):
    xf = x.astype(jnp.float32)
    y = xf * lax.rsqrt(jnp.mean(xf * xf, axis=-1, keepdims=True) + NORM_EPS)
    return (y * g.astype(jnp.float32)).astype(x.dtype)

def rope(x, positions):
    half = x.shape[-1] // 2
    inv_freq = ROPE_BASE ** (-jnp.arange(half, dtype=jnp.float32) / half)
    ang = positions.astype(jnp.float32)[..., None] * inv_freq
    cos = jnp.cos(ang)[:, :, None, :]
    sin = jnp.sin(ang)[:, :, None, :]
    xf = x.astype(jnp.float32)
    x1, x2 = xf[..., :half], xf[..., half:]
    out = jnp.concatenate([x1 * cos - x2 * sin, x2 * cos + x1 * sin], axis=-1)
    return out.astype(x.dtype)

def retention(q, k, v, gn_w):
    B, S, H, d = q.shape
    C = RET_CHUNK
    N = S // C
    log_gamma = jnp.log1p(-jnp.power(2.0, -5.0 - jnp.arange(H, dtype=jnp.float32)))
    qc = q.reshape(B, N, C, H, d)
    kc = (k * (d ** -0.5)).reshape(B, N, C, H, d)
    vc = v.reshape(B, N, C, H, d)
    idx = jnp.arange(C, dtype=jnp.float32)
    rel = idx[:, None] - idx[None, :]
    causal = rel >= 0
    decay = jnp.where(causal[None], jnp.exp(jnp.where(causal, rel, 0.0)[None] * log_gamma[:, None, None]), 0.0)
    scores = jnp.einsum('bnchd,bnmhd->bnhcm', qc, kc) * decay
    intra = jnp.einsum('bnhcm,bnmhd->bnchd', scores, vc)
    zeta = jnp.exp((C - 1 - idx)[None, :] * log_gamma[:, None])
    kv = jnp.einsum('bnmhd,hm,bnmhe->bnhde', kc, zeta, vc)
    chunk_decay = jnp.exp(C * log_gamma)[:, None, None]

    def step(state, kv_i):
        return chunk_decay * state + kv_i, state

    init = jnp.zeros((B, H, d, d), dtype=kv.dtype)
    _, states = lax.scan(step, init, jnp.moveaxis(kv, 1, 0))
    states = jnp.moveaxis(states, 0, 1)
    xi = jnp.exp((idx + 1.0)[None, :] * log_gamma[:, None])
    cross = jnp.einsum('bnchd,bnhde,hc->bnche', qc, states, xi)
    y = (intra + cross).reshape(B, S, H, d).astype(jnp.float32)
    mu = jnp.mean(y, axis=-1, keepdims=True)
    var = jnp.mean(jnp.square(y - mu), axis=-1, keepdims=True)
    y = (y - mu) * lax.rsqrt(var + GN_EPS)
    y = y.reshape(B, S, H * d) * gn_w.astype(jnp.float32)
    return y.astype(q.dtype)

def pool_mixer(u, w_pool, pool_scale):
    B, S, _ = u.shape
    ug = u.reshape(B, S, POOL_GROUPS, POOL_GROUP_DIM).astype(jnp.float32)
    P = jnp.pad(jnp.cumsum(ug, axis=1), ((0, 0), (1, 0), (0, 0), (0, 0)))
    t = jnp.arange(S, dtype=jnp.float32)
    outs = []
    for gi, w in enumerate(POOL_WINDOWS):
        Pg = P[:, :, gi]
        lag = jnp.pad(Pg, ((0, 0), (w, 0), (0, 0)))[:, :S + 1]
        window_sum = Pg[:, 1:] - lag[:, 1:]
        count = jnp.minimum(t + 1.0, float(w))
        outs.append(window_sum / count[None, :, None] - ug[:, :, gi])
    pooled = jnp.stack(outs, axis=2).astype(u.dtype)
    mixed = jnp.einsum('bsgc,gcd->bsgd', pooled, w_pool)
    return mixed.reshape(B, S, D_POOL) * pool_scale

def moe(hn, router_w, router_b, w_gu, b_gu, w_down, b_down):
    B, S, D = hn.shape
    xt = hn.reshape(-1, D)
    logits = xt.astype(jnp.float32) @ router_w.astype(jnp.float32) + router_b.astype(jnp.float32)
    top_vals, top_idx = lax.top_k(logits, TOP_K)
    gates = jax.nn.softmax(top_vals, axis=-1)
    flat_e = top_idx.reshape(-1)
    order = jnp.argsort(flat_e)
    sorted_e = flat_e[order]
    tok = order // TOP_K
    xs = xt[tok]
    group_sizes = jnp.bincount(flat_e, length=N_EXPERTS).astype(jnp.int32)
    gu = lax.ragged_dot(xs, w_gu, group_sizes) + b_gu[sorted_e]
    gate = jnp.minimum(gu[:, ::2], SWIGLU_LIMIT)
    up = jnp.clip(gu[:, 1::2], -SWIGLU_LIMIT, SWIGLU_LIMIT)
    act = (up + 1.0) * (gate * jax.nn.sigmoid(SWIGLU_ALPHA * gate))
    y = lax.ragged_dot(act.astype(w_down.dtype), w_down, group_sizes) + b_down[sorted_e]
    y = y * gates.reshape(-1)[order][:, None].astype(y.dtype)
    out = jnp.zeros_like(xt).at[tok].add(y.astype(xt.dtype))
    return out.reshape(B, S, D)

def first_inputs(seed: int = 0) -> dict:
    key = jax.random.key(seed)
    ks = jax.random.split(key, 24)
    f32 = jnp.float32
    L = DEPTH

    def nrm(k, shape, scale):
        return jax.random.normal(k, shape, dtype=f32) * scale

    offsets = jax.random.randint(ks[2], (BATCH, 1), 0, 1024, dtype=jnp.int32)
    positions = (jnp.arange(SEQ, dtype=jnp.int32)[None, :] + offsets).astype(jnp.int32)
    return {
        "x": nrm(ks[0], (BATCH, SEQ, D_MODEL), 1.0),
        "p": nrm(ks[1], (DEPTH, BATCH, SEQ, PLE_DIM), 1.0),
        "positions": positions,
        "w_in": nrm(ks[3], (L, D_MODEL, D_IN_PROJ), D_MODEL ** -0.5),
        "w_out": nrm(ks[4], (L, D_MIX, D_MODEL), D_MIX ** -0.5),
        "ret_gn_w": 1.0 + nrm(ks[5], (L, D_RET), 0.02),
        "pool_w": nrm(ks[6], (L, POOL_GROUPS, POOL_GROUP_DIM, POOL_GROUP_DIM), POOL_GROUP_DIM ** -0.5),
        "pool_scale": 1.0 + nrm(ks[7], (L, D_POOL), 0.02),
        "norm_mix_w": 1.0 + nrm(ks[8], (L, D_MODEL), 0.02),
        "norm_moe_w": 1.0 + nrm(ks[9], (L, D_MODEL), 0.02),
        "router_w": nrm(ks[10], (L, D_MODEL, N_EXPERTS), D_MODEL ** -0.5),
        "router_b": nrm(ks[11], (L, N_EXPERTS), 0.01),
        "expert_w_gate_up": nrm(ks[12], (L, N_EXPERTS, D_MODEL, 2 * D_EXPERT), D_MODEL ** -0.5),
        "expert_b_gate_up": nrm(ks[13], (L, N_EXPERTS, 2 * D_EXPERT), 0.02),
        "expert_w_down": nrm(ks[14], (L, N_EXPERTS, D_EXPERT, D_MODEL), D_EXPERT ** -0.5),
        "expert_b_down": nrm(ks[15], (L, N_EXPERTS, D_MODEL), 0.02),
        "norm_ple_w": 1.0 + nrm(ks[16], (L, D_MODEL), 0.02),
        "ple_gate_w": nrm(ks[17], (L, D_MODEL, D_MODEL), D_MODEL ** -0.5),
        "ple_proj_w": nrm(ks[18], (L, PLE_DIM, D_MODEL), PLE_DIM ** -0.5),
        "final_norm_w": 1.0 + nrm(ks[19], (D_MODEL,), 0.02),
    }

def first_block(x, p, positions, w_in, w_out, ret_gn_w, pool_w, pool_scale, norm_mix_w,
              norm_moe_w, router_w, router_b, expert_w_gate_up, expert_b_gate_up,
              expert_w_down, expert_b_down, norm_ple_w, ple_gate_w, ple_proj_w, final_norm_w):
    B, S, _ = x.shape
    h = x
    for l in range(DEPTH):
        hn = rms_norm(h, norm_mix_w[l])
        proj = hn @ w_in[l]
        q = proj[..., 0 * D_RET:1 * D_RET].reshape(B, S, RET_HEADS, RET_HEAD_DIM)
        k = proj[..., 1 * D_RET:2 * D_RET].reshape(B, S, RET_HEADS, RET_HEAD_DIM)
        v = proj[..., 2 * D_RET:3 * D_RET].reshape(B, S, RET_HEADS, RET_HEAD_DIM)
        g = proj[..., 3 * D_RET:4 * D_RET]
        u = proj[..., 4 * D_RET:]
        q = rope(q, positions)
        k = rope(k, positions)
        ret = jax.nn.silu(g) * retention(q, k, v, ret_gn_w[l])
        pool = pool_mixer(u, pool_w[l], pool_scale[l])
        h = h + jnp.concatenate([ret, pool], axis=-1) @ w_out[l]
        h = h + moe(rms_norm(h, norm_moe_w[l]), router_w[l], router_b[l],
                    expert_w_gate_up[l], expert_b_gate_up[l], expert_w_down[l], expert_b_down[l])
        gate = jax.nn.sigmoid(rms_norm(h, norm_ple_w[l]) @ ple_gate_w[l])
        h = h + gate * (p[l] @ ple_proj_w[l])
    return rms_norm(h, final_norm_w)


DEPTH_2 = 2

N_MIXERS = 2
SSM_GROUP = 16
SSM_GROUPS = D_MODEL // SSM_GROUP
SSM_STATE = 64
CONV_WIDTH = 3
FFN_HIDDEN = ((8 * D_MODEL + 3 * 256 - 1) // (3 * 256)) * 256
N_SSM_LAYERS = (DEPTH_2 + 1) // 2
N_CONV_LAYERS = DEPTH_2 // 2
RMS_EPS = 1e-6
DT_MIN = 1e-3
DT_MAX = 1e-1


def rms_norm_2(x, g):
    x32 = x.astype(jnp.float32)
    y = x32 * lax.rsqrt(jnp.mean(x32 * x32, axis=-1, keepdims=True) + RMS_EPS)
    return (y * g.astype(jnp.float32)).astype(x.dtype)

def modulate(h, shift, scale):
    return h * (1.0 + scale) + shift

def _ssm_combine(e1, e2):
    a1r, a1i, b1r, b1i = e1
    a2r, a2i, b2r, b2i = e2
    ar = a2r * a1r - a2i * a1i
    ai = a2r * a1i + a2i * a1r
    br = a2r * b1r - a2i * b1i + b2r
    bi = a2r * b1i + a2i * b1r + b2i
    return (ar, ai, br, bi)

def s5_mixer(h, a_re, a_im, log_step, b_re, b_im, c_re, c_im, d, w_out):
    bsz, seqlen, _ = h.shape
    f32 = jnp.float32
    u = h.astype(f32).reshape(bsz, seqlen, SSM_GROUPS, SSM_GROUP)
    lr = jnp.minimum(a_re.astype(f32), -1e-4)
    li = a_im.astype(f32)
    dt = jnp.exp(log_step.astype(f32))[:, None]
    mag = jnp.exp(lr * dt)
    abr = mag * jnp.cos(li * dt)
    abi = mag * jnp.sin(li * dt)
    den = lr * lr + li * li
    qr = ((abr - 1.0) * lr + abi * li) / den
    qi = (abi * lr - (abr - 1.0) * li) / den
    br, bim = b_re.astype(f32), b_im.astype(f32)
    bbar_re = qr[..., None] * br - qi[..., None] * bim
    bbar_im = qr[..., None] * bim + qi[..., None] * br
    bu_re = jnp.einsum('blgh,gph->blgp', u, bbar_re)
    bu_im = jnp.einsum('blgh,gph->blgp', u, bbar_im)
    a_r = jnp.broadcast_to(abr[None, None], (1, seqlen, SSM_GROUPS, SSM_STATE))
    a_i = jnp.broadcast_to(abi[None, None], (1, seqlen, SSM_GROUPS, SSM_STATE))
    _, _, xr, xi = lax.associative_scan(_ssm_combine, (a_r, a_i, bu_re, bu_im), axis=1)
    y = (jnp.einsum('ghp,blgp->blgh', c_re.astype(f32), xr)
         - jnp.einsum('ghp,blgp->blgh', c_im.astype(f32), xi))
    y = y.reshape(bsz, seqlen, D_MODEL) + d.astype(f32) * h.astype(f32)
    y = jax.nn.gelu(y).astype(h.dtype)
    val, gate = jnp.split(y @ w_out, 2, axis=-1)
    return val * jax.nn.sigmoid(gate)

def short_conv_mixer(h, w_in, conv_w, w_out):
    bg, cg, v = jnp.split(h @ w_in, 3, axis=-1)
    cv = cg * v
    conv = lax.conv_general_dilated(
        cv, conv_w[:, None, :].astype(cv.dtype), window_strides=(1,),
        padding=[(CONV_WIDTH - 1, 0)], dimension_numbers=('NWC', 'WIO', 'NWC'),
        feature_group_count=D_MODEL)
    return (bg * conv) @ w_out

def swiglu(h, w_in, w_out):
    g, u = jnp.split(h @ w_in, 2, axis=-1)
    return (jax.nn.silu(g) * u) @ w_out

def second_inputs(seed: int = 0) -> dict:
    key = jax.random.key(seed)
    ks = jax.random.split(key, 24)
    D, G, P, H, F = D_MODEL, SSM_GROUPS, SSM_STATE, SSM_GROUP, FFN_HIDDEN
    nrm = jax.random.normal
    x = nrm(ks[0], (BATCH, SEQ, D), jnp.float32)
    c = nrm(ks[1], (BATCH, D), jnp.float32)
    norm1_g = 1.0 + 0.02 * nrm(ks[2], (DEPTH_2, D), jnp.float32)
    norm2_g = 1.0 + 0.02 * nrm(ks[3], (DEPTH_2, D), jnp.float32)
    w_ada = 0.5 * D ** -0.5 * nrm(ks[4], (DEPTH_2, D, 6 * D), jnp.float32)
    b_ada = 0.01 * nrm(ks[5], (DEPTH_2, 6 * D), jnp.float32)
    n_idx = jnp.arange(P, dtype=jnp.float32)
    ssm_a_re = -0.5 + 0.01 * nrm(ks[6], (N_SSM_LAYERS, G, P), jnp.float32)
    ssm_a_im = math.pi * n_idx + 0.01 * nrm(ks[7], (N_SSM_LAYERS, G, P), jnp.float32)
    ssm_log_step = jax.random.uniform(ks[8], (N_SSM_LAYERS, G), jnp.float32,
                                      math.log(DT_MIN), math.log(DT_MAX))
    ssm_b_re = (2 * H) ** -0.5 * nrm(ks[9], (N_SSM_LAYERS, G, P, H), jnp.float32)
    ssm_b_im = (2 * H) ** -0.5 * nrm(ks[10], (N_SSM_LAYERS, G, P, H), jnp.float32)
    ssm_c_re = (2 * P) ** -0.5 * nrm(ks[11], (N_SSM_LAYERS, G, H, P), jnp.float32)
    ssm_c_im = (2 * P) ** -0.5 * nrm(ks[12], (N_SSM_LAYERS, G, H, P), jnp.float32)
    ssm_d = nrm(ks[13], (N_SSM_LAYERS, D), jnp.float32)
    ssm_w_out = D ** -0.5 * nrm(ks[14], (N_SSM_LAYERS, D, 2 * D), jnp.float32)
    conv_w_in = D ** -0.5 * nrm(ks[15], (N_CONV_LAYERS, D, 3 * D), jnp.float32)
    conv_w = CONV_WIDTH ** -0.5 * nrm(ks[16], (N_CONV_LAYERS, CONV_WIDTH, D), jnp.float32)
    conv_w_out = D ** -0.5 * nrm(ks[17], (N_CONV_LAYERS, D, D), jnp.float32)
    w_ffn_in = D ** -0.5 * nrm(ks[18], (DEPTH_2, D, 2 * F), jnp.float32)
    w_ffn_out = F ** -0.5 * nrm(ks[19], (DEPTH_2, F, D), jnp.float32)
    final_g = 1.0 + 0.02 * nrm(ks[20], (D,), jnp.float32)
    return {"x": x, "c": c, "norm1_g": norm1_g, "norm2_g": norm2_g,
            "w_ada": w_ada, "b_ada": b_ada,
            "ssm_a_re": ssm_a_re, "ssm_a_im": ssm_a_im, "ssm_log_step": ssm_log_step,
            "ssm_b_re": ssm_b_re, "ssm_b_im": ssm_b_im,
            "ssm_c_re": ssm_c_re, "ssm_c_im": ssm_c_im,
            "ssm_d": ssm_d, "ssm_w_out": ssm_w_out,
            "conv_w_in": conv_w_in, "conv_w": conv_w, "conv_w_out": conv_w_out,
            "w_ffn_in": w_ffn_in, "w_ffn_out": w_ffn_out, "final_g": final_g}

def second_block(x, c, norm1_g, norm2_g, w_ada, b_ada,
              ssm_a_re, ssm_a_im, ssm_log_step, ssm_b_re, ssm_b_im,
              ssm_c_re, ssm_c_im, ssm_d, ssm_w_out,
              conv_w_in, conv_w, conv_w_out,
              w_ffn_in, w_ffn_out, final_g):
    c_act = jax.nn.silu(c)
    for i in range(DEPTH_2):
        mods = c_act @ w_ada[i] + b_ada[i]
        sh1, sc1, g1, sh2, sc2, g2 = [m[:, None, :] for m in jnp.split(mods, 6, axis=-1)]
        h = modulate(rms_norm_2(x, norm1_g[i]), sh1, sc1)
        j = i // N_MIXERS
        if i % N_MIXERS == 0:
            mix = s5_mixer(h, ssm_a_re[j], ssm_a_im[j], ssm_log_step[j],
                           ssm_b_re[j], ssm_b_im[j], ssm_c_re[j], ssm_c_im[j],
                           ssm_d[j], ssm_w_out[j])
        else:
            mix = short_conv_mixer(h, conv_w_in[j], conv_w[j], conv_w_out[j])
        x = x + g1 * mix
        h = modulate(rms_norm_2(x, norm2_g[i]), sh2, sc2)
        x = x + g2 * swiglu(h, w_ffn_in[i], w_ffn_out[i])
    return rms_norm_2(x, final_g)


def setup_inputs(seed=0):
    out = dict(first_inputs(seed))
    for name, value in second_inputs(seed + 1).items():
        if name != "x":
            out[name + "_2"] = value
    return out


def reference(
    x, p, positions, w_in, w_out, ret_gn_w, pool_w, pool_scale, norm_mix_w, norm_moe_w,
    router_w, router_b, expert_w_gate_up, expert_b_gate_up, expert_w_down, expert_b_down,
    norm_ple_w, ple_gate_w, ple_proj_w, final_norm_w, c_2, norm1_g_2, norm2_g_2, w_ada_2,
    b_ada_2, ssm_a_re_2, ssm_a_im_2, ssm_log_step_2, ssm_b_re_2, ssm_b_im_2, ssm_c_re_2,
    ssm_c_im_2, ssm_d_2, ssm_w_out_2, conv_w_in_2, conv_w_2, conv_w_out_2, w_ffn_in_2,
    w_ffn_out_2, final_g_2,
):
    x = first_block(
        x, p, positions, w_in, w_out, ret_gn_w, pool_w, pool_scale, norm_mix_w, norm_moe_w,
        router_w, router_b, expert_w_gate_up, expert_b_gate_up, expert_w_down, expert_b_down,
        norm_ple_w, ple_gate_w, ple_proj_w, final_norm_w,
    )
    return second_block(
        x, c_2, norm1_g_2, norm2_g_2, w_ada_2, b_ada_2, ssm_a_re_2, ssm_a_im_2, ssm_log_step_2,
        ssm_b_re_2, ssm_b_im_2, ssm_c_re_2, ssm_c_im_2, ssm_d_2, ssm_w_out_2, conv_w_in_2,
        conv_w_2, conv_w_out_2, w_ffn_in_2, w_ffn_out_2, final_g_2,
    )


_drawn_inputs = setup_inputs


def setup_inputs(seed=0):
    import zlib

    import numpy as np

    out = dict(_drawn_inputs(seed))
    spreads = {}
    factors = {'expert_b_gate_up': 5.682,
     'expert_b_down': 6.529,
     'norm_ple_w': 8.0,
     'norm1_g_2': 4.492,
     'norm2_g_2': 6.459,
     'b_ada_2': 2.951,
     'ssm_a_re_2': 64.0,
     'ssm_a_im_2': 50.216,
     'ssm_log_step_2': 59.088,
     'ssm_b_re_2': 64.0,
     'ssm_b_im_2': 64.0,
     'ssm_c_re_2': 64.0,
     'ssm_c_im_2': 64.0,
     'final_g_2': 7.977}
    for name, (base, spread) in spreads.items():
        noise = np.random.default_rng([zlib.crc32(name.encode()), seed]).standard_normal(out[name].shape)
        drawn = base * np.exp(spread * noise) if base else spread * noise
        out[name] = __import__('jax').numpy.asarray(drawn.astype(out[name].dtype))
    for name, factor in factors.items():
        out[name] = (out[name] * factor).astype(out[name].dtype)
    return out
```

```python
from contextlib import ExitStack

import concourse.bass as bass
from concourse import mybir

F32 = mybir.dt.float32
I32 = mybir.dt.int32
U32 = mybir.dt.uint32
ALU = mybir.AluOpType
ACT = mybir.ActivationFunctionType
AXX = mybir.AxisListType.X

P = 128
S = 512
D = 1024
NT = S // P
KD = D // P
HEADS, HD = 8, 64
RET = HEADS * HD
NPROJ = 4 * RET + (D - RET)
WINDOWS = (2, 4, 8, 16)
E, TOPK = 32, 4
MAX_EXTRA = S * TOPK // P - 1
TILES = E + MAX_EXTRA + 1
PLE = 256
G, GC, NS = 64, 16, 64
CH = P // GC
NC = S // CH
GP = G // 2
FF = 2816
KF = FF // P
EPS1, EPS2 = 1e-5, 1e-6
LIMIT, ALPHA = 7.0, 1.702
PI = 3.14159265358979
TWO_PI = (6.28125, 1.93500518798828125e-3, 3.019915981956753e-7)
MAGIC = 12582912.0
PI_IN = 3.1415925
RSQRT_SEED = 0x5F3759DF
GELU_C, GELU_S = 0.044715, 1.5957691216057308

VEC = {}
_at = 0
for _name, _rows in (("norm_mix_w", 8), ("ret_gn_w", 4), ("pool_scale", 4), ("norm_ple_w", 8),
                     ("norm1_g_2", 16), ("norm2_g_2", 16), ("ssm_d_2", 8), ("conv_w_2", 24),
                     ("final_g_2", 8), ("c_2", 8)):
    VEC[_name] = (_at, _rows)
    _at += _rows
NVEC = _at
NADA = 96
ADA_N = 768
ADA_C = 6 * D // ADA_N

CONST = {}
_at = 0
for _name, _cols in (("ident", P), ("ones", P), ("tri", P), ("iota", 32), ("freq", 32), ("token", NT),
                     ("chunk", NC)):
    CONST[_name] = (_at, _at + _cols)
    _at += _cols
NCONST = _at


COLS_XT = KD + KD + 4 + KD + 2 + KD + KD
SCORE_AT = (0, 512, 896, 1152)
MASK_AT = NT * E + 2 * NT * TOPK * E
COLS_OUT = COLS_XT + 2 * (GP // 4)
LINEAR = ("glu", "fin0", "fout0", "cin", "cout", "fin1", "fout1")


class Steps:

    def __init__(self, eng, sem):
        self.eng, self.sem, self.n, self.off = eng, sem, 0, 0

    def __call__(self, ins):
        ins.then_inc(self.sem, 1)
        self.n += 1
        self.eng.wait_ge(self.sem, self.n + self.off)


def program(nc, a, out):
    with ExitStack() as ctx:
        def sb(name, shape, dt=F32):
            return ctx.enter_context(nc.sbuf_tensor(name, shape, dt))

        def sem(name):
            return ctx.enter_context(nc.semaphore(name))

        ps = [ctx.enter_context(nc.psum_tensor(f"bank{i}", [P, 512], F32)) for i in range(8)]

        ring = sb("ring", [P, 24576])
        rows = sb("rows", [P, NT, D])
        nat = sb("nat", [P, 4096])
        ca = sb("ca", [P, KD, S])
        cb = sb("cb", [P, 4096])
        work = sb("work", [P, 10240])
        const = sb("const", [P, NCONST])
        vec = sb("vec", [P, NVEC + NADA])
        mods = sb("mods", [P, 2, 48])
        scale1 = sb("scale1", [P, 2, 16])
        cact = sb("cact", [P, 8])
        sm = sb("sm", [P, 640])
        smi = sb("smi", [P, 216], I32)
        ident, ones, tri, iota, freq, token, chunk = (
            const[:, x:y] for x, y in CONST.values())

        def vcol(name, k):
            return vec[:, VEC[name][0] + k:VEC[name][0] + k + 1]

        nat3 = nat[:].rearrange("p (i d) -> p i d", i=NT)
        cb3 = cb[:].rearrange("p (k t) -> p k t", k=KD)

        w_in_sb = [ring[:, n * 4096:(n + 1) * 4096].rearrange("p (k n) -> p k n", k=KD) for n in (0, 1, 2, 0, 1)]
        w_out_sb = [ring[:, n * 4096:(n + 1) * 4096].rearrange("p (k n) -> p k n", k=KD) for n in (2, 0)]
        pooled = [ring[:, 12288 + 512 * b:12288 + 512 * (b + 1)] for b in range(2)]
        decay = ring[:, 16384:20480].rearrange("p (h t) -> p h t", h=HEADS)
        band = ring[:, 20480:22016].rearrange("p (g v t) -> p g v t", g=4, v=3)
        scr_s = [ring[:, 22016 + 1280 * b:22016 + 1280 * (b + 1)] for b in range(2)]
        pool_w_sb = ring[:, 13312:13824].rearrange("p (g d) -> p g d", g=4)
        trig = ring[:, 13824:13824 + 1024].rearrange("p (v i f) -> p v i f", v=8, i=NT)
        proj = work[:].rearrange("p (i n) -> p i n", i=NT)
        ada_acc = [cb[:, 0:ADA_N], work[:, 6144:6144 + ADA_N]]
        ada_w = [[r[:, ADA_N * (b + 1):ADA_N * (b + 2)] for b in range(3)] for r in (cb[:], work[:, 6144:10240])]
        vec_rows, ada_rows = ca[:, 0, 0:P], ca[:, 0, P:2 * P]
        qkr = nat[:].rearrange("p (i h two f) -> p i h two f", i=NT, h=2 * HEADS, two=2)
        s5r = nat[0:GP, :].rearrange("p (v n) -> p v n", n=P)
        rope_t = [ring[:, 14848 + 512 * b:15360 + 512 * b].rearrange("p (h f) -> p h f", f=32) for b in range(2)]
        ret_y = nat[:, 0:2048].rearrange("p (n e) -> p n e", e=HD)
        ret_sq = nat[:, 2048:4096].rearrange("p (n e) -> p n e", e=HD)
        silu_g = ca[:, 0:4, :]
        route = work[:, 5120:10240]
        c_rows = [ring[:, 3072 + 1024 * r:4096 + 1024 * r].rearrange("p (t two n) -> p t two n", t=8, two=2) for r in range(2)]
        b_in = [ring[:, 512 * r:512 * (r + 1)].rearrange("p (j h) -> p j h", j=GP) for r in range(2)]
        s5_ta = [ring[:, 1024 + 512 * r:1536 + 512 * r].rearrange("p (j h) -> p j h", j=GP) for r in range(2)]
        s5_tb = [ring[:, 2048 + 512 * r:2560 + 512 * r].rearrange("p (j h) -> p j h", j=GP) for r in range(2)]
        k_sb = work[:, 8192:9216].rearrange("p (two j h) -> p two j h", two=2, j=GP)
        k_zero = work[0:GC, 9216:9216 + (CH - 1) * GC]

        slot = [ring[:, 2048 * s:2048 * (s + 1)].rearrange("p (k n) -> p k n", k=2) for s in range(12)]
        bias_gu = work[:, 0:2048]
        bias_dn = work[:, 2048:3072]
        xs = work[:, 3072:4096]
        xst = work[:, 4096:5120].rearrange("p (k t) -> p k t", k=KD)
        t_g = [work[:, 5120 + 512 * h:5632 + 512 * h] for h in range(2)]
        t_u = [work[:, 6144 + 512 * h:6656 + 512 * h] for h in range(2)]
        t_s = [work[:, 7168 + 512 * h:7680 + 512 * h] for h in range(2)]
        act_n = [work[:, 8192 + 512 * h:8704 + 512 * h] for h in range(2)]
        act_t = [work[:, 9216 + 512 * h:9728 + 512 * h].rearrange("p (k t) -> p k t", k=4) for h in range(2)]
        y_sb = cb[:, 0:1024]
        rw_sb = cb[:, 1024:1280].rearrange("p (k e) -> p k e", k=KD)
        norm_bc = cb[:, 2048:3072]
        fnorm_bc = cb[:, 3072:4096]
        rb_bc = cb[:, 1280:1312]
        got = [ring[:, 1024 * n:1024 * (n + 1)] for n in range(8)] + \
              [ring[:, 16384 + 1024 * n:16384 + 1024 * (n + 1)] for n in range(8)]

        ple_w_sb = [work[:, 4096 * n:4096 * (n + 1)].rearrange("p (k n) -> p k n", k=KD) for n in range(2)]
        ple_p_sb = work[:, 8192:10240].rearrange("p (k n) -> p k n", k=2)
        p_rows = cb[:, 0:1024].rearrange("p (i d) -> p i d", i=NT)
        p_cols = cb[:, 1024:2048].rearrange("p (k t) -> p k t", k=2)
        gate_sb = [nat[:, 512 * b:512 * (b + 1)] for b in range(8)]

        m_w = [ring[:, 4096 * r:4096 * (r + 1)].rearrange("p (j m) -> p j m", j=GP) for r in range(2)]
        m_t = ring[:, 8192:16384].rearrange("p (g m) -> p g m", g=G)
        m_b = [ring[:, 8192 + 4096 * r:12288 + 4096 * r].rearrange("p (j s h) -> p j s h", j=GP, s=CH) for r in range(2)]
        m_c = [ring[:, 16384 + 4096 * r:20480 + 4096 * r].rearrange("p (j s h) -> p j s h", j=GP, s=CH) for r in range(2)]
        xt = work[:, 0:4096].rearrange("p (k t) -> p k t", k=KD)
        u_sb = work[:, 4096:8192].rearrange("p (g c) -> p g c", g=G)
        mag_sb = work[:, 8192:10240]
        rot_c = rows[:, 0:2, :].rearrange("p i d -> p (i d)")
        rot_s = rows[:, 2:4, :].rearrange("p i d -> p (i d)")
        z_re, z_im = cb[:, 0:2048], cb[:, 2048:4096]
        tmp1, tmp2 = nat[:, 0:2048], nat[:, 2048:4096]
        x_re = ring[:, 0:2048].rearrange("p (j c) -> p j c", j=GP)
        x_im = ring[:, 2048:4096].rearrange("p (j c) -> p j c", j=GP)
        y_ch = [nat[0:NC, 1024 * b:1024 * (b + 1)].rearrange("c (s h) -> c s h", s=CH) for b in range(2)]
        par = sb("par", [P, 6, GP])
        s5c = [cb[:, 2048 + 512 * r:2560 + 512 * r].rearrange("p (j h) -> p j h", j=GP) for r in range(2)]

        glu_sb = [rows[:, 2 * b:2 * b + 2, :].rearrange("p i (j n) -> p i j n", n=P) for b in range(2)]
        cin_sb = [r[:, 0:3072].rearrange("p (v k n) -> p v k n", v=3, k=KD)
                  for r in (nat[:], rows[:].rearrange("p i d -> p (i d)"))]
        cout_sb = [work[:, 4096 + 1024 * b:5120 + 1024 * b].rearrange("p (v k n) -> p v k n", v=1, k=KD) for b in range(2)]
        f_act = ring[:, 0:KF * S].rearrange("p (f t) -> p f t", f=KF)
        fin_sb = [ring[:, 11264 + 2048 * b:13312 + 2048 * b].rearrange("p (v k n) -> p v k n", v=2, k=KD) for b in range(2)]
        fout_sb = [ring[:, 15360 + KF * P * b:15360 + KF * P * (b + 1)].rearrange("p (v k n) -> p v k n", v=1, k=KF) for b in range(2)]
        scratch = ring[:, 20992:24576]
        sig_sb = [scratch[:, 512 * b:512 * (b + 1)] for b in range(2)]
        lin_t = [scratch[:, 1024 + 512 * b:1536 + 512 * b] for b in range(2)]
        conv_x = scratch[:, 2048:2048 + 640].rearrange("p (s c) -> p s c", c=NC)
        n_v = [tmp2[:, 512:1024], scratch[:, 2688:3200]]
        n_y, n_t = tmp2[:, 1024:1536], tmp2[:, 1536:2048]

        hn_dram = nc.dram_tensor("hn_dram", [S, D], F32).ap()
        y_dram = nc.dram_tensor("y_dram", [E * P, D], F32).ap()
        y_more = nc.dram_tensor("y_more", [MAX_EXTRA * P, D], F32).ap()
        table = nc.dram_tensor("slot_table", [P * TILES, 1], I32).ap()
        k_dram = nc.dram_tensor("k_dram", [GC, G, 2 * CH, GC], F32).ap()

        s_const_in = sem("const_in")
        s_x_in = sem("x_in")
        s_vec_in = sem("vec_in")
        s_pos_in = sem("pos_in")
        s_mix_in = [sem(f"mix_in{i}") for i in range(3)]
        s_ret_in = sem("ret_in")
        s_cols_ready = sem("cols_ready")
        s_s5_in = sem("s5_in")
        s_proj_ready = sem("proj_ready")
        s_score_ps = sem("score_ps")
        s_norm_in = sem("norm_in")
        s_slot_in = [sem(f"slot_in{i}") for i in range(12)]
        s_bias_in = sem("bias_in")
        s_gu_ready = sem("gu_ready")
        s_y_ready = sem("y_ready")
        s_slot_free = sem("slot_free")
        s_y_sb = sem("y_sb")
        s_wout_ready = sem("wout_ready")
        s_route_ok = sem("route_ok")
        s_moe_done = sem("moe_done")
        s_ple_in = sem("ple_in")
        s_got_used = sem("got_used")
        s_b_in = sem("b_in")
        s_c_in = sem("c_in")
        s_k_sb = sem("k_sb")
        s_k_out = sem("k_out")
        s_t_in = sem("t_in")
        s_h_ready = sem("h_ready")
        s_u_in = sem("u_in")
        s_lin_in = [[sem(f"{name}_in{b}") for b in range(2)] for name in LINEAR[:4]]
        s_lin_ready = sem("lin_ready")
        s_ada1_used = sem("ada1_used")
        s_ada1_sum = sem("ada1_sum")
        s_ada_in = [sem(f"ada_in{i}") for i in range(3)]
        s_ada1_in = [sem(f"ada1_in{i}") for i in range(3)]
        s_x_state = sem("x_state")
        s_yo_ps = sem("yo_ps")
        s_lin_taken = sem("lin_taken")
        s_cols_taken = sem("cols_taken")
        s_out_done = sem("out_done")
        s_ada_used = sem("ada_used")
        s_table_zero = sem("table_zero")
        s_table_set = sem("table_set")
        s_ids_in = sem("ids_in")
        s_hn_stored = sem("hn_stored")
        s_ids_cur = sem("ids_cur")
        s_xs_in = sem("xs_in")
        s_xt_ready = sem("xt_ready")
        s_got_in = [sem(f"got_in{i}") for i in range(4)]
        s_more_in = sem("more_in")
        s_pool_step = sem("pool_step")
        s_more_done = sem("more_done")
        s_b_ready = sem("b_ready")
        s_pproj_ready = sem("pproj_ready")
        s_sq = sem("sq")
        s_vec_t = sem("vec_t")
        s_vec_ok = sem("vec_ok")
        s_c_sig = sem("c_sig")
        s_proj_taken = sem("proj_taken")
        s_trig_ready = sem("trig_ready")
        s_trig_done = sem("trig_done")
        s_s5_exp = sem("s5_exp")
        s_s5_angle = sem("s5_angle")
        s_s5_fun = sem("s5_fun")
        s_pool_ps = sem("pool_ps")
        s_pool_sb = sem("pool_sb")
        s_mix_ps = sem("mix_ps")
        s_mix_sb = sem("mix_sb")
        s_sil = sem("sil")
        s_y_ps = sem("y_ps")
        s_ret_y = sem("ret_y")
        s_wout_taken = sem("wout_taken")
        s_nat_ready = sem("nat_ready")
        s_gate_d = sem("gate_d")
        s_gate_e = sem("gate_e")
        s_xst_ready = sem("xst_ready")
        s_g_ready = sem("g_ready")
        s_sig_ready = sem("sig_ready")
        s_actt_ps = sem("actt_ps")
        s_actt_ready = sem("actt_ready")
        s_y_stored = sem("y_stored")
        s_more_zero = sem("more_zero")
        s_ct_ps = sem("ct_ps")
        s_ct_sb = sem("ct_sb")
        s_pgate_ready = sem("pgate_ready")
        s_pgate_act = sem("pgate_act")
        s_pproj_taken = sem("pproj_taken")
        s_sq2 = sem("sq2")
        s_hs_ready = sem("hs_ready")
        s_k_ps = sem("k_ps")
        s_rot_ready = sem("rot_ready")
        s_rot_done = sem("rot_done")
        s_yt_ps = sem("yt_ps")
        s_yo_sb = sem("yo_sb")
        s_gl_in = sem("gl_in")
        s_gl_s = sem("gl_s")
        s_lin_sig = sem("lin_sig")
        s_mods1 = sem("mods1")
        s_dve_step = sem("dve_step")
        s_ada_sum = sem("ada_sum")
        s_s5_par = sem("s5_par")
        s_s5_tr = sem("s5_tr")
        s_par_ok = sem("par_ok")
        s_rope_ready = sem("rope_ready")
        s_score_sb = sem("score_sb")
        s_ret_ready = sem("ret_ready")
        s_log_ps = sem("log_ps")
        s_mask_ready = sem("mask_ready")
        s_rank_ps = sem("rank_ps")
        s_act_ready = sem("act_ready")
        s_dve_more = sem("dve_more")
        s_dve_more2 = sem("dve_more2")
        s_more_used = sem("more_used")
        s_c_ready = sem("c_ready")
        s_ss_ps = sem("ss_ps")
        s_ws_ps = sem("ws_ps")
        s_gelu_ready = sem("gelu_ready")
        s_yt_used = sem("yt_used")

        ctx.enter_context(nc.allow_non_contiguous_dma(reason="columns of weights"))

        x_v = a["x"][0].rearrange("(i p) d -> p i d", p=P)
        w_in_v = a["w_in"][0].rearrange("(k p) n -> p k n", p=P)
        w_out_v = a["w_out"][0].rearrange("(k p) n -> p k n", p=P)
        gu_v = a["expert_w_gate_up"][0].rearrange("e (k p) n -> p e k n", p=P)
        dn_v = a["expert_w_down"][0].rearrange("e (k p) n -> p e k n", p=P)
        ple_gate_v = a["ple_gate_w"][0].rearrange("(k p) n -> p k n", p=P)
        ple_proj_v = a["ple_proj_w"][0].rearrange("(k p) n -> p k n", p=P)
        ada_v = a["w_ada_2"].rearrange("l (k p) n -> p l k n", p=P)
        hn_v = hn_dram.rearrange("(i p) d -> p i d", p=P)

        def cols_view(w):
            return w.rearrange("(k p) n -> p k n", p=P)

        linear = [
            (cb3, cols_view(a["ssm_w_out_2"][0]), (0, D), KD, glu_sb),
            (ca, cols_view(a["w_ffn_in_2"][0]), (0, FF), KF, fin_sb),
            (f_act, cols_view(a["w_ffn_out_2"][0]), (0,), KD, fout_sb),
            (ca, cols_view(a["conv_w_in_2"][0]), (0, D, 2 * D), KD, cin_sb),
            (cb3, cols_view(a["conv_w_out_2"][0]), (0,), KD, cout_sb),
            (ca, cols_view(a["w_ffn_in_2"][1]), (0, FF), KF, fin_sb),
            (f_act, cols_view(a["w_ffn_out_2"][1]), (0,), KD, fout_sb),
        ]
        GLU, FIN0, FOUT0, CIN, COUT, FIN1, FOUT1 = range(7)
        lin_before = [16 * len(linear[n - 4][2]) * (linear[n - 4][3] // 2) if n >= 4 else 0 for n in range(len(linear))]
        lin_base = [sum(x[3] for x in linear[:n]) for n in range(len(linear) + 1)]

        block = ctx.enter_context(nc.Block())

        @block.sync
        def _(sp):
            def load(dst, src, done):
                sp.dma_start(dst, src).then_inc(done, 16)

            load(const[:], a["consts"], s_const_in)
            load(rows[:], x_v, s_x_in)
            for name, (r0, n) in VEC.items():
                v = a[name]
                v = v.rearrange("(r c) -> r c", c=P) if len(v.shape) == 1 else \
                    v.rearrange("l (r c) -> (l r) c", c=P) if len(v.shape) == 2 else \
                    v.rearrange("l t (r c) -> (l t r) c", c=P)
                load(vec_rows[r0:r0 + n, :], v, s_vec_in)
            load(ada_rows[0:NADA, :], a["b_ada_2"].rearrange("l (r c) -> (l r) c", c=P), s_vec_in)
            load(smi[:, 0:NT], a["positions"][0].rearrange("(i p) -> p i", p=P), s_pos_in)
            for n in range(3):
                load(w_in_sb[n], w_in_v[:, :, 512 * n:512 * (n + 1)], s_mix_in[n % 3])
            load(decay, a["decay"].rearrange("p (h t) -> p h t", h=HEADS), s_ret_in)
            load(band, a["band"].rearrange("p (g v t) -> p g v t", g=4, v=3), s_ret_in)
            load(pool_w_sb, a["pool_w"][0].rearrange("g c d -> c g d"), s_ret_in)
            sp.wait_ge(s_cols_ready, 8)
            for v, name in enumerate(("ssm_a_re_2", "ssm_a_im_2")):
                load(s5r[:, v, :], a[name][0].rearrange("(j two) n -> j (two n)", two=2), s_s5_in)
            load(s5r[:, 2, 0:2], a["ssm_log_step_2"][0].rearrange("(j two) -> j two", two=2), s_s5_in)
            for n in (3, 4):
                sp.wait_ge(s_proj_ready, NT * (n - 2))
                load(w_in_sb[n], w_in_v[:, :, 512 * n:512 * (n + 1)], s_mix_in[n % 3])
            for n in range(2):
                sp.wait_ge(s_proj_ready, NT * (n + 3))
                load(w_out_sb[n], w_out_v[:, :, 512 * n:512 * (n + 1)], s_mix_in[(n + 5) % 3])
            sp.wait_ge(s_score_ps, HEADS * NT)
            load(rw_sb, a["router_w"][0].rearrange("(k p) e -> p k e", p=P), s_norm_in)
            load(rb_bc, a["router_b"][0].partition_broadcast(P), s_norm_in)
            load(norm_bc, a["norm_moe_w"][0].partition_broadcast(P), s_norm_in)
            load(fnorm_bc, a["final_norm_w"].partition_broadcast(P), s_norm_in)

            def load_slot(q, expert):
                e = bass.ds(expert, 1)
                if q < 8:
                    h, k = q // 4, 2 * (q % 4)
                    src = gu_v[:, e, k:k + 2, D * h:D * (h + 1)]
                else:
                    k = 2 * (q - 8)
                    src = dn_v[:, e, k:k + 2, :]
                load(slot[q], src.rearrange("p e k n -> p (e k) n"), s_slot_in[q])

            def load_bias(expert):
                e = bass.ds(expert, 1)
                load(bias_gu, a["expert_b_gate_up"][0][e, :].rearrange("e n -> (e n)").partition_broadcast(P), s_bias_in)
                load(bias_dn, a["expert_b_down"][0][e, :].rearrange("e n -> (e n)").partition_broadcast(P), s_bias_in)

            def stream(tile, expert):
                for q in range(12):
                    if q in (3, 7):
                        sp.wait_ge(s_gu_ready, 2 * tile - 1 + q // 4)
                    elif q == 11:
                        sp.wait_ge(s_y_ready, tile)
                    else:
                        sp.wait_ge(s_slot_free, 9 * tile - 8 + q - q // 4)
                    load_slot(q, expert)
                    if q == 8:
                        sp.wait_ge(s_y_sb, tile + 1)
                        load_bias(expert)

            sp.wait_ge(s_wout_ready, 2 * NT)
            for q in range(12):
                load_slot(q, 0)
            load_bias(0)
            with sp.Fori(1, E) as e:
                stream(e, e)
            sp.wait_ge(s_route_ok, 1)
            extra = sp.value_load(smi[0:1, 72:73], min_val=0, max_val=MAX_EXTRA)
            with sp.If(extra > 0):
                with sp.Fori(0, extra) as n:
                    expert = sp.value_load(smi[0:1, bass.ds(n + 56, 1)], min_val=0, max_val=E - 1)
                    stream(n + E, expert)

            sp.wait_ge(s_moe_done, 1)
            load(p_rows, a["p"][0, 0].rearrange("(i p) d -> p i d", p=P), s_ple_in)
            for n in range(2):
                load(ple_w_sb[n], ple_gate_v[:, :, 512 * n:512 * (n + 1)], s_ple_in)
            load(ple_p_sb, ple_proj_v, s_ple_in)
            sp.wait_ge(s_more_done, 1)
            for r, name in enumerate(("ssm_b_re_2", "ssm_b_im_2")):
                load(b_in[r], a[name][0].rearrange("(j two) n h -> (two n) j h", two=2), s_b_in)
            for r, name in enumerate(("ssm_c_re_2", "ssm_c_im_2")):
                for d in range(2):
                    load(c_rows[r][:, :, d, :], a[name][0].rearrange("(t g) h n -> (g h) t n", t=8), s_c_in)

            kd = k_dram.rearrange("h g v o -> h g (v o)")
            sp.wait_ge(s_k_sb, 3)
            for v in range(CH):
                for two in range(2):
                    sp.dma_start(k_dram[:, two:G:2, 2 * CH - 2 - v, :],
                                 k_sb[GC * v:GC * (v + 1), two, :, :]).then_inc(s_k_out, 16)
            sp.dma_start(kd[:, :, 0:(CH - 1) * GC],
                         k_zero.unsqueeze(1).broadcast_to([GC, G, (CH - 1) * GC])).then_inc(s_k_out, 16)
            sp.wait_ge(s_k_out, 16 * (2 * CH + 1))
            for v in range(CH):
                load(m_t[GC * v:GC * (v + 1), :, :], kd[:, :, (CH - 1 - v) * GC:(2 * CH - 1 - v) * GC], s_t_in)

            sp.wait_ge(s_h_ready, KD)
            for v in range(0, CH, 2):
                for g in range(8):
                    load(u_sb[GC * v:GC * (v + 1), g:G:8, :], ca[GC * g:GC * (g + 1), :, NC * v:NC * (v + 1)], s_u_in)

            def load_lin(n, b, at):
                _, w, parts, _, buf = linear[n]
                for v, col in enumerate(parts):
                    load(buf[b][:, v, :, :], w[:, :, bass.ds(at * P + col, P)], s_lin_in[n % 4][b])

            def first_lin(n):
                for b in range(2):
                    load_lin(n, b, b)

            def rest_lin(n, each=None):
                with sp.Fori(0, linear[n][3] // 2 - 1) as i:
                    if each:
                        each(i)
                    for b in range(2):
                        sp.wait_ge(s_lin_ready, 2 * i + lin_base[n] + b + 1)
                        load_lin(n, b, 2 * i + 2 + b)

            def load_ada1(i):
                for c in range(2):
                    for k in range(KD):
                        t = KD * c + k
                        if t >= 3:
                            sp.wait_ge(s_ada1_used, 16 * i + t - 2)
                        else:
                            sp.wait_ge(s_ada1_sum, 2 * i + 1)
                        load(ada_w[1][t % 3], ada_v[:, 1, k, bass.ds(2 * ADA_N * i + ADA_N * c, ADA_N)], s_ada1_in[t % 3])

            sp.wait_ge(s_x_state, 1)
            first_lin(GLU)
            rest_lin(GLU)
            sp.wait_ge(s_yo_ps, KD)
            first_lin(FIN0)
            first_lin(FOUT0)
            rest_lin(FIN0)
            sp.wait_ge(s_lin_taken, lin_base[FIN0] + 2)
            first_lin(COUT)
            first_lin(CIN)
            rest_lin(FOUT0, load_ada1)
            load_ada1(KD // 2 - 1)
            first_lin(FIN1)
            rest_lin(CIN)
            rest_lin(COUT)
            first_lin(FOUT1)
            rest_lin(FIN1)
            rest_lin(FOUT1)

            out_v = out[0].rearrange("(c s) d -> s c d", s=CH)
            for i in range(NT):
                sp.wait_ge(s_cols_taken, COLS_OUT + 2 * i + 2)
                for d in range(2):
                    sp.dma_start(out_v[2 * i + d], nat3[NC * d:NC * (d + 1), i, :]).then_inc(s_out_done, 16)
            sp.wait_ge(s_out_done, 16 * 2 * NT)

        @block.gpsimd
        def _(pool):
            for t in range(ADA_C * KD):
                if t >= 3:
                    pool.wait_ge(s_ada_used, t - 2)
                c, k = divmod(t, KD)
                pool.dma_start(ada_w[0][t % 3], ada_v[:, 0, k, ADA_N * c:ADA_N * (c + 1)]).then_inc(s_ada_in[t % 3], 16)

            pool.memset(smi[:, 130:130 + TILES], 0).then_inc(s_table_zero, 1)
            pool.wait_ge(s_table_zero, 1)
            table_v = table.rearrange("(p t) one -> p (t one)", p=P)
            pool.dma_start(table_v, smi[:, 130:130 + TILES]).then_inc(s_table_set, 16)
            pool.wait_ge(s_table_set, 16)
            pool.wait_ge(s_route_ok, 1)
            for n in range(NT * TOPK):
                i = n // TOPK
                pool.indirect_dma_start(
                    out=table, out_offset=bass.IndirectOffsetOnAxis(ap=smi[:, 4 + n:5 + n].bitcast(U32), axis=0),
                    in_=smi[:, 52 + i:53 + i], in_offset=None).then_inc(s_table_set, 16)
            pool.wait_ge(s_table_set, 16 * (NT * TOPK + 1))
            pool.dma_start(smi[:, 80:80 + TILES], table_v).then_inc(s_ids_in, 16)
            pool.wait_ge(s_ids_in, 16)
            pool.wait_ge(s_hn_stored, 16)

            def gather(tile):
                pool.tensor_copy(smi[:, 128:129], smi[:, bass.ds(tile + 80, 1)]).then_inc(s_ids_cur, 1)
                pool.wait_ge(s_ids_cur, tile + 1)
                pool.tensor_tensor(smi[:, 129:130], smi[:, 52:53], smi[:, 52:53], ALU.add)
                pool.indirect_dma_start(
                    out=xs, out_offset=None, in_=hn_dram,
                    in_offset=bass.IndirectOffsetOnAxis(ap=smi[:, 128:129].bitcast(U32), axis=0)).then_inc(s_xs_in, 16)

            def next_tile(tile):
                pool.wait_ge(s_xs_in, 16 * tile + 16)
                pool.wait_ge(s_xt_ready, 2 * tile + 2)
                gather(tile + 1)

            gather(0)
            with pool.Fori(0, E) as e:
                next_tile(e)
            extra = pool.value_load(smi[0:1, 72:73], min_val=0, max_val=MAX_EXTRA)
            with pool.If(extra > 0):
                with pool.Fori(0, extra) as n:
                    next_tile(n + E)

            def take(source, index, done):
                for n in range(NT * TOPK):
                    pool.indirect_dma_start(
                        out=got[n], out_offset=None, in_=source,
                        in_offset=bass.IndirectOffsetOnAxis(ap=smi[:, index + n:index + n + 1].bitcast(U32), axis=0),
                    ).then_inc(done[n // TOPK], 16)

            pool.wait_ge(s_moe_done, 1)
            take(y_dram, 20, s_got_in)
            with pool.If(extra > 0):
                pool.wait_ge(s_got_used, NT)
                take(y_more, 36, [s_more_in] * NT)
            step = Steps(pool, s_pool_step)

            def cmul(dst, x, y, tmp, shape):
                (xr, xi), (yr, yi) = [[v.unsqueeze(2).broadcast_to(shape) for v in x], y]
                step(pool.tensor_tensor(tmp[0], xr, yr, ALU.mult))
                step(pool.tensor_tensor(tmp[1], xi, yi, ALU.mult))
                step(pool.tensor_tensor(dst[0], tmp[0], tmp[1], ALU.subtract))
                step(pool.tensor_tensor(tmp[0], xr, yi, ALU.mult))
                step(pool.tensor_tensor(tmp[1], xi, yr, ALU.mult))
                step(pool.tensor_tensor(dst[1], tmp[0], tmp[1], ALU.add))

            pool.wait_ge(s_more_done, 1)
            pool.wait_ge(s_b_in, 32)
            sh = [P, GP, GC]
            cmul([m_b[r][:, :, CH - 1, :] for r in range(2)], [par[:, 2 + r, :] for r in range(2)], b_in, s5_ta, sh)
            for v in range(CH - 2, -1, -1):
                cmul([m_b[r][:, :, v, :] for r in range(2)], [par[:, r, :] for r in range(2)],
                     [m_b[r][:, :, v + 1, :] for r in range(2)], s5_ta, sh)
            pool.sem_inc(s_b_ready, 1)
            pool.wait_ge(s_pproj_ready, 2 * NT)
            pool.memset(k_zero, 0.0).then_inc(s_k_sb, 1)

        @block.scalar
        def _(act):
            rounds = [0]

            def column(dst, scale=None, view=None):
                r = rounds[0]
                rounds[0] += 1
                act.wait_ge(s_cols_ready, r + 1)
                src = ps[4 + r % 2][:]
                src = src if view is None else view(src)
                if scale is None:
                    act.activation(dst, src, ACT.Copy).then_inc(s_cols_taken, 1)
                else:
                    act.activation(dst, src, ACT.Copy, scale=scale).then_inc(s_cols_taken, 1)

            def squares():
                for i in range(NT):
                    act.activation(nat3[:, i, :], rows[:, i, :], ACT.Square, accum_out=sm[:, i:i + 1]).then_inc(s_sq, 1)

            act.sem_inc(s_y_stored, 16)
            act.wait_ge(s_x_in, 16)
            squares()
            act.wait_ge(s_vec_t, 1)
            act.activation(vec[:, 0:NVEC], ps[6][:, 0:NVEC], ACT.Copy).then_inc(s_vec_ok, 1)
            act.activation(vec[:, NVEC:NVEC + NADA], ps[6][:, P:P + NADA], ACT.Copy).then_inc(s_vec_ok, 1)
            act.wait_ge(s_vec_ok, 2)
            c0 = VEC["c_2"][0]
            act.activation(cact[:], vec[:, c0:c0 + 8], ACT.Sigmoid).then_inc(s_c_sig, 1)
            for k in range(KD):
                column(ca[:, k, :], vcol("norm_mix_w", k))
            for r in range(5 * NT):
                n, i = divmod(r, NT)
                act.wait_ge(s_proj_ready, r + 1)
                act.activation(proj[:, i, 512 * n:512 * (n + 1)], ps[i][:], ACT.Copy).then_inc(s_proj_taken, 1)
                if r == 4:
                    act.wait_ge(s_trig_ready, 1)
                    act.activation(trig[:, 4:6, :, :], trig[:, 2:4, :, :], ACT.Sin).then_inc(s_trig_done, 1)
                if r == 6:
                    act.wait_ge(s_s5_in, 48)
                    act.activation(s5r[:, 2, 2:4], s5r[:, 2, 0:2], ACT.Exp).then_inc(s_s5_exp, 1)
                if r == 14:
                    act.wait_ge(s_s5_angle, 1)
                    act.activation(s5r[:, 10, :], s5r[:, 3, :], ACT.Exp).then_inc(s_s5_fun, 1)
                    act.activation(s5r[:, 24, :], s5r[:, 3, :], ACT.Exp, scale=float(CH)).then_inc(s_s5_fun, 1)
                    act.activation(s5r[:, 11, :], s5r[:, 5, :], ACT.Sin).then_inc(s_s5_fun, 1)
                    act.activation(s5r[:, 12, :], s5r[:, 9, :], ACT.Sin).then_inc(s_s5_fun, 1)
            for g in range(4):
                act.wait_ge(s_pool_ps, g + 1)
                act.activation(pooled[g % 2], ps[6][:], ACT.Copy).then_inc(s_pool_sb, 1)
                act.wait_ge(s_mix_ps, g + 1)
                act.activation(ca[:, 4 + g, :], ps[7][:], ACT.Copy, scale=vcol("pool_scale", g)).then_inc(s_mix_sb, 1)
            for k in range(KD):
                column(cb3[:, k, :])
            act.activation(silu_g, proj[:, :, 3 * RET:4 * RET], ACT.Sigmoid).then_inc(s_sil, 1)
            act.wait_ge(s_y_ps, HEADS)
            for i in range(NT):
                act.activation(nat[:, 512 * i:512 * (i + 1)], ps[i][:], ACT.Copy).then_inc(s_ret_y, 1)
            for k in range(4):
                column(ca[:, k, :], vcol("ret_gn_w", k))
            act.wait_ge(s_wout_taken, 2 * NT)
            squares()
            act.wait_ge(s_nat_ready, 2 * NT)
            act.dma_start(hn_v, nat3).then_inc(s_hn_stored, 16)
            for k in range(KD):
                column(ca[:, k, :])
            act.wait_ge(s_gate_d, 1)
            act.activation(sm[:, 144:160], sm[:, 144:160], ACT.Exp).then_inc(s_gate_e, 1)

            def tokens_columns(tile):
                for r in range(2):
                    act.wait_ge(s_xt_ready, 2 * tile + r + 1)
                    act.activation(xst[:, 4 * r:4 * r + 4, :], ps[6 + r][:].rearrange("p (k t) -> p k t", k=4),
                                   ACT.Copy).then_inc(s_xst_ready, 1)

            def expert(tile, store):
                def sigmoid(h):
                    act.wait_ge(s_g_ready, 2 * tile + h + 1)
                    act.activation(t_s[h], t_g[h], ACT.Sigmoid, scale=ALPHA).then_inc(s_sig_ready, 1)

                def hidden_columns(h):
                    act.wait_ge(s_actt_ps, 2 * tile + h + 1)
                    act.activation(act_t[h], ps[2 * h][:].rearrange("p (k t) -> p k t", k=4),
                                   ACT.Copy).then_inc(s_actt_ready, 1)

                sigmoid(0)
                hidden_columns(0)
                tokens_columns(tile + 1)
                sigmoid(1)
                hidden_columns(1)
                act.wait_ge(s_y_sb, tile + 2)
                act.dma_start(store, y_sb).then_inc(s_y_stored, 16)

            tokens_columns(0)
            with act.Fori(0, E) as e:
                expert(e, y_dram[bass.ds(e * P, P), :])
            act.wait_ge(s_route_ok, 1)
            extra = act.value_load(smi[0:1, 72:73], min_val=0, max_val=MAX_EXTRA)
            act.wait_ge(s_y_stored, 16 * (E + 1))
            with act.If(extra > 0):
                for n in range(MAX_EXTRA):
                    act.dma_start(y_more[P * n:P * (n + 1), :], nat3[:, 0, :]).then_inc(s_more_zero, 16)
                act.wait_ge(s_more_zero, 16 * MAX_EXTRA)
                with act.Fori(0, extra) as n:
                    expert(n + E, y_more[bass.ds(n * P, P), :])
                    act.wait_ge(s_y_stored, 16 * n + 16 * (E + 2))
            act.sem_inc(s_moe_done, 1)

            for k in range(2):
                column(p_cols[:, k, :])
            act.wait_ge(s_more_done, 1)
            squares()
            for k in range(KD):
                column(ca[:, k, :], vcol("norm_ple_w", k))
            for r in range(2):
                for q in range(2):
                    act.wait_ge(s_ct_ps, 2 * r + q + 1)
                    v = ps[q][:].rearrange("p (j two h) -> p j two h", two=2, h=GC)
                    for two in range(2):
                        pp = slice(NS * two, NS * (two + 1))
                        act.activation(s5c[r][pp, 16 * q:16 * (q + 1), :], v[pp, :, two, :], ACT.Copy,
                                       scale=(1.0, -1.0)[r]).then_inc(s_ct_sb, 1)
            for r in range(2 * NT):
                act.wait_ge(s_pgate_ready, r + 1)
                act.activation(gate_sb[r], ps[r % 4][:], ACT.Sigmoid).then_inc(s_pgate_act, 1)
            act.wait_ge(s_pproj_taken, 2 * NT)
            squares()
            for k in range(KD):
                column(xt[:, k, :].rearrange("p (s c) -> p s c", s=CH), None, lambda v: v.rearrange("p (c s) -> p s c", s=CH))
            def norm_squares(sq):
                act.activation(sq, xt[:].rearrange("p k t -> p (k t)"), ACT.Square).then_inc(s_sq2, 1)

            def norm_shift(n, shift):
                for k in range(KD):
                    act.wait_ge(s_hs_ready, KD * n + k + 1)
                    act.activation(ca[:, k, :], ca[:, k, :], ACT.Identity, bias=shift(k)).then_inc(s_h_ready, 1)

            act.wait_ge(s_cols_taken, COLS_XT)
            norm_squares(nat[:])
            norm_shift(0, lambda k: mods[:, 0, k:k + 1])
            act.wait_ge(s_h_ready, KD)
            for v in range(1, CH, 2):
                for g in range(8):
                    act.dma_start(u_sb[GC * v:GC * (v + 1), g:G:8, :],
                                  ca[GC * g:GC * (g + 1), :, NC * v:NC * (v + 1)]).then_inc(s_u_in, 16)
            for r in range(2):
                for q in range(GP // 4):
                    column(m_w[r][:, 4 * q:4 * q + 4, :].rearrange("p j m -> p (j m)"))
            for two in range(2):
                act.wait_ge(s_k_ps, 1)
                act.activation(k_sb[:, two, :, :], ps[6 + two][:].rearrange("p (j h) -> p j h", j=GP), ACT.Copy).then_inc(s_k_sb, 1)

            act.wait_ge(s_rot_ready, 1)
            act.activation(rot_c, rot_c, ACT.Sin).then_inc(s_rot_done, 1)
            act.activation(rot_s, rot_s, ACT.Sin).then_inc(s_rot_done, 1)
            def s5_rows(k):
                act.wait_ge(s_yo_ps, k + 1)
                if k >= 2:
                    act.wait_ge(s_yt_ps, k - 1)
                for two in range(2):
                    dst = y_ch[k % 2].rearrange("c s (j g h) -> c j g s h", j=4, g=2)[:, :, two]
                    src = ps[2 * (k % 2) + two][0:NC, :].rearrange("c (j s h) -> c j s h", j=4, s=CH)
                    act.activation(dst, src, ACT.Copy).then_inc(s_yo_sb, 1)

            act.wait_ge(s_x_state, 1)
            for k in range(KD):
                s5_rows(k)
                if k >= 1:
                    act.wait_ge(s_gl_in, k)
                    act.activation(tmp2[:, 1024:1536], tmp2[:, 512:1024], ACT.Sigmoid, scale=GELU_S).then_inc(s_gl_s, 1)
            act.wait_ge(s_gl_in, KD)
            act.activation(tmp2[:, 1024:1536], tmp2[:, 512:1024], ACT.Sigmoid, scale=GELU_S).then_inc(s_gl_s, 1)

            def lin_sig(n, part, func):
                with act.Fori(0, linear[n][3] // 2) as i:
                    for b in range(2):
                        act.wait_ge(s_lin_ready, 2 * i + lin_base[n] + b + 1)
                        act.activation(sig_sb[b], ps[3 * b + part][:], func).then_inc(s_lin_sig, 1)

            def norm(n, layer):
                norm_squares(cb[:])
                norm_shift(n, layer)

            lin_sig(GLU, 1, ACT.Sigmoid)
            act.wait_ge(s_lin_taken, lin_base[FIN0] + 2)
            norm(1, lambda k: mods[:, 0, 24 + k:25 + k])
            lin_sig(FIN0, 0, ACT.Sigmoid)
            act.wait_ge(s_lin_taken, lin_base[CIN] + 2)
            act.wait_ge(s_mods1, 1)
            norm(2, lambda k: mods[:, 1, k:k + 1])
            lin_sig(CIN, 1, ACT.Copy)
            act.wait_ge(s_lin_taken, lin_base[FIN1] + 2)
            norm(3, lambda k: mods[:, 1, 24 + k:25 + k])
            lin_sig(FIN1, 0, ACT.Sigmoid)
            act.wait_ge(s_lin_taken, lin_base[7] + 2)
            norm_squares(cb[:])
            for i in range(2 * NT):
                column(nat3[:, i // 2, 512 * (i % 2):512 * (i % 2 + 1)])

        @block.vector
        def _(dve):
            step = Steps(dve, s_dve_step)
            tt, ts, stt = dve.tensor_tensor, dve.tensor_scalar, dve.scalar_tensor_tensor

            def rsqrt(y, v, t):
                yi, vi = y.bitcast(I32), v.bitcast(I32)
                step(ts(yi, vi, 1, None, ALU.logical_shift_right))
                step(ts(yi, yi, -1.0, float(RSQRT_SEED), ALU.mult, ALU.add))
                for _ in range(3):
                    step(tt(t, y, y, ALU.mult))
                    step(stt(t, t, -0.5, v, ALU.mult, ALU.mult))
                    step(stt(y, t, 1.5, y, ALU.add, ALU.mult))

            def row_rstd(eps):
                step(ts(sm[:, 8:12], sm[:, 0:4], 1.0 / D, eps, ALU.mult, ALU.add))
                rsqrt(sm[:, 4:8], sm[:, 8:12], sm[:, 12:16])

            def reduce_angle(r, x, n):
                step(ts(n, x, 0.5 / PI, MAGIC, ALU.mult, ALU.add))
                step(ts(n, n, MAGIC, None, ALU.subtract))
                step(stt(r, n, -TWO_PI[0], x, ALU.mult, ALU.add))
                step(stt(r, n, -TWO_PI[1], r, ALU.mult, ALU.add))
                step(stt(r, n, -TWO_PI[2], r, ALU.mult, ALU.add))
                step(ts(r, r, PI_IN, -PI_IN, ALU.min, ALU.max))

            def cosine_angle(r2, r, m):
                step(ts(r2, r, PI / 2, None, ALU.add))
                step(ts(m, r2, PI, -2 * PI, ALU.is_gt, ALU.mult))
                step(tt(r2, r2, m, ALU.add))
                step(ts(r2, r2, PI_IN, -PI_IN, ALU.min, ALU.max))

            dve.sem_inc(s_lin_taken, 2)
            dve.sem_inc(s_y_sb, 1)

            dve.wait_ge(s_sq, NT)
            row_rstd(EPS1)
            for i in range(NT):
                ts(nat3[:, i, :], rows[:, i, :], sm[:, 4 + i:5 + i], None, ALU.mult).then_inc(s_nat_ready, 1)

            dve.wait_ge(s_const_in, 16)
            dve.wait_ge(s_pos_in, 16)
            step(dve.tensor_copy(sm[:, 192:196], smi[:, 0:NT]))
            for i in range(NT):
                step(ts(trig[:, 0, i, :], freq, sm[:, 192 + i:193 + i], None, ALU.mult))
            reduce_angle(trig[:, 2], trig[:, 0], trig[:, 1])
            cosine_angle(trig[:, 3], trig[:, 2], trig[:, 1])
            dve.sem_inc(s_trig_ready, 1)

            dve.wait_ge(s_c_sig, 1)
            c0 = VEC["c_2"][0]
            step(tt(cact[:], cact[:], vec[:, c0:c0 + 8], ALU.mult))

            def ada_tile(acc, w, k):
                if k == 0:
                    return ts(acc, w, cact[:, 0:1], None, ALU.mult)
                return stt(acc, w, cact[:, k:k + 1], acc, ALU.mult, ALU.add)

            def ada_chunk(c):
                for k in range(KD):
                    t = KD * c + k
                    dve.wait_ge(s_ada_in[t % 3], 16 * (t // 3 + 1))
                    if k == 0:
                        dve.wait_ge(s_ada_sum, c)
                    ada_tile(ada_acc[0], ada_w[0][t % 3], k).then_inc(s_ada_used, 1)
                    dve.wait_ge(s_ada_used, t + 1)

            def finish_mods(layer):
                step(tt(mods[:, layer, :], ps[7][:, 0:48], vec[:, NVEC + 48 * layer:NVEC + 48 * (layer + 1)], ALU.add))
                for h, name in enumerate(("norm1_g_2", "norm2_g_2")):
                    g0 = VEC[name][0] + 8 * layer
                    step(stt(scale1[:, layer, 8 * h:8 * (h + 1)], mods[:, layer, 24 * h + 8:24 * h + 16], 1.0,
                             vec[:, g0:g0 + 8], ALU.add, ALU.mult))

            q = [s5r[:, n, :] for n in range(32)]
            for c in range(4):
                ada_chunk(c)
            dve.wait_ge(s_s5_exp, 1)
            dt = s5r[:, 2, 2:4].unsqueeze(2).broadcast_to([GP, 2, NS])
            halves = [v.rearrange("p (g n) -> p g n", g=2) for v in q]
            step(ts(q[0], q[0], -1e-4, None, ALU.min))
            step(tt(halves[3], halves[0], dt, ALU.mult))
            step(tt(halves[4], halves[1], dt, ALU.mult))
            reduce_angle(q[5], q[4], q[6])
            step(ts(q[7], q[5], float(CH), None, ALU.mult))
            reduce_angle(q[25], q[7], q[6])
            cosine_angle(q[9], q[5], q[6])
            dve.sem_inc(s_s5_angle, 1)
            for c in range(4, ADA_C):
                ada_chunk(c)
            dve.wait_ge(s_ada_sum, ADA_C)
            finish_mods(0)
            dve.wait_ge(s_s5_fun, 4)
            step(tt(q[20], q[10], q[12], ALU.mult))
            step(tt(q[21], q[10], q[11], ALU.mult))
            step(tt(q[13], q[0], q[0], ALU.mult))
            step(tt(q[14], q[1], q[1], ALU.mult))
            step(tt(q[13], q[13], q[14], ALU.add))
            step(dve.reciprocal(q[13], q[13]))
            step(ts(q[14], q[20], -1.0, None, ALU.add))
            step(tt(q[15], q[14], q[0], ALU.mult))
            step(tt(q[16], q[21], q[1], ALU.mult))
            step(tt(q[15], q[15], q[16], ALU.add))
            step(tt(q[22], q[15], q[13], ALU.mult))
            step(tt(q[15], q[21], q[0], ALU.mult))
            step(tt(q[16], q[14], q[1], ALU.mult))
            step(tt(q[15], q[15], q[16], ALU.subtract))
            step(tt(q[23], q[15], q[13], ALU.mult))
            dve.sem_inc(s_s5_par, 1)
            dve.wait_ge(s_s5_tr, 1)
            step(dve.tensor_copy(par[:], ps[6][:, 0:6 * GP].rearrange("p (v j) -> p v j", v=6)))
            dve.sem_inc(s_par_ok, 1)

            dve.wait_ge(s_proj_taken, 2 * NT)
            dve.wait_ge(s_trig_done, 1)
            for i in range(NT):
                x = proj[:, i, 0:2 * RET].rearrange("p (h two f) -> p h two f", h=2 * HEADS, two=2)
                sh = [P, 2 * HEADS, 32]
                sin, cos = [trig[:, v, i, :].unsqueeze(1).broadcast_to(sh) for v in (4, 5)]
                x1, x2 = x[:, :, 0, :], x[:, :, 1, :]
                t0, t1 = rope_t
                step(tt(t0, x1, cos, ALU.mult))
                step(tt(t1, x2, sin, ALU.mult))
                step(tt(qkr[:, i, :, 0, :], t0, t1, ALU.subtract))
                step(tt(t0, x2, cos, ALU.mult))
                step(tt(t1, x1, sin, ALU.mult))
                step(tt(qkr[:, i, :, 1, :], t0, t1, ALU.add))
                dve.sem_inc(s_rope_ready, 1)

            dve.wait_ge(s_ret_in, 48)
            for h in range(HEADS):
                for j in range(NT):
                    n = S - P * j
                    dve.wait_ge(s_score_ps, NT * h + j + 1)
                    if h >= 2 and j == 0:
                        dve.wait_ge(s_y_ps, h - 1)
                    tt(scr_s[h % 2][:, SCORE_AT[j]:SCORE_AT[j] + n], ps[4 + j][:, 0:n], decay[:, h, 0:n],
                       ALU.mult).then_inc(s_score_sb, 1)
            dve.wait_ge(s_sil, 1)
            step(tt(silu_g, silu_g, proj[:, :, 3 * RET:4 * RET], ALU.mult))
            dve.wait_ge(s_ret_y, NT)
            nh = NT * HEADS
            mu, var, rs, nt = [sm[:, 16 + nh * v:16 + nh * (v + 1)] for v in range(4)]
            wide = [P, nh, HD]
            step(dve.tensor_reduce(mu, ret_y, AXX, ALU.add))
            step(ts(mu, mu, 1.0 / HD, None, ALU.mult))
            step(tt(ret_y, ret_y, mu.unsqueeze(2).broadcast_to(wide), ALU.subtract))
            step(tt(ret_sq, ret_y, ret_y, ALU.mult))
            step(dve.tensor_reduce(var, ret_sq, AXX, ALU.add))
            step(ts(var, var, 1.0 / HD, EPS1, ALU.mult, ALU.add))
            rsqrt(rs, var, nt)
            step(tt(ret_y, ret_y, rs.unsqueeze(2).broadcast_to(wide), ALU.mult))
            step(tt(nat[:, 0:2048], nat[:, 0:2048], silu_g.rearrange("p k t -> p (k t)"), ALU.mult))
            dve.sem_inc(s_ret_ready, 1)

            for r in range(2 * NT):
                n, i = divmod(r, NT)
                dve.wait_ge(s_wout_ready, r + 1)
                v = rows[:, i, 512 * n:512 * (n + 1)]
                tt(v, v, ps[i][:], ALU.add).then_inc(s_wout_taken, 1)

            dve.wait_ge(s_sq, 2 * NT)
            row_rstd(EPS1)
            dve.wait_ge(s_norm_in, 64)
            for i in range(NT):
                stt(nat3[:, i, :], rows[:, i, :], sm[:, 4 + i:5 + i], norm_bc, ALU.mult, ALU.mult).then_inc(s_nat_ready, 1)

            at = [0]

            def scratch_of(*shape):
                n = 1
                for d in shape:
                    n *= d
                v = route[:, at[0]:at[0] + n]
                at[0] += n
                if len(shape) == 2:
                    v = v.rearrange("p (a b) -> p a b", a=shape[0])
                if len(shape) == 3:
                    v = v.rearrange("p (a b c) -> p a b c", a=shape[0], b=shape[1])
                return v

            logits, hot, prod = scratch_of(NT, E), scratch_of(NT, TOPK, E), scratch_of(NT, TOPK, E)
            mask, rank, over, tile, tmp = [scratch_of(NT, E) for _ in range(5)]
            count, need, total, base = [scratch_of(E) for _ in range(4)]
            ext = scratch_of(MAX_EXTRA + 1, E)
            ext_e, pick_t, pick_r, where = scratch_of(MAX_EXTRA + 1), scratch_of(16), scratch_of(16), scratch_of(16)
            assert at[0] <= 5120
            dve.wait_ge(s_log_ps, 1)
            step(tt(logits, ps[6][:, 0:NT * E].rearrange("p (i e) -> p i e", i=NT),
                    rb_bc.unsqueeze(1).broadcast_to([P, NT, E]), ALU.add))
            top = sm[:, 112:144].rearrange("p (i k) -> p i k", i=NT)
            idx = smi[:, 178:210].rearrange("p (i k) -> p i k", i=NT).bitcast(U32)
            gates = sm[:, 144:160].rearrange("p (i k) -> p i k", i=NT)
            idxf = sm[:, 192:208].rearrange("p (i k) -> p i k", i=NT)
            for i in range(NT):
                step(dve.max(top[:, i, :], logits[:, i, :]))
                step(dve.max_index(idx[:, i, :], top[:, i, :], logits[:, i, :]))
                step(ts(gates[:, i, :], top[:, i, 0:TOPK], top[:, i, 0:1], None, ALU.subtract))
            dve.sem_inc(s_gate_d, 1)
            step(dve.tensor_copy(idxf, idx[:, :, 0:TOPK]))
            for i in range(NT):
                for k in range(TOPK):
                    step(ts(hot[:, i, k, :], iota, idxf[:, i, k:k + 1], None, ALU.is_equal))
            step(dve.tensor_reduce(mask, hot.rearrange("p i k e -> p i e k"), AXX, ALU.add))
            dve.sem_inc(s_mask_ready, 1)
            dve.wait_ge(s_rank_ps, 1)
            step(dve.tensor_copy(rank, ps[7][:, 0:NT * E].rearrange("p (i e) -> p i e", i=NT)))
            step(dve.tensor_copy(count, ps[7][:, NT * E:NT * E + E]))

            def tiles_before(dst, v, limit):
                t = tmp if len(dst.shape) == 3 else base
                step(ts(dst, v, float(limit), None, ALU.is_ge))
                for m in (1, 2):
                    step(ts(t, v, float(P * m + limit), None, ALU.is_ge))
                    step(tt(dst, dst, t, ALU.add))

            tiles_before(need, count, P + 1)
            step(dve.tensor_tensor_scan(total, ones[:, 0:E], need, 0.0, ALU.mult, ALU.add))
            step(tt(base, total, need, ALU.subtract))
            tiles_before(over, rank, P)
            wide = [P, NT, E]
            iota_b = iota.unsqueeze(1).broadcast_to(wide)
            step(ts(base, base, float(E - 1), None, ALU.add))
            step(tt(tile, over, base.unsqueeze(1).broadcast_to(wide), ALU.add))
            step(tt(tile, tile, iota_b, ALU.subtract))
            step(ts(tmp, over, 0.0, None, ALU.is_gt))
            step(tt(tile, tile, tmp, ALU.mult))
            step(tt(tile, tile, iota_b, ALU.add))
            step(stt(rank, over, -float(P), rank, ALU.mult, ALU.add))
            for pick, v in ((pick_t, tile), (pick_r, rank)):
                step(tt(prod, hot, v.unsqueeze(2).broadcast_to([P, NT, TOPK, E]), ALU.mult))
                step(dve.tensor_reduce(pick.rearrange("p (i k) -> p i k", i=NT), prod, AXX, ALU.add))
            step(stt(where, pick_r, float(TILES), pick_t, ALU.mult, ALU.add))
            step(dve.tensor_copy(smi[:, 4:20], where))
            step(dve.tensor_copy(smi[:, 52:56], token))
            step(ts(ext_e, pick_t, float(E), None, ALU.is_ge))
            step(stt(where, pick_t, float(P), pick_r, ALU.mult, ALU.add))
            more, main = sm[:, 176:192], sm[:, 160:176]
            step(stt(prod[:, 0, 0, 0:16], where, -float(E * P), ext_e, ALU.add, ALU.mult))
            step(dve.tensor_copy(smi[:, 36:52], prod[:, 0, 0, 0:16]))
            step(ts(prod[:, 0, 1, 0:16], ext_e, -1.0, 1.0, ALU.mult, ALU.add))
            step(tt(where, where, prod[:, 0, 1, 0:16], ALU.mult))
            step(dve.tensor_copy(smi[:, 20:36], where))
            dve.wait_ge(s_gate_e, 1)
            step(dve.tensor_reduce(sm[:, 12:16], gates, AXX, ALU.add))
            step(dve.reciprocal(sm[:, 12:16], sm[:, 12:16]))
            step(tt(gates, gates, sm[:, 12:16].unsqueeze(2).broadcast_to([P, NT, TOPK]), ALU.mult))
            step(tt(more, sm[:, 144:160], ext_e, ALU.mult))
            step(tt(main, sm[:, 144:160], more, ALU.subtract))
            nx = MAX_EXTRA + 1
            step(tt(ext, total.unsqueeze(1).broadcast_to([P, nx, E]),
                    iota[:, 0:nx].unsqueeze(2).broadcast_to([P, nx, E]), ALU.is_le))
            step(dve.tensor_reduce(ext_e, ext, AXX, ALU.add))
            step(ts(ext_e, ext_e, float(E - 1), None, ALU.min))
            step(dve.tensor_copy(smi[:, 56:72], ext_e))
            step(dve.tensor_copy(smi[:, 72:73], total[:, E - 1:E]))
            dve.sem_inc(s_route_ok, 1)

            def swiglu(tile, h):
                bias = bias_gu.rearrange("p (n f two) -> p n f two", n=4, two=2)
                dve.wait_ge(s_gu_ready, 2 * tile + h + 1)
                for n in range(2):
                    v = ps[2 * h + n][:].rearrange("p (f two) -> p f two", two=2)
                    b = bias[:, 2 * h + n]
                    step(tt(t_g[h][:, 256 * n:256 * (n + 1)], v[:, :, 0], b[:, :, 0], ALU.add))
                    step(tt(t_u[h][:, 256 * n:256 * (n + 1)], v[:, :, 1], b[:, :, 1], ALU.add))
                ts(t_g[h], t_g[h], LIMIT, None, ALU.min).then_inc(s_g_ready, 1)
                dve.wait_ge(s_g_ready, 2 * tile + h + 1)
                step(ts(t_u[h], t_u[h], LIMIT, -LIMIT, ALU.min, ALU.max))
                step(stt(t_u[h], t_u[h], 1.0, t_g[h], ALU.add, ALU.mult))
                dve.wait_ge(s_sig_ready, 2 * tile + h + 1)
                tt(act_n[h], t_u[h], t_s[h], ALU.mult).then_inc(s_act_ready, 1)

            def expert(tile):
                dve.wait_ge(s_bias_in, 32 * tile + 32)
                swiglu(tile, 0)
                swiglu(tile, 1)
                dve.wait_ge(s_y_ready, tile + 1)
                dve.wait_ge(s_y_stored, 16 * tile + 16)
                step(tt(y_sb[:, 0:512], ps[4][:], bias_dn[:, 0:512], ALU.add))
                tt(y_sb[:, 512:1024], ps[5][:], bias_dn[:, 512:1024], ALU.add).then_inc(s_y_sb, 1)

            per = 2 * 6 + 1
            n0 = step.n
            with dve.Fori(0, E) as e:
                step.n, step.off = n0, e * per
                expert(e)
                assert step.n == n0 + per
            n0 += E * per
            extra = dve.value_load(smi[0:1, 72:73], min_val=0, max_val=MAX_EXTRA)
            with dve.If(extra > 0):
                main_step, step = step, Steps(dve, s_dve_more)
                with dve.Fori(0, extra) as n:
                    step.n, step.off = 0, n * per
                    expert(n + E)
                step = main_step
            step.n, step.off = n0, 0

            def combine(i, weights, done):
                for k in range(TOPK):
                    n = TOPK * i + k
                    ins = stt(rows[:, i, :], got[n], weights[:, n:n + 1], rows[:, i, :], ALU.mult, ALU.add)
                    if k < TOPK - 1:
                        step(ins)
                    else:
                        ins.then_inc(done, 1)

            for i in range(NT):
                dve.wait_ge(s_got_in[i], 16 * TOPK)
                combine(i, main, s_got_used)
            with dve.If(extra > 0):
                main_step, step = step, Steps(dve, s_dve_more2)
                dve.wait_ge(s_got_used, NT)
                dve.wait_ge(s_more_in, 16 * NT * TOPK)
                for i in range(NT):
                    combine(i, more, s_more_used)
                dve.wait_ge(s_more_used, NT)
                step = main_step
            dve.wait_ge(s_got_used, NT)
            dve.sem_inc(s_more_done, 1)

            dve.wait_ge(s_sq, 3 * NT)
            row_rstd(EPS1)
            for i in range(NT):
                ts(nat3[:, i, :], rows[:, i, :], sm[:, 4 + i:5 + i], None, ALU.mult).then_inc(s_nat_ready, 1)
            dve.wait_ge(s_ct_sb, 8)
            sh = [P, GP, GC]
            ar, ai = [par[:, r, :].unsqueeze(2).broadcast_to(sh) for r in range(2)]
            src = s5c
            for v in range(CH):
                dst = [m_c[r][:, :, v, :] for r in range(2)]
                step(tt(s5_tb[0], src[0], ar, ALU.mult))
                step(tt(s5_tb[1], src[1], ai, ALU.mult))
                step(tt(dst[0], s5_tb[0], s5_tb[1], ALU.add))
                step(tt(s5_tb[0], src[1], ar, ALU.mult))
                step(tt(s5_tb[1], src[0], ai, ALU.mult))
                step(tt(dst[1], s5_tb[0], s5_tb[1], ALU.subtract))
                src = dst
            dve.sem_inc(s_c_ready, 1)
            for r in range(2 * NT):
                n, i = divmod(r, NT)
                dve.wait_ge(s_pgate_act, r + 1)
                dve.wait_ge(s_pproj_ready, r + 1)
                step(tt(gate_sb[r], gate_sb[r], ps[4 + r % 4][:], ALU.mult))
                v = rows[:, i, 512 * n:512 * (n + 1)]
                tt(v, v, gate_sb[r], ALU.add).then_inc(s_pproj_taken, 1)
            dve.wait_ge(s_sq, 4 * NT)
            row_rstd(EPS1)
            for i in range(NT):
                stt(nat3[:, i, :], rows[:, i, :], sm[:, 4 + i:5 + i], fnorm_bc, ALU.mult, ALU.mult).then_inc(s_nat_ready, 1)

            def norm(n, scale, v):
                dve.wait_ge(s_ss_ps, n + 1)
                step(ts(v, ps[6][:], 1.0 / D, EPS2, ALU.mult, ALU.add))
                rsqrt(n_y, v, n_t)
                for k in range(KD):
                    stt(ca[:, k, :], xt[:, k, :], scale(k), n_y, ALU.mult, ALU.mult).then_inc(s_hs_ready, 1)

            norm(0, lambda k: scale1[:, 0, k:k + 1], n_v[0])

            rot_c3, rot_s3 = [v.rearrange("p (j c) -> p j c", j=GP) for v in (rot_c, rot_s)]
            wide = [P, GP, NC]
            dve.wait_ge(s_nat_ready, 4 * NT)
            dve.wait_ge(s_k_ps, 1)
            step(tt(rot_s3, par[:, 5, :].unsqueeze(2).broadcast_to(wide), chunk.unsqueeze(1).broadcast_to(wide), ALU.mult))
            reduce_angle(rot_s, rot_s, z_re)
            cosine_angle(rot_c, rot_s, z_re)
            dve.sem_inc(s_rot_ready, 1)
            mag3 = mag_sb.rearrange("p (j c) -> p j c", j=GP)
            dve.wait_ge(s_k_out, 16 * (2 * CH + 1))
            step(dve.tensor_copy(mag3, par[:, 4, :].unsqueeze(2).broadcast_to(wide)))
            step(dve.memset(mag3[:, :, 0:1], 0.0))
            dve.wait_ge(s_rot_done, 2)
            t1, t2 = tmp1[:, 0:512], tmp1[:, 512:1024]
            for b in range(4):
                dve.wait_ge(s_ws_ps, b + 1)
                c, sn = rot_c[:, 512 * b:512 * (b + 1)], rot_s[:, 512 * b:512 * (b + 1)]
                wr, wi = ps[2 * b][:], ps[2 * b + 1][:]
                step(tt(t1, wr, c, ALU.mult))
                step(tt(t2, wi, sn, ALU.mult))
                step(tt(z_re[:, 512 * b:512 * (b + 1)], t1, t2, ALU.add))
                step(tt(t1, wi, c, ALU.mult))
                step(tt(t2, wr, sn, ALU.mult))
                step(tt(z_im[:, 512 * b:512 * (b + 1)], t1, t2, ALU.subtract))
            step(dve.tensor_tensor_scan(tmp1, mag_sb, z_re, 0.0, ALU.mult, ALU.add))
            step(dve.tensor_tensor_scan(tmp2, mag_sb, z_im, 0.0, ALU.mult, ALU.add))
            def later(x, z, w, op):
                zv, wv = [v.rearrange("p (j c) -> p j c", j=GP)[:, :, 0:NC - 1] for v in (z, w)]
                step(dve.memset(x[:, :, 0:1], 0.0))
                step(tt(x[:, :, 1:NC], zv, wv, op))

            step(tt(z_re, tmp1, rot_c, ALU.mult))
            step(tt(z_im, tmp2, rot_s, ALU.mult))
            later(x_re, z_re, z_im, ALU.subtract)
            step(tt(z_re, tmp1, rot_s, ALU.mult))
            step(tt(z_im, tmp2, rot_c, ALU.mult))
            later(x_im, z_re, z_im, ALU.add)
            dve.sem_inc(s_x_state, 1)
            y_g, sq_g, sg = tmp2[:, 0:512], tmp2[:, 512:1024], tmp2[:, 1024:1536]
            for k in range(KD):
                dve.wait_ge(s_yt_ps, k + 1)
                dve.wait_ge(s_gelu_ready, k)
                ins = stt(y_g, ca[:, k, :], vcol("ssm_d_2", k), ps[4 + k % 2][:], ALU.mult, ALU.add)
                ins.then_inc(s_yt_used, 1)
                dve.wait_ge(s_yt_used, k + 1)
                step(tt(sq_g, y_g, y_g, ALU.mult))
                step(ts(sq_g, sq_g, GELU_C, 1.0, ALU.mult, ALU.add))
                tt(sq_g, sq_g, y_g, ALU.mult).then_inc(s_gl_in, 1)
                dve.wait_ge(s_gl_s, k + 1)
                tt(cb3[:, k, :], y_g, sg, ALU.mult).then_inc(s_gelu_ready, 1)

            def each_tile(n, per, body, extra=None):
                n0 = step.n
                with dve.Fori(0, linear[n][3] // 2) as i:
                    step.n, step.off = n0, i * per
                    if extra:
                        extra(i)
                    for b in range(2):
                        dve.wait_ge(s_lin_taken, 2 * i + b + lin_base[n] + 2)
                        body(i, b, 2 * i + b, bass.ds(2 * i + b, 1))
                    assert step.n == n0 + per
                step.n, step.off = n0 + per * (linear[n][3] // 2), 0

            sig_n = {GLU: 0, FIN0: KD, CIN: KD + KF, FIN1: 2 * KD + KF}

            def flat(v):
                return v.rearrange("p one t -> p (one t)")

            def glu(i, b, t, at):
                dve.wait_ge(s_lin_sig, t + sig_n[GLU] + 1)
                step(stt(lin_t[b], ps[3 * b][:], mods[:, 0, bass.ds(2 * i + 16 + b, 1)], sig_sb[b], ALU.mult, ALU.mult))
                x = flat(xt[:, at, :])
                tt(x, x, lin_t[b], ALU.add).then_inc(s_lin_taken, 1)

            def hidden(n):
                def body(i, b, t, at):
                    dve.wait_ge(s_lin_sig, t + sig_n[n] + 1)
                    step(tt(lin_t[b], ps[3 * b][:], sig_sb[b], ALU.mult))
                    tt(flat(f_act[:, at, :]), ps[3 * b + 1][:], lin_t[b], ALU.mult).then_inc(s_lin_taken, 1)
                return body

            def residual(n, layer, gate):
                def body(i, b, t, at):
                    dve.wait_ge(s_lin_ready, t + lin_base[n] + 1)
                    x = flat(xt[:, at, :])
                    stt(x, ps[3 * b][:], mods[:, layer, bass.ds(2 * i + gate + b, 1)], x, ALU.mult,
                        ALU.add).then_inc(s_lin_taken, 1)
                return body

            def ada1_pair(i):
                for c in range(2):
                    for k in range(KD):
                        t = KD * c + k
                        before = sum(1 for u in range(t) if u % 3 == t % 3)
                        total = sum(1 for u in range(2 * KD) if u % 3 == t % 3)
                        dve.wait_ge(s_ada1_in[t % 3], 16 * total * i + 16 * (before + 1))
                        if k == 0:
                            dve.wait_ge(s_ada1_sum, 2 * i + c + 1)
                        ada_tile(ada_acc[1], ada_w[1][t % 3], k).then_inc(s_ada1_used, 1)
                        dve.wait_ge(s_ada1_used, 2 * KD * i + t + 1)

            cx = conv_x.rearrange("p s c -> p (s c)")

            def conv(i, b, t, at):
                def w(tap):
                    return vec[:, bass.ds(2 * i + VEC["conv_w_2"][0] + KD * tap + b, 1)]

                dve.wait_ge(s_lin_sig, t + sig_n[CIN] + 1)
                step(tt(cx[:, 2 * NC:], ps[3 * b + 2][:], sig_sb[b], ALU.mult))
                step(dve.tensor_copy(conv_x[:, 0:2, 1:NC], conv_x[:, CH:CH + 2, 0:NC - 1]))
                step(ts(lin_t[b], cx[:, 0:S], w(0), None, ALU.mult))
                step(stt(lin_t[b], cx[:, NC:NC + S], w(1), lin_t[b], ALU.mult, ALU.add))
                step(stt(lin_t[b], cx[:, 2 * NC:], w(2), lin_t[b], ALU.mult, ALU.add))
                tt(flat(cb3[:, at, :]), lin_t[b], ps[3 * b][:], ALU.mult).then_inc(s_lin_taken, 1)

            each_tile(GLU, 2, glu)
            norm(1, lambda k: scale1[:, 0, 8 + k:9 + k], n_v[1])
            each_tile(FIN0, 2, hidden(FIN0))
            each_tile(FOUT0, 0, residual(FOUT0, 0, 40), ada1_pair)
            dve.wait_ge(s_ada1_sum, ADA_C + 1)
            finish_mods(1)
            dve.sem_inc(s_mods1, 1)
            norm(2, lambda k: scale1[:, 1, k:k + 1], n_v[1])
            step(dve.memset(conv_x[:, 0:2, 0:1], 0.0))
            each_tile(CIN, 10, conv)
            each_tile(COUT, 0, residual(COUT, 1, 16))
            norm(3, lambda k: scale1[:, 1, 8 + k:9 + k], n_v[1])
            each_tile(FIN1, 2, hidden(FIN1))
            each_tile(FOUT1, 0, residual(FOUT1, 1, 40))
            norm(4, lambda k: vcol("final_g_2", k), n_v[1])

        @block.tensor
        def _(pe):
            mm = pe.matmul
            pe.sem_inc(s_ada1_sum, 1)
            rounds = [0]

            def column(tiles):
                r = rounds[0]
                rounds[0] += 1
                if r >= 2:
                    pe.wait_ge(s_cols_taken, r - 1)
                at = 0
                for src in tiles:
                    n = src.shape[0]
                    m = src.free_size()
                    last = pe.transpose(ps[4 + r % 2][0:m, at:at + n], src, ident[0:n, 0:n])
                    at += n
                last.then_inc(s_cols_ready, 1)

            def columns_of(v, tiles=KD):
                for k in range(tiles):
                    column([v[:, i, P * k:P * (k + 1)] for i in range(NT)])

            pe.wait_ge(s_const_in, 16)
            pe.wait_ge(s_vec_in, 16 * (len(VEC) + 1))
            pe.transpose(ps[6][:, 0:NVEC], vec_rows[0:NVEC, :], ident[0:NVEC, 0:NVEC])
            pe.transpose(ps[6][:, P:P + NADA], ada_rows[0:NADA, :], ident[0:NADA, 0:NADA]).then_inc(s_vec_t, 1)
            pe.wait_ge(s_nat_ready, NT)
            columns_of(nat3)
            def ada_sum(layer, c, acc, done, wait):
                wait()
                for t in range(ADA_N // P):
                    last = mm(ps[7][:, c * (ADA_N // P) + t:c * (ADA_N // P) + t + 1], acc[:, P * t:P * (t + 1)],
                              ones[:, 0:1], start=True, stop=True)
                last.then_inc(done, 1)

            pe.wait_ge(s_cols_taken, KD)
            for r in range(5 * NT):
                n, i = divmod(r, NT)
                if i == 0:
                    pe.wait_ge(s_mix_in[n % 3], 16 * (n // 3 + 1))
                if r >= NT:
                    pe.wait_ge(s_proj_taken, r - NT + 1)
                for k in range(KD):
                    last = mm(ps[i][:], ca[:, k, P * i:P * (i + 1)], w_in_sb[n][:, k, :], start=(k == 0), stop=(k == KD - 1))
                last.then_inc(s_proj_ready, 1)
                c = r // 2 - 1
                if r % 2 == 0 and 0 <= c < ADA_C:
                    ada_sum(0, c, ada_acc[0], s_ada_sum, lambda: pe.wait_ge(s_ada_used, KD * (c + 1)))
            pe.wait_ge(s_s5_par, 1)
            pe.wait_ge(s_vec_ok, 2)
            for v in range(6):
                last = pe.transpose(ps[6][:, GP * v:GP * (v + 1)], s5r[:, 20 + v, :], ident[0:GP, 0:GP])
            last.then_inc(s_s5_tr, 1)
            pe.wait_ge(s_proj_taken, 5 * NT)
            pe.wait_ge(s_ret_in, 48)
            pe.wait_ge(s_par_ok, 1)
            for g in range(4):
                if g >= 1:
                    pe.wait_ge(s_pool_sb, g)
                for i in range(NT):
                    def u(j):
                        return proj[:, j, 4 * RET + P * g:4 * RET + P * (g + 1)]

                    dst = ps[6][:, P * i:P * (i + 1)]
                    last = mm(dst, u(i), band[:, g, min(i, 1), :], start=True, stop=(i == 0))
                    if i:
                        last = mm(dst, u(i - 1), band[:, g, 2, :], start=False, stop=True)
                last.then_inc(s_pool_ps, 1)
                pe.wait_ge(s_pool_sb, g + 1)
                if g >= 1:
                    pe.wait_ge(s_mix_sb, g)
                mm(ps[7][:], pool_w_sb[:, g, :], pooled[g % 2], start=True, stop=True).then_inc(s_mix_ps, 1)
            pe.wait_ge(s_rope_ready, NT)
            columns_of(nat3)
            pe.wait_ge(s_cols_taken, 2 * KD)
            pe.wait_ge(s_mix_sb, 4)

            def scores(h):
                pp = slice(HD * (h % 2), HD * (h % 2 + 1))
                for j in range(NT):
                    if h >= 1:
                        pe.wait_ge(s_score_sb, NT * (h - 1) + j + 1)
                    mm(ps[4 + j][:, 0:S - P * j], cb3[pp, 4 + h // 2, P * j:P * (j + 1)], cb3[pp, h // 2, P * j:S],
                       start=True, stop=True).then_inc(s_score_ps, 1)

            def values(h):
                pe.wait_ge(s_score_sb, NT * (h + 1))
                for i in range(NT):
                    for j in range(i + 1):
                        at = SCORE_AT[j] + P * (i - j)
                        last = mm(ps[i][:, HD * h:HD * (h + 1)], scr_s[h % 2][:, at:at + P],
                                  proj[:, j, 2 * RET + HD * h:2 * RET + HD * (h + 1)], start=(j == 0), stop=(j == i))
                last.then_inc(s_y_ps, 1)

            scores(0)
            for h in range(HEADS):
                if h + 1 < HEADS:
                    scores(h + 1)
                values(h)
            pe.wait_ge(s_ret_ready, 1)
            columns_of(nat[:].rearrange("p (two i d) -> p two i d", two=2, i=NT)[:, 0], 4)
            pe.wait_ge(s_cols_taken, 2 * KD + 4)
            for r in range(2 * NT):
                n, i = divmod(r, NT)
                if i == 0:
                    pe.wait_ge(s_mix_in[(n + 5) % 3], 16 * ((n + 5) // 3 + 1))
                if r >= NT:
                    pe.wait_ge(s_wout_taken, r - NT + 1)
                for k in range(KD):
                    last = mm(ps[i][:], ca[:, k, P * i:P * (i + 1)], w_out_sb[n][:, k, :], start=(k == 0), stop=(k == KD - 1))
                last.then_inc(s_wout_ready, 1)
            pe.wait_ge(s_nat_ready, 2 * NT)
            columns_of(nat3)
            pe.wait_ge(s_norm_in, 64)
            pe.wait_ge(s_cols_taken, 3 * KD + 4)
            for i in range(NT):
                for k in range(KD):
                    last = mm(ps[6][:, E * i:E * (i + 1)], ca[:, k, P * i:P * (i + 1)], rw_sb[:, k, :],
                              start=(k == 0), stop=(k == KD - 1))
            last.then_inc(s_log_ps, 1)
            pe.wait_ge(s_mask_ready, 1)
            mask = route[:, MASK_AT:MASK_AT + NT * E].rearrange("p (i e) -> p i e", i=NT)
            for i in range(NT):
                for j in range(i):
                    mm(ps[7][:, E * i:E * (i + 1)], ones, mask[:, j, :], start=(j == 0), stop=False)
                mm(ps[7][:, E * i:E * (i + 1)], tri, mask[:, i, :], start=(i == 0), stop=True)
            for j in range(NT):
                last = mm(ps[7][:, E * NT:E * (NT + 1)], ones, mask[:, j, :], start=(j == 0), stop=(j == NT - 1))
            last.then_inc(s_rank_ps, 1)
            pe.wait_ge(s_route_ok, 1)

            def tokens_columns(tile):
                pe.wait_ge(s_xs_in, 16 * tile + 16)
                for r in range(2):
                    for k in range(4):
                        last = pe.transpose(ps[6 + r][:, P * k:P * (k + 1)], xs[:, P * (4 * r + k):P * (4 * r + k + 1)], ident)
                    last.then_inc(s_xt_ready, 1)

            def hidden_columns(tile, h):
                pe.wait_ge(s_act_ready, 2 * tile + h + 1)
                for k in range(4):
                    last = pe.transpose(ps[2 * h][:, P * k:P * (k + 1)], act_n[h][:, P * k:P * (k + 1)], ident)
                last.then_inc(s_actt_ps, 1)

            def up(tile, h):
                for k in range(KD):
                    q = 4 * h + k // 2
                    if k % 2 == 0:
                        pe.wait_ge(s_slot_in[q], 16 * tile + 16)
                    for n in range(2):
                        last = mm(ps[2 * h + n][:], xst[:, k, :], slot[q][:, k % 2, 512 * n:512 * (n + 1)],
                                  start=(k == 0), stop=(k == KD - 1))
                    if k % 2 and k < KD - 1:
                        last.then_inc(s_slot_free, 1)
                last.then_inc(s_gu_ready, 1)

            def down(tile, h):
                pe.wait_ge(s_actt_ready, 2 * tile + h + 1)
                if h == 0:
                    pe.wait_ge(s_y_sb, tile + 1)
                for k in range(4):
                    q = 8 + 2 * h + k // 2
                    if k % 2 == 0:
                        pe.wait_ge(s_slot_in[q], 16 * tile + 16)
                    for n in range(2):
                        last = mm(ps[4 + n][:], act_t[h][:, k, :], slot[q][:, k % 2, 512 * n:512 * (n + 1)],
                                  start=(h == 0 and k == 0), stop=(h == 1 and k == 3))
                    if k % 2 and not (h and k == 3):
                        last.then_inc(s_slot_free, 1)
                if h:
                    last.then_inc(s_y_ready, 1)

            def expert(tile):
                pe.wait_ge(s_xst_ready, 2 * tile + 2)
                up(tile, 0)
                up(tile, 1)
                hidden_columns(tile, 0)
                tokens_columns(tile + 1)
                down(tile, 0)
                hidden_columns(tile, 1)
                down(tile, 1)

            tokens_columns(0)
            with pe.Fori(0, E) as e:
                expert(e)
            extra = pe.value_load(smi[0:1, 72:73], min_val=0, max_val=MAX_EXTRA)
            with pe.If(extra > 0):
                with pe.Fori(0, extra) as n:
                    expert(n + E)

            pe.wait_ge(s_ple_in, 64)
            pe.wait_ge(s_moe_done, 1)
            columns_of(p_rows, 2)
            pe.wait_ge(s_nat_ready, 3 * NT)
            columns_of(nat3)
            pe.wait_ge(s_c_in, 64)
            for r in range(2):
                for q in range(2):
                    if r:
                        pe.wait_ge(s_ct_sb, 2 * q + 2)
                    for t in range(4):
                        last = pe.transpose(ps[q][:, P * t:P * (t + 1)], c_rows[r][:, 4 * q + t].rearrange("p two n -> p (two n)"), ident)
                    last.then_inc(s_ct_ps, 1)
            pe.wait_ge(s_cols_taken, COLS_XT - KD)
            pe.wait_ge(s_ct_sb, 8)
            for r in range(2 * NT):
                n, i = divmod(r, NT)
                if r >= NT:
                    pe.wait_ge(s_pgate_act, r - NT + 1)
                for k in range(KD):
                    last = mm(ps[i][:], ca[:, k, P * i:P * (i + 1)], ple_w_sb[n][:, k, :], start=(k == 0), stop=(k == KD - 1))
                last.then_inc(s_pgate_ready, 1)
            for r in range(2 * NT):
                n, i = divmod(r, NT)
                if r >= NT:
                    pe.wait_ge(s_pproj_taken, r - NT + 1)
                for k in range(2):
                    last = mm(ps[4 + i][:], p_cols[:, k, P * i:P * (i + 1)], ple_p_sb[:, k, 512 * n:512 * (n + 1)],
                              start=(k == 0), stop=(k == 1))
                last.then_inc(s_pproj_ready, 1)
            pe.wait_ge(s_nat_ready, 4 * NT)
            columns_of(nat3)

            def norm_sums(n, sq):
                pe.wait_ge(s_sq2, n + 1)
                for k in range(KD):
                    last = mm(ps[6][:], ones, sq[:, S * k:S * (k + 1)], start=(k == 0), stop=(k == KD - 1))
                last.then_inc(s_ss_ps, 1)

            norm_sums(0, nat)
            pe.wait_ge(s_b_ready, 1)
            for r in range(2):
                for g in range(GP // 4):
                    column([m_b[r][:, 4 * g + j].rearrange("p s h -> p (s h)") for j in range(4)])
            pe.wait_ge(s_hs_ready, KD)
            for j in range(GP):
                for two in range(2):
                    pp = slice(NS * two, NS * (two + 1))
                    for r in range(2):
                        last = mm(ps[6 + two][:, GC * j:GC * (j + 1)], m_b[r][pp, j].rearrange("p s h -> p (s h)"),
                                  s5c[r][pp, j, :], start=(r == 0), stop=(r == 1))
            last.then_inc(s_k_ps, 1)
            pe.wait_ge(s_u_in, 16 * 8 * CH)
            pe.wait_ge(s_cols_taken, COLS_OUT)
            pe.wait_ge(s_k_sb, 3)
            for b in range(4):
                for r in range(2):
                    for j in range(8 * b, 8 * b + 8):
                        for two in range(2):
                            pp = slice(NS * two, NS * (two + 1))
                            last = mm(ps[2 * b + r][pp, NC * (j % 8):NC * (j % 8 + 1)], m_w[r][:, j, pp], u_sb[:, 2 * j + two, :],
                                      start=True, stop=True)
                last.then_inc(s_ws_ps, 1)
            pe.wait_ge(s_x_state, 1)
            pe.wait_ge(s_t_in, 16 * CH)
            pe.wait_ge(s_c_ready, 1)

            def chunk_rows(k):
                if k >= 2:
                    pe.wait_ge(s_yo_sb, 2 * k - 2)
                for j in range(4 * k, 4 * k + 4):
                    for two in range(2):
                        pp = slice(NS * two, NS * (two + 1))
                        dst = ps[2 * (k % 2) + two][0:NC, P * (j % 4):P * (j % 4 + 1)]
                        mm(dst, u_sb[:, 2 * j + two, :], m_t[:, 2 * j + two, :], start=True, stop=False)
                        for r, x in enumerate((x_re, x_im)):
                            last = mm(dst, x[pp, j, :], m_c[r][pp, j].rearrange("p s h -> p (s h)"), start=False, stop=(r == 1))
                last.then_inc(s_yo_ps, 1)

            def chunk_columns(k):
                pe.wait_ge(s_yo_sb, 2 * k + 2)
                if k >= 2:
                    pe.wait_ge(s_yt_used, k - 1)
                for v in range(CH):
                    last = pe.transpose(ps[4 + k % 2][:, NC * v:NC * (v + 1)], y_ch[k % 2][:, v, :], ident[0:NC, 0:NC])
                last.then_inc(s_yt_ps, 1)

            chunk_rows(0)
            for k in range(KD):
                if k + 1 < KD:
                    chunk_rows(k + 1)
                chunk_columns(k)

            def products(n, extra=None):
                src, _, parts, tiles, buf = linear[n]
                depth = KF if src is f_act else KD
                with pe.Fori(0, tiles // 2) as i:
                    for b in range(2):
                        pe.wait_ge(s_lin_in[n % 4][b], 16 * len(parts) * i + lin_before[n] + 16 * len(parts))
                        pe.wait_ge(s_lin_taken, 2 * i + lin_base[n] + b + 1)
                        for v in range(len(parts)):
                            for k in range(depth):
                                last = mm(ps[3 * b + v][:], buf[b][:, v, k, :], src[:, k, :], start=(k == 0), stop=(k == depth - 1))
                            if v < len(parts) - 1:
                                continue
                            last.then_inc(s_lin_ready, 1)
                        if extra:
                            extra(i, b)

            def ada1_sum(i, b):
                pe.wait_ge(s_ada1_used, 2 * KD * i + KD * (b + 1))
                per = ADA_N // P
                for t in range(per):
                    last = mm(ps[7][:, bass.ds(2 * per * i + per * b + t, 1)], ada_acc[1][:, P * t:P * (t + 1)], ones[:, 0:1],
                              start=True, stop=True)
                last.then_inc(s_ada1_sum, 1)

            pe.wait_ge(s_gelu_ready, KD)
            products(GLU)
            norm_sums(1, cb)
            pe.wait_ge(s_h_ready, 2 * KD)
            products(FIN0)
            pe.wait_ge(s_lin_taken, lin_base[FOUT0] + 2)
            products(FOUT0, ada1_sum)
            norm_sums(2, cb)
            pe.wait_ge(s_h_ready, 3 * KD)
            products(CIN)
            pe.wait_ge(s_lin_taken, lin_base[COUT] + 2)
            products(COUT)
            norm_sums(3, cb)
            pe.wait_ge(s_h_ready, 4 * KD)
            products(FIN1)
            pe.wait_ge(s_lin_taken, lin_base[FOUT1] + 2)
            products(FOUT1)
            norm_sums(4, cb)
            for i in range(NT):
                for h in range(2):
                    pe.wait_ge(s_hs_ready, 4 * KD + 4 * h + 4)
                    column([ca[:, 4 * h + k, P * i:P * (i + 1)] for k in range(4)])


def _constants():
    import numpy as np

    consts = np.zeros((P, NCONST), np.float32)

    def put(name, value):
        lo, hi = CONST[name]
        consts[:, lo:hi] = value

    t = np.arange(P)
    put("ident", np.eye(P))
    put("ones", 1.0)
    put("tri", t[:, None] < t[None, :])
    put("iota", np.arange(32)[None, :])
    put("freq", (10000.0 ** (-np.arange(32) / 32.0))[None, :])
    put("token", t[:, None] + P * np.arange(NT)[None, :])
    put("chunk", np.arange(NC)[None, :])
    gamma = np.log1p(-(2.0 ** (-5.0 - np.arange(HEADS))))
    lag = np.arange(S)[None, :] - t[:, None]
    decay = np.where(lag[:, None, :] >= 0, np.exp(np.maximum(lag, 0)[:, None, :] * gamma[None, :, None]), 0.0)
    decay = (decay * HD ** -0.5).astype(np.float32).reshape(P, HEADS * S)
    band = np.zeros((P, len(WINDOWS), 3, P), np.float32)
    for g, w in enumerate(WINDOWS):
        back = t[None, :] - t[:, None]
        inside = (back >= 0) & (back < w)
        band[:, g, 0] = inside / np.minimum(t + 1, w)[None, :] - np.eye(P)
        band[:, g, 1] = inside / w - np.eye(P)
        band[:, g, 2] = (back + P < w) / w
    return {"consts": consts, "decay": decay, "band": band.reshape(P, -1)}


_INS = ["x", "p", "positions", "w_in", "w_out", "ret_gn_w", "pool_w", "pool_scale", "norm_mix_w", "norm_moe_w",
        "router_w", "router_b", "expert_w_gate_up", "expert_b_gate_up", "expert_w_down", "expert_b_down",
        "norm_ple_w", "ple_gate_w", "ple_proj_w", "final_norm_w", "c_2", "norm1_g_2", "norm2_g_2", "w_ada_2",
        "b_ada_2", "ssm_a_re_2", "ssm_a_im_2", "ssm_log_step_2", "ssm_b_re_2", "ssm_b_im_2", "ssm_c_re_2",
        "ssm_c_im_2", "ssm_d_2", "ssm_w_out_2", "conv_w_in_2", "conv_w_2", "conv_w_out_2", "w_ffn_in_2",
        "w_ffn_out_2", "final_g_2"]


def kernel(**inputs):
    import numpy as np
    import concourse.bacc as bacc
    from concourse.bass_utils import run_bass_kernel_spmd

    nc = bacc.Bacc("TRN2", target_bir_lowering=False, num_devices=1)
    arrays = {name: np.ascontiguousarray(inputs[name]) for name in _INS}
    arrays.update(_constants())
    aps = {name: nc.dram_tensor(f"in_{name}", v.shape, mybir.dt.from_np(v.dtype), kind="ExternalInput").ap()
           for name, v in arrays.items()}
    out = nc.dram_tensor("out", (1, S, D), F32, kind="ExternalOutput").ap()
    program(nc, aps, out)
    got = run_bass_kernel_spmd(nc, [{f"in_{name}": v for name, v in arrays.items()}], core_ids=[0])
    return got.results[0]["out"]
```

```python
from contextlib import ExitStack

import concourse.bass as bass
from concourse import mybir

F32 = mybir.dt.float32
F32R = mybir.dt.float32r
I32 = mybir.dt.int32
U32 = mybir.dt.uint32
ALU = mybir.AluOpType
ACT = mybir.ActivationFunctionType
AXX = mybir.AxisListType.X

P = 128
S = 512
D = 1024
NT = S // P
KD = D // P
HEADS, HD = 8, 64
RET = HEADS * HD
NPROJ = 4 * RET + (D - RET)
WINDOWS = (2, 4, 8, 16)
E, TOPK = 32, 4
MAX_EXTRA = S * TOPK // P - 1
TILES = E + MAX_EXTRA + 1
PLE = 256
G, GC, NS = 64, 16, 64
CH = P // GC
NC = S // CH
GP = G // 2
FF = 2816
KF = FF // P
EPS1, EPS2 = 1e-5, 1e-6
LIMIT, ALPHA = 7.0, 1.702
PI = 3.14159265358979
TWO_PI = (6.28125, 1.93500518798828125e-3, 3.019915981956753e-7)
MAGIC = 12582912.0
PI_IN = 3.1415925
RSQRT_SEED = 0x5F3759DF
GELU_C, GELU_S = 0.044715, 1.5957691216057308

VEC = {}
_at = 0
for _name, _rows in (("norm_mix_w", 8), ("ret_gn_w", 4), ("pool_scale", 4), ("norm_ple_w", 8),
                     ("norm1_g_2", 16), ("norm2_g_2", 16), ("ssm_d_2", 8), ("conv_w_2", 24),
                     ("final_g_2", 8), ("c_2", 8)):
    VEC[_name] = (_at, _rows)
    _at += _rows
NVEC = _at
NADA = 96
ADA_N = 768
ADA_C = 6 * D // ADA_N

CONST = {}
_at = 0
for _name, _cols in (("ident", P), ("ones", P), ("tri", P), ("iota", 32), ("freq", 32), ("token", NT),
                     ("chunk", NC), ("pick", E)):
    CONST[_name] = (_at, _at + _cols)
    _at += _cols
NCONST = _at


COLS_ROUTE = KD + KD + 4 + KD
COLS_PLE = COLS_ROUTE + 2 + KD
COLS_XT = COLS_PLE + G // 4 + KD
SCORE_AT = (0, 512, 896, 1152)
MASK_AT = NT * E + 2 * NT * TOPK * E
LINEAR = ("glu", "fin0", "fout0", "cin", "cout", "fin1", "fout1")


class Steps:

    def __init__(self, eng, sem):
        self.eng, self.sem, self.n, self.off = eng, sem, 0, 0

    def __call__(self, ins):
        ins.then_inc(self.sem, 1)
        self.n += 1
        self.eng.wait_ge(self.sem, self.n + self.off)


def program(nc, a, out):
    with ExitStack() as ctx:
        place = {}

        def sb(name, shape, dt=F32):
            place[name] = -(-nc.sbuf_base // 32) * 32
            return ctx.enter_context(nc.sbuf_tensor(name, shape, dt))

        def parts_at(name, region, first, cols):
            return nc.alloc_sbuf_tensor_at(name, [P, cols], F32R, offset=place[region] + 4 * first)

        def sem(name):
            return ctx.enter_context(nc.semaphore(name))

        ps = [ctx.enter_context(nc.psum_tensor(f"bank{i}", [P, 512], F32)) for i in range(8)]

        ring = sb("ring", [P, 24576])
        rows = sb("rows", [P, NT, D])
        nat = sb("nat", [P, 4096])
        ca = sb("ca", [P, KD, S])
        cb = sb("cb", [P, 4096])
        work = sb("work", [P, 10240])
        const = sb("const", [P, NCONST])
        vec = sb("vec", [P, NVEC + NADA])
        mods = sb("mods", [P, 2, 48])
        scale1 = sb("scale1", [P, 2, 16])
        cact = sb("cact", [P, 8])
        sm = sb("sm", [P, 208])
        smi = sb("smi", [P, 216], I32)
        ident, ones, tri, iota, freq, token, chunk, pick_e = (
            const[:, x:y] for x, y in CONST.values())

        def vcol(name, k):
            return vec[:, VEC[name][0] + k:VEC[name][0] + k + 1]

        nat3 = nat[:].rearrange("p (i d) -> p i d", i=NT)
        cb3 = cb[:].rearrange("p (k t) -> p k t", k=KD)

        w_in_sb = [ring[:, n * 4096:(n + 1) * 4096].rearrange("p (k n) -> p k n", k=KD) for n in (0, 1, 2, 0, 1)]
        w_out_sb = [ring[:, n * 4096:(n + 1) * 4096].rearrange("p (k n) -> p k n", k=KD) for n in (2, 0)]
        pooled = [ring[:, 12288 + 512 * b:12288 + 512 * (b + 1)] for b in range(2)]
        decay = ring[:, 16384:20480].rearrange("p (h t) -> p h t", h=HEADS)
        band = ring[:, 20480:22016].rearrange("p (g v t) -> p g v t", g=4, v=3)
        scr_s = [ring[:, 22016 + 1280 * b:22016 + 1280 * (b + 1)] for b in range(2)]
        pool_w_sb = ring[:, 13312:13824].rearrange("p (g d) -> p g d", g=4)
        trig = ring[:, 13824:13824 + 1024].rearrange("p (v i f) -> p v i f", v=8, i=NT)
        proj = work[:].rearrange("p (i n) -> p i n", i=NT)
        ada_acc = cb[:, 0:ADA_N]
        ada_w = [cb[:, ADA_N * (b + 1):ADA_N * (b + 2)] for b in range(3)]
        vec_rows, ada_rows = ca[:, 0, 0:P], ca[:, 0, P:2 * P]
        qkr = nat[:].rearrange("p (i h two f) -> p i h two f", i=NT, h=2 * HEADS, two=2)
        s5r = nat[0:G, :].rearrange("p (v n) -> p v n", n=P)
        rope_t = [ring[:, 14848 + 512 * b:15360 + 512 * b].rearrange("p (h f) -> p h f", f=32) for b in range(2)]
        ret_y = nat[:, 0:2048].rearrange("p (n e) -> p n e", e=HD)
        ret_sq = nat[:, 2048:4096].rearrange("p (n e) -> p n e", e=HD)
        silu_g = ca[:, 0:4, :]
        route = work[:, 5120:10240]
        c_rows = [ring[:, 12288 + 1024 * r:13312 + 1024 * r].rearrange("p (t two n) -> p t two n", t=8, two=2) for r in range(2)]
        b_in = [ring[:, 10240 + 1024 * r:11264 + 1024 * r].rearrange("p (g h) -> p g h", g=G) for r in range(2)]
        s5_ta = [ring[:, 14336 + 1024 * r:15360 + 1024 * r].rearrange("p (g h) -> p g h", g=G) for r in range(2)]
        s5_tb = [ring[:, 12288 + 1024 * r:13312 + 1024 * r].rearrange("p (g h) -> p g h", g=G) for r in range(2)]
        k_sb = work[:, 8192:9216].rearrange("p (g h) -> p g h", g=G)
        p_t = [sb(f"power_t{r}", [P, G])[:] for r in range(2)]
        k_zero = work[0:GC, 9216:9216 + (CH - 1) * GC]

        slot = [ring[:, 2048 * s:2048 * (s + 1)].rearrange("p (k n) -> p k n", k=2) for s in range(12)]
        bias_rows = nat[0:2 * E, 0:3 * D]
        xs = work[:, 3072:4096]
        gu_lo = parts_at("gu_lo", "ring", 0, 8 * 2048)[:].rearrange("p (q k n) -> p q k n", q=8, k=2)
        gu_hi = [v for region in ("ca", "nat")
                 for v in [parts_at(f"gu_hi_{region}", region, 0, 4096)[:].rearrange("p (q k n) -> p q k n", q=2, k=2)]]
        gu_hi = [gu_hi[q // 2][:, q % 2] for q in range(4)]
        xs_hi = parts_at("xs_hi", "work", 4096, D)[:].rearrange("p (k t) -> p k t", k=KD)
        xs_lo = parts_at("xs_lo", "cb", 1024, D)[:].rearrange("p (k t) -> p k t", k=KD)
        bias_t = parts_at("bias_parts", "work", 0, 3 * D)
        pick = sb("pick", [2 * E, P], F32R)
        t_g = [work[:, 5120 + 512 * h:5632 + 512 * h] for h in range(2)]
        t_u = [work[:, 6144 + 512 * h:6656 + 512 * h] for h in range(2)]
        t_s = [work[:, 7168 + 512 * h:7680 + 512 * h] for h in range(2)]
        act_n = [work[:, 8192 + 512 * h:8704 + 512 * h] for h in range(2)]
        act_t = [work[:, 9216 + 512 * h:9728 + 512 * h].rearrange("p (k t) -> p k t", k=4) for h in range(2)]
        y_sb = cb[:, 0:1024]
        rw_sb = cb[:, 1024:1280].rearrange("p (k e) -> p k e", k=KD)
        norm_bc = cb[:, 2048:3072]
        fnorm_bc = cb[:, 3072:4096]
        rb_bc = cb[:, 1280:1312]
        got = [ring[:, 1024 * n:1024 * (n + 1)] for n in range(8)] + \
              [ring[:, 16384 + 1024 * n:16384 + 1024 * (n + 1)] for n in range(8)]

        ple_w_sb = [work[:, 4096 * n:4096 * (n + 1)].rearrange("p (k n) -> p k n", k=KD) for n in range(2)]
        ple_p_sb = work[:, 8192:10240].rearrange("p (k n) -> p k n", k=2)
        p_rows = cb[:, 0:1024].rearrange("p (i d) -> p i d", i=NT)
        p_cols = cb[:, 1024:2048].rearrange("p (k t) -> p k t", k=2)
        gate_sb = [nat[:, 512 * b:512 * (b + 1)] for b in range(8)]

        m_c = ring[:, 0:8192].rearrange("p (g s h) -> p g s h", g=G, s=CH)
        m_w = ring[:, 8192:16384].rearrange("p (g m) -> p g m", g=G)
        m_b = ring[:, 16384:24576].rearrange("p (g s h) -> p g s h", g=G, s=CH)
        m_t = ring[:, 16384:24576].rearrange("p (g m) -> p g m", g=G)
        power = cb[:, 2048:3072].rearrange("p (r v g) -> p r v g", r=2, v=CH)
        xt = work[:, 0:4096].rearrange("p (k t) -> p k t", k=KD)
        u_sb = work[:, 4096:8192].rearrange("p (g c) -> p g c", g=G)
        mag_sb = work[:, 8192:10240]
        rot_c = rows[:, 0:2, :].rearrange("p i d -> p (i d)")
        rot_s = rows[:, 2:4, :].rearrange("p i d -> p (i d)")
        z_re, z_im = cb[:, 0:2048], cb[:, 2048:4096]
        tmp1, tmp2 = nat[:, 0:2048], nat[:, 2048:4096]
        x_s = ring[:, 8192:12288].rearrange("p (g c) -> p g c", g=G)
        y_ch = [nat[0:NC, 1024 * b:1024 * (b + 1)].rearrange("c (s h) -> c s h", s=CH) for b in range(2)]
        par = sb("par", [P, 6, G])
        s5c = [v.rearrange("p (g h) -> p g h", g=G) for v in (cb[:, 0:1024], ring[:, 8192:9216])]

        glu_sb = [rows[:, 2 * b:2 * b + 2, :].rearrange("p i (j n) -> p i j n", n=P) for b in range(2)]
        cin_sb = [r[:, 0:3072].rearrange("p (v k n) -> p v k n", v=3, k=KD)
                  for r in (nat[:], rows[:].rearrange("p i d -> p (i d)"))]
        cout_sb = [ring[:, 15360 + 1024 * b:16384 + 1024 * b].rearrange("p (v k n) -> p v k n", v=1, k=KD) for b in range(2)]
        f_act = ring[:, 0:KF * S].rearrange("p (f t) -> p f t", f=KF)
        fin_sb = [ring[:, 11264 + 2048 * b:13312 + 2048 * b].rearrange("p (v k n) -> p v k n", v=2, k=KD) for b in range(2)]
        fout_sb = [ring[:, 15360 + KF * P * b:15360 + KF * P * (b + 1)].rearrange("p (v k n) -> p v k n", v=1, k=KF) for b in range(2)]
        def weight_parts(name, v, places):
            return [parts_at(f"{name}{b}", region, first, v * D)[:].rearrange("p (v k n) -> p v k n", v=v, k=KD)
                    for b, (region, first) in enumerate(places)]

        fin_hi = weight_parts("fin_hi", 2, [("work", 4096), ("work", 6144)])
        fin_lo = weight_parts("fin_lo", 2, [("ring", 11264), ("ring", 13312)])
        cin_hi = weight_parts("cin_hi", 3, [("work", 4096), ("work", 7168)])
        cin_lo = weight_parts("cin_lo", 3, [("nat", 0), ("rows", 0)])
        h_lo, fin_h, cin_h = [parts_at(name, region, 0, KD * S)[:].rearrange("p (k t) -> p k t", k=KD)
                              for name, region in (("h_lo", "ca"), ("fin_h", "cb"), ("cin_h", "ring"))]
        scratch = ring[:, 20992:24576]
        sig_sb = [scratch[:, 512 * b:512 * (b + 1)] for b in range(2)]
        lin_t = [scratch[:, 1024 + 512 * b:1536 + 512 * b] for b in range(2)]
        conv_x = scratch[:, 2048:2048 + 640].rearrange("p (s c) -> p s c", c=NC)
        n_v = [tmp2[:, 512:1024], scratch[:, 2688:3200]]
        n_y, n_t = tmp2[:, 1024:1536], tmp2[:, 1536:2048]
        sq_acc, sq_t = ca[:, 0, :], [ca[:, 1, :], ca[:, 2, :]]

        hn_dram = nc.dram_tensor("hn_dram", [S, D], F32).ap()
        y_dram = nc.dram_tensor("y_dram", [E * P, D], F32).ap()
        y_more = nc.dram_tensor("y_more", [MAX_EXTRA * P, D], F32).ap()
        table = nc.dram_tensor("slot_table", [P * TILES, 1], I32).ap()
        k_dram = nc.dram_tensor("k_dram", [GC, G, 2 * CH, GC], F32).ap()
        u_dram = nc.dram_tensor("u_dram", [D, S], F32).ap()

        s_const_in = sem("const_in")
        s_x_in = sem("x_in")
        s_vec_in = sem("vec_in")
        s_pos_in = sem("pos_in")
        s_mix_in = [sem(f"mix_in{i}") for i in range(3)]
        s_ret_in = sem("ret_in")
        s_cols_ready = sem("cols_ready")
        s_s5_in = sem("s5_in")
        s_proj_ready = sem("proj_ready")
        s_score_ps = sem("score_ps")
        s_norm_in = sem("norm_in")
        s_slot_in = [sem(f"slot_in{i}") for i in range(12)]
        s_bias_in = sem("bias_in")
        s_gu_ready = sem("gu_ready")
        s_y_ready = sem("y_ready")
        s_slot_free = sem("slot_free")
        s_y_sb = sem("y_sb")
        s_wout_ready = sem("wout_ready")
        s_route_ok = sem("route_ok")
        s_moe_done = sem("moe_done")
        s_ple_in = sem("ple_in")
        s_got_used = sem("got_used")
        s_b_in = sem("b_in")
        s_c_in = sem("c_in")
        s_k_sb = sem("k_sb")
        s_k_out = sem("k_out")
        s_t_in = sem("t_in")
        s_h_ready = sem("h_ready")
        s_u_in = sem("u_in")
        s_u_out = sem("u_out")
        s_power_ok = sem("power_ok")
        s_lin_in = [[sem(f"{name}_in{b}") for b in range(2)] for name in LINEAR[:4]]
        s_lin_ready = sem("lin_ready")
        s_ada1_used = sem("ada1_used")
        s_ada1_sum = sem("ada1_sum")
        s_ada_in = [sem(f"ada_in{i}") for i in range(3)]
        s_ada1_in = [sem(f"ada1_in{i}") for i in range(3)]
        s_x_state = sem("x_state")
        s_yo_ps = sem("yo_ps")
        s_lin_taken = sem("lin_taken")
        s_cols_taken = sem("cols_taken")
        s_out_done = sem("out_done")
        s_ada_used = sem("ada_used")
        s_table_set = sem("table_set")
        s_ids_in = sem("ids_in")
        s_hn_stored = sem("hn_stored")
        s_ids_cur = sem("ids_cur")
        s_xs_in = sem("xs_in")
        s_xt_ready = sem("xt_ready")
        s_got_in = [sem(f"got_in{i}") for i in range(4)]
        s_more_in = sem("more_in")
        s_pool_step = sem("pool_step")
        s_more_done = sem("more_done")
        s_b_ready = sem("b_ready")
        s_pproj_ready = sem("pproj_ready")
        s_sq = sem("sq")
        s_vec_t = sem("vec_t")
        s_vec_ok = sem("vec_ok")
        s_proj_taken = sem("proj_taken")
        s_trig_ready = sem("trig_ready")
        s_trig_done = sem("trig_done")
        s_s5_exp = sem("s5_exp")
        s_s5_angle = sem("s5_angle")
        s_s5_fun = sem("s5_fun")
        s_pool_ps = sem("pool_ps")
        s_pool_sb = sem("pool_sb")
        s_mix_ps = sem("mix_ps")
        s_mix_sb = sem("mix_sb")
        s_sil = sem("sil")
        s_y_ps = sem("y_ps")
        s_ret_y = sem("ret_y")
        s_wout_taken = sem("wout_taken")
        s_nat_ready = sem("nat_ready")
        s_gate_d = sem("gate_d")
        s_gate_e = sem("gate_e")
        s_xst_ready = sem("xst_ready")
        s_g_ready = sem("g_ready")
        s_sig_ready = sem("sig_ready")
        s_actt_ps = sem("actt_ps")
        s_actt_ready = sem("actt_ready")
        s_y_stored = sem("y_stored")
        s_more_zero = sem("more_zero")
        s_ct_ps = sem("ct_ps")
        s_ct_sb = sem("ct_sb")
        s_pgate_ready = sem("pgate_ready")
        s_pgate_act = sem("pgate_act")
        s_pproj_taken = sem("pproj_taken")
        s_sq2 = sem("sq2")
        s_sqt = sem("sqt")
        s_gu_hi = sem("gu_hi")
        s_gu_lo = sem("gu_lo")
        s_xs_hi = sem("xs_hi")
        s_bias_hi = sem("bias_hi")
        s_pick = sem("pick")
        s_bias_ok = sem("bias_ok")
        s_h_hi = sem("h_hi")
        s_h_lo = sem("h_lo")
        s_w_hi = sem("w_hi")
        s_w_lo = sem("w_lo")
        s_sq_used = sem("sq_used")
        s_hs_ready = sem("hs_ready")
        s_k_ps = sem("k_ps")
        s_rot_ready = sem("rot_ready")
        s_rot_done = sem("rot_done")
        s_yt_ps = sem("yt_ps")
        s_yo_sb = sem("yo_sb")
        s_gl_in = sem("gl_in")
        s_gl_s = sem("gl_s")
        s_lin_sig = sem("lin_sig")
        s_mods1 = sem("mods1")
        s_dve_step = sem("dve_step")
        s_ada_sum = sem("ada_sum")
        s_s5_par = sem("s5_par")
        s_s5_tr = sem("s5_tr")
        s_par_ok = sem("par_ok")
        s_rope_ready = sem("rope_ready")
        s_score_sb = sem("score_sb")
        s_ret_ready = sem("ret_ready")
        s_log_ps = sem("log_ps")
        s_mask_ready = sem("mask_ready")
        s_rank_ps = sem("rank_ps")
        s_act_ready = sem("act_ready")
        s_dve_more = sem("dve_more")
        s_dve_more2 = sem("dve_more2")
        s_more_used = sem("more_used")
        s_c_ready = sem("c_ready")
        s_ss_ps = sem("ss_ps")
        s_ws_ps = sem("ws_ps")
        s_gelu_ready = sem("gelu_ready")
        s_yt_used = sem("yt_used")

        ctx.enter_context(nc.allow_non_contiguous_dma(reason="columns of weights"))

        x_v = a["x"][0].rearrange("(i p) d -> p i d", p=P)
        w_in_v = a["w_in"][0].rearrange("(k p) n -> p k n", p=P)
        w_out_v = a["w_out"][0].rearrange("(k p) n -> p k n", p=P)
        gu_v = a["expert_w_gate_up"][0].rearrange("e (k p) n -> p e k n", p=P)
        dn_v = a["expert_w_down"][0].rearrange("e (k p) n -> p e k n", p=P)
        ple_gate_v = a["ple_gate_w"][0].rearrange("(k p) n -> p k n", p=P)
        ple_proj_v = a["ple_proj_w"][0].rearrange("(k p) n -> p k n", p=P)
        ada_v = a["w_ada_2"].rearrange("l (k p) n -> p l k n", p=P)
        hn_v = hn_dram.rearrange("(i p) d -> p i d", p=P)

        def cols_view(w):
            return w.rearrange("(k p) n -> p k n", p=P)

        linear = [
            (cb3, cols_view(a["ssm_w_out_2"][0]), (0, D), KD, glu_sb),
            (ca, cols_view(a["w_ffn_in_2"][0]), (0, FF), KF, fin_sb),
            (f_act, cols_view(a["w_ffn_out_2"][0]), (0,), KD, fout_sb),
            (ca, cols_view(a["conv_w_in_2"][0]), (0, D, 2 * D), KD, cin_sb),
            (cb3, cols_view(a["conv_w_out_2"][0]), (0,), KD, cout_sb),
            (ca, cols_view(a["w_ffn_in_2"][1]), (0, FF), KF, fin_sb),
            (f_act, cols_view(a["w_ffn_out_2"][1]), (0,), KD, fout_sb),
        ]
        GLU, FIN0, FOUT0, CIN, COUT, FIN1, FOUT1 = range(7)
        lin_before = [16 * len(linear[n - 4][2]) * (linear[n - 4][3] // 2) if n >= 4 else 0 for n in range(len(linear))]
        split = {FIN0: (fin_hi, fin_lo, fin_h), CIN: (cin_hi, cin_lo, cin_h), FIN1: (fin_hi, fin_lo, fin_h)}
        hi_before = {n: sum(len(linear[m][2]) * linear[m][3] for m in split if m < n) for n in split}
        lin_base = [sum(x[3] for x in linear[:n]) for n in range(len(linear) + 1)]

        def flat(v):
            return v.rearrange("p one t -> p (one t)")

        def gu_used(eng, tile, q):
            if q % 4 == 3:
                eng.wait_ge(s_gu_ready, 2 * tile + q // 4 + 1)
            else:
                eng.wait_ge(s_slot_free, 9 * tile + q - q // 4 + 1)

        def whole(v):
            return v.bitcast(F32)

        block = ctx.enter_context(nc.Block())

        @block.sync
        def _(sp):
            def load(dst, src, done):
                sp.dma_start(dst, src).then_inc(done, 16)

            load(const[:], a["consts"], s_const_in)
            load(rows[:], x_v, s_x_in)
            for name, (r0, n) in VEC.items():
                v = a[name]
                v = v.rearrange("(r c) -> r c", c=P) if len(v.shape) == 1 else \
                    v.rearrange("l (r c) -> (l r) c", c=P) if len(v.shape) == 2 else \
                    v.rearrange("l t (r c) -> (l t r) c", c=P)
                load(vec_rows[r0:r0 + n, :], v, s_vec_in)
            load(ada_rows[0:NADA, :], a["b_ada_2"].rearrange("l (r c) -> (l r) c", c=P), s_vec_in)
            load(smi[:, 0:NT], a["positions"][0].rearrange("(i p) -> p i", p=P), s_pos_in)
            for n in range(3):
                load(w_in_sb[n], w_in_v[:, :, 512 * n:512 * (n + 1)], s_mix_in[n % 3])
            load(decay, a["decay"].rearrange("p (h t) -> p h t", h=HEADS), s_ret_in)
            load(band, a["band"].rearrange("p (g v t) -> p g v t", g=4, v=3), s_ret_in)
            load(pool_w_sb, a["pool_w"][0].rearrange("g c d -> c g d"), s_ret_in)
            sp.wait_ge(s_cols_ready, 8)
            for v, name in enumerate(("ssm_a_re_2", "ssm_a_im_2")):
                for half in range(2):
                    load(s5r[:, v, NS * half:NS * (half + 1)], a[name][0], s_s5_in)
            load(s5r[:, 2, 0:1], a["ssm_log_step_2"][0].rearrange("(g one) -> g one", one=1), s_s5_in)
            for n in (3, 4):
                sp.wait_ge(s_proj_ready, NT * (n - 2))
                load(w_in_sb[n], w_in_v[:, :, 512 * n:512 * (n + 1)], s_mix_in[n % 3])
            for n in range(2):
                sp.wait_ge(s_proj_ready, NT * (n + 3))
                load(w_out_sb[n], w_out_v[:, :, 512 * n:512 * (n + 1)], s_mix_in[(n + 5) % 3])
            sp.wait_ge(s_score_ps, HEADS * NT)
            load(rw_sb, a["router_w"][0].rearrange("(k p) e -> p k e", p=P), s_norm_in)
            load(rb_bc, a["router_b"][0].partition_broadcast(P), s_norm_in)
            load(norm_bc, a["norm_moe_w"][0].partition_broadcast(P), s_norm_in)
            load(fnorm_bc, a["final_norm_w"].partition_broadcast(P), s_norm_in)

            def load_slot(q, expert):
                e = bass.ds(expert, 1)
                if q < 8:
                    h, k = q // 4, 2 * (q % 4)
                    src = gu_v[:, e, k:k + 2, D * h:D * (h + 1)]
                else:
                    k = 2 * (q - 8)
                    src = dn_v[:, e, k:k + 2, :]
                load(slot[q], src.rearrange("p e k n -> p (e k) n"), s_slot_in[q])

            def stream(tile, expert):
                for q in range(12):
                    if q in (3, 7):
                        sp.wait_ge(s_gu_ready, 2 * tile - 1 + q // 4)
                    elif q == 11:
                        sp.wait_ge(s_y_ready, tile)
                    else:
                        sp.wait_ge(s_slot_free, 9 * tile - 8 + q - q // 4)
                    load_slot(q, expert)

            sp.wait_ge(s_wout_ready, 2 * NT)
            for q in range(12):
                load_slot(q, 0)
            sp.wait_ge(s_hn_stored, 16)
            sp.wait_ge(s_cols_ready, COLS_ROUTE)
            for half in range(2):
                pp = slice(E * half, E * (half + 1))
                load(bias_rows[pp, 0:2 * D], a["expert_b_gate_up"][0], s_bias_in)
                load(bias_rows[pp, 2 * D:], a["expert_b_down"][0], s_bias_in)
            with sp.Fori(1, E) as e:
                stream(e, e)
            sp.wait_ge(s_route_ok, 1)
            extra = sp.value_load(smi[0:1, 72:73], min_val=0, max_val=MAX_EXTRA)
            with sp.If(extra > 0):
                with sp.Fori(0, extra) as n:
                    expert = sp.value_load(smi[0:1, bass.ds(n + 56, 1)], min_val=0, max_val=E - 1)
                    stream(n + E, expert)

            sp.wait_ge(s_moe_done, 1)
            load(p_rows, a["p"][0, 0].rearrange("(i p) d -> p i d", p=P), s_ple_in)
            for r in range(2):
                for d in range(2):
                    part = ("re", "im")[(r + d) % 2]
                    load(c_rows[r][:, :, d, :], a[f"ssm_c_{part}_2"][0].rearrange("(t g) h n -> (g h) t n", t=8), s_c_in)
                    load(b_in[r][NS * d:NS * (d + 1)], a[f"ssm_b_{part}_2"][0].rearrange("g n h -> n g h"), s_b_in)
            for n in range(2):
                load(ple_w_sb[n], ple_gate_v[:, :, 512 * n:512 * (n + 1)], s_ple_in)
            load(ple_p_sb, ple_proj_v, s_ple_in)

            for k in range(KD):
                sp.wait_ge(s_h_ready, k + 1)
                sp.dma_start(u_dram[P * k:P * (k + 1), :], ca[:, k, :]).then_inc(s_u_out, 16)
            sp.wait_ge(s_u_out, 16 * KD)
            u_v = u_dram.rearrange("(g h) (s c) -> s h g c", h=GC, s=CH)
            for v in range(CH):
                load(u_sb[GC * v:GC * (v + 1), :, :], u_v[v], s_u_in)

            kd = k_dram.rearrange("h g v o -> h g (v o)")
            sp.wait_ge(s_k_sb, 3)
            for v in range(CH):
                sp.dma_start(k_dram[:, :, 2 * CH - 2 - v, :], k_sb[GC * v:GC * (v + 1), :, :]).then_inc(s_k_out, 16)
            sp.dma_start(kd[:, :, 0:(CH - 1) * GC],
                         k_zero.unsqueeze(1).broadcast_to([GC, G, (CH - 1) * GC])).then_inc(s_k_out, 16)
            sp.wait_ge(s_k_out, 16 * (CH + 1))
            for v in range(CH):
                load(m_t[GC * v:GC * (v + 1), :, :], kd[:, :, (CH - 1 - v) * GC:(2 * CH - 1 - v) * GC], s_t_in)

            def load_lin(n, b, at):
                _, w, parts, _, buf = linear[n]
                for v, col in enumerate(parts):
                    load(buf[b][:, v, :, :], w[:, :, bass.ds(at * P + col, P)], s_lin_in[n % 4][b])

            def first_lin(n):
                for b in range(2):
                    load_lin(n, b, b)

            def rest_lin(n, each=None):
                with sp.Fori(0, linear[n][3] // 2 - 1) as i:
                    if each:
                        each(i)
                    for b in range(2):
                        sp.wait_ge(s_lin_ready, 2 * i + lin_base[n] + b + 1)
                        load_lin(n, b, 2 * i + 2 + b)

            def load_ada1(i):
                for c in range(2):
                    for k in range(KD):
                        t = KD * c + k
                        if t >= 3:
                            sp.wait_ge(s_ada1_used, 16 * i + t - 2)
                        else:
                            sp.wait_ge(s_ada1_sum, 2 * i + 1)
                        load(ada_w[t % 3], ada_v[:, 1, k, bass.ds(2 * ADA_N * i + ADA_N * c, ADA_N)], s_ada1_in[t % 3])

            sp.wait_ge(s_x_state, 1)
            first_lin(GLU)
            sp.wait_ge(s_yo_ps, KD)
            first_lin(FIN0)
            rest_lin(GLU)
            first_lin(FOUT0)
            rest_lin(FIN0)
            sp.wait_ge(s_lin_taken, lin_base[FIN0] + 2)
            first_lin(CIN)
            sp.wait_ge(s_lin_ready, lin_base[FOUT0])
            rest_lin(FOUT0, load_ada1)
            load_ada1(KD // 2 - 1)
            first_lin(FIN1)
            sp.wait_ge(s_lin_ready, lin_base[CIN])
            first_lin(COUT)
            rest_lin(CIN)
            rest_lin(COUT)
            sp.wait_ge(s_lin_ready, lin_base[FIN1])
            first_lin(FOUT1)
            rest_lin(FIN1)
            rest_lin(FOUT1)

            out_v = out[0].rearrange("(c s) d -> s c d", s=CH)
            for i in range(NT):
                sp.wait_ge(s_cols_taken, COLS_XT + 2 * i + 2)
                for d in range(2):
                    sp.dma_start(out_v[2 * i + d], nat3[NC * d:NC * (d + 1), i, :]).then_inc(s_out_done, 16)
            sp.wait_ge(s_out_done, 16 * 2 * NT)

        @block.gpsimd
        def _(pool):
            for t in range(ADA_C * KD):
                if t >= 3:
                    pool.wait_ge(s_ada_used, t - 2)
                c, k = divmod(t, KD)
                pool.dma_start(ada_w[t % 3], ada_v[:, 0, k, ADA_N * c:ADA_N * (c + 1)]).then_inc(s_ada_in[t % 3], 16)

            step = Steps(pool, s_pool_step)
            step(pool.memset(smi[:, 130:130 + TILES], 0))
            table_v = table.rearrange("(p t) one -> p (t one)", p=P)
            pool.dma_start(table_v, smi[:, 130:130 + TILES]).then_inc(s_table_set, 16)
            pool.wait_ge(s_table_set, 16)
            pool.wait_ge(s_route_ok, 1)
            for n in range(NT * TOPK):
                i = n // TOPK
                pool.indirect_dma_start(
                    out=table, out_offset=bass.IndirectOffsetOnAxis(ap=smi[:, 4 + n:5 + n].bitcast(U32), axis=0),
                    in_=smi[:, 52 + i:53 + i], in_offset=None).then_inc(s_table_set, 16)
            pool.wait_ge(s_table_set, 16 * (NT * TOPK + 1))
            pool.dma_start(smi[:, 80:80 + TILES], table_v).then_inc(s_ids_in, 16)
            pool.wait_ge(s_ids_in, 16)
            pool.wait_ge(s_hn_stored, 16)

            def gather(tile):
                pool.tensor_copy(smi[:, 128:129], smi[:, bass.ds(tile + 80, 1)]).then_inc(s_ids_cur, 1)
                pool.wait_ge(s_ids_cur, tile + 1)
                pool.tensor_tensor(smi[:, 129:130], smi[:, 52:53], smi[:, 52:53], ALU.add)
                pool.indirect_dma_start(
                    out=xs, out_offset=None, in_=hn_dram,
                    in_offset=bass.IndirectOffsetOnAxis(ap=smi[:, 128:129].bitcast(U32), axis=0)).then_inc(s_xs_in, 16)

            def next_tile(tile):
                pool.wait_ge(s_xs_in, 16 * tile + 16)
                pool.wait_ge(s_xt_ready, 2 * tile + 2)
                gather(tile + 1)

            gather(0)
            ptt = pool.tensor_tensor
            for r in range(2):
                step(pool.tensor_copy(power[:, r, 0, :], par[:, r, :]))
            for v in range(1, CH):
                (xr, xi), (ar, ai) = [power[:, r, v - 1, :] for r in range(2)], [par[:, r, :] for r in range(2)]
                step(ptt(p_t[0], xr, ar, ALU.mult))
                step(ptt(p_t[1], xi, ai, ALU.mult))
                step(ptt(power[:, 0, v, :], p_t[0], p_t[1], ALU.subtract))
                step(ptt(p_t[0], xr, ai, ALU.mult))
                step(ptt(p_t[1], xi, ar, ALU.mult))
                step(ptt(power[:, 1, v, :], p_t[0], p_t[1], ALU.add))
            pool.sem_inc(s_power_ok, 1)
            with pool.Fori(0, E) as e:
                next_tile(e)
            extra = pool.value_load(smi[0:1, 72:73], min_val=0, max_val=MAX_EXTRA)
            with pool.If(extra > 0):
                with pool.Fori(0, extra) as n:
                    next_tile(n + E)

            def take(source, index, done):
                for n in range(NT * TOPK):
                    pool.indirect_dma_start(
                        out=got[n], out_offset=None, in_=source,
                        in_offset=bass.IndirectOffsetOnAxis(ap=smi[:, index + n:index + n + 1].bitcast(U32), axis=0),
                    ).then_inc(done[n // TOPK], 16)

            pool.wait_ge(s_moe_done, 1)
            take(y_dram, 20, s_got_in)
            with pool.If(extra > 0):
                pool.wait_ge(s_got_used, NT)
                take(y_more, 36, [s_more_in] * NT)
            def wide(v):
                return v.unsqueeze(2).broadcast_to([P, G, GC])

            def turned(dst, x, y, z, w, op):
                step(ptt(s5_ta[0], x, wide(z), ALU.mult))
                step(ptt(s5_ta[1], y, wide(w), ALU.mult))
                step(ptt(dst, s5_ta[0], s5_ta[1], op))

            pool.wait_ge(s_b_in, 64)
            step(pool.tensor_scalar(b_in[1][0:NS], b_in[1][0:NS], -1.0, None, ALU.mult))
            pool.wait_ge(s_more_done, 1)
            bbar = m_b[:, :, CH - 1, :]
            turned(bbar, b_in[0], b_in[1], par[:, 2, :], par[:, 3, :], ALU.add)
            turned(b_in[1], b_in[1], b_in[0], par[:, 2, :], par[:, 3, :], ALU.subtract)
            for v in range(CH - 2, -1, -1):
                turned(m_b[:, :, v, :], bbar, b_in[1], power[:, 0, CH - 2 - v, :], power[:, 1, CH - 2 - v, :], ALU.add)
            pool.sem_inc(s_b_ready, 1)
            pool.wait_ge(s_pproj_ready, 2 * NT)
            pool.memset(k_zero, 0.0).then_inc(s_k_sb, 1)

        @block.scalar
        def _(act):
            rounds = [0]

            def column(dst, scale=None, view=None):
                r = rounds[0]
                rounds[0] += 1
                act.wait_ge(s_cols_ready, r + 1)
                src = ps[4 + r % 2][:]
                src = src if view is None else view(src)
                if scale is None:
                    act.activation(dst, src, ACT.Copy).then_inc(s_cols_taken, 1)
                else:
                    act.activation(dst, src, ACT.Copy, scale=scale).then_inc(s_cols_taken, 1)

            def squares():
                for i in range(NT):
                    act.activation(nat3[:, i, :], rows[:, i, :], ACT.Square, accum_out=sm[:, i:i + 1]).then_inc(s_sq, 1)

            act.sem_inc(s_sqt, 1)
            act.sem_inc(s_y_sb, 1)
            act.sem_inc(s_y_stored, 16)
            act.wait_ge(s_x_in, 16)
            squares()
            act.wait_ge(s_vec_t, 1)
            act.activation(vec[:, 0:NVEC], ps[6][:, 0:NVEC], ACT.Copy).then_inc(s_vec_ok, 1)
            act.activation(vec[:, NVEC:NVEC + NADA], ps[6][:, P:P + NADA], ACT.Copy).then_inc(s_vec_ok, 1)
            act.wait_ge(s_vec_ok, 2)
            c0 = VEC["c_2"][0]
            act.activation(cact[:], vec[:, c0:c0 + 8], ACT.Sigmoid).then_inc(s_vec_ok, 1)
            for k in range(KD):
                column(ca[:, k, :], vcol("norm_mix_w", k))
            for r in range(5 * NT):
                n, i = divmod(r, NT)
                act.wait_ge(s_proj_ready, r + 1)
                act.activation(proj[:, i, 512 * n:512 * (n + 1)], ps[i][:], ACT.Copy).then_inc(s_proj_taken, 1)
                if r == 4:
                    act.wait_ge(s_trig_ready, 1)
                    act.activation(trig[:, 4:6, :, :], trig[:, 2:4, :, :], ACT.Sin).then_inc(s_trig_done, 1)
                if r == 6:
                    act.wait_ge(s_s5_in, 80)
                    act.activation(s5r[:, 2, 1:2], s5r[:, 2, 0:1], ACT.Exp).then_inc(s_s5_exp, 1)
                if r == 14:
                    act.wait_ge(s_s5_angle, 1)
                    act.activation(s5r[:, 10, :], s5r[:, 3, :], ACT.Exp).then_inc(s_s5_fun, 1)
                    act.activation(s5r[:, 24, :], s5r[:, 3, :], ACT.Exp, scale=float(CH)).then_inc(s_s5_fun, 1)
                    act.activation(s5r[:, 11, :], s5r[:, 5, :], ACT.Sin).then_inc(s_s5_fun, 1)
                    act.activation(s5r[:, 12, :], s5r[:, 9, :], ACT.Sin).then_inc(s_s5_fun, 1)
            for g in range(4):
                act.wait_ge(s_pool_ps, g + 1)
                act.activation(pooled[g % 2], ps[6][:], ACT.Copy).then_inc(s_pool_sb, 1)
                act.wait_ge(s_mix_ps, g + 1)
                act.activation(ca[:, 4 + g, :], ps[7][:], ACT.Copy, scale=vcol("pool_scale", g)).then_inc(s_mix_sb, 1)
            for k in range(KD):
                column(cb3[:, k, :])
            act.activation(silu_g, proj[:, :, 3 * RET:4 * RET], ACT.Sigmoid).then_inc(s_sil, 1)
            act.wait_ge(s_y_ps, HEADS)
            for i in range(NT):
                act.activation(nat[:, 512 * i:512 * (i + 1)], ps[i][:], ACT.Copy).then_inc(s_ret_y, 1)
            for k in range(4):
                column(ca[:, k, :], vcol("ret_gn_w", k))
            act.wait_ge(s_wout_taken, 2 * NT)
            squares()
            act.wait_ge(s_nat_ready, 2 * NT)
            act.dma_start(hn_v, nat3).then_inc(s_hn_stored, 16)
            for k in range(KD):
                column(ca[:, k, :])
            act.wait_ge(s_gate_d, 1)
            act.activation(sm[:, 144:160], sm[:, 144:160], ACT.Exp).then_inc(s_gate_e, 1)

            def tokens_columns(tile):
                for r in range(2):
                    act.wait_ge(s_xt_ready, 2 * tile + r + 1)
                    act.activation(xs_hi[:, 4 * r:4 * r + 4, :], ps[6 + r][:].rearrange("p (k t) -> p k t", k=4),
                                   ACT.Copy).then_inc(s_xs_hi, 1)

            def weights_high(tile, q, first=False):
                act.wait_ge(s_slot_in[q], 16 * tile + 16)
                if not first:
                    gu_used(act, tile - (q < 4), (q + 4) % 8)
                act.activation(gu_hi[q % 4], slot[q], ACT.Copy).then_inc(s_gu_hi, 1)

            def pick_biases(index):
                act.activation(pick[:], pick_e[0:2 * E, bass.ds(index, 1)].broadcast_to([2 * E, P]), ACT.Copy).then_inc(s_pick, 1)

            def expert(tile, store, ahead):
                def sigmoid(h):
                    act.wait_ge(s_g_ready, 4 * tile + 2 * h + 2)
                    act.activation(t_s[h], t_g[h], ACT.Sigmoid, scale=ALPHA).then_inc(s_sig_ready, 1)

                def hidden_columns(h):
                    act.wait_ge(s_actt_ps, 2 * tile + h + 1)
                    act.activation(act_t[h], ps[2 * h][:].rearrange("p (k t) -> p k t", k=4),
                                   ACT.Copy).then_inc(s_actt_ready, 1)

                for q in range(4, 8):
                    weights_high(tile, q)
                sigmoid(0)
                if ahead:
                    weights_high(tile + 1, 0)
                    weights_high(tile + 1, 1)
                hidden_columns(0)
                sigmoid(1)
                tokens_columns(tile + 1)
                if ahead:
                    weights_high(tile + 1, 2)
                    weights_high(tile + 1, 3)
                hidden_columns(1)
                if ahead:
                    pick_biases(tile + 1)
                act.wait_ge(s_y_ready, tile + 1)
                act.wait_ge(s_y_stored, 16 * tile + 16)
                for n in range(2):
                    act.activation(y_sb[:, 512 * n:512 * (n + 1)], ps[4 + n][:], ACT.Copy).then_inc(s_y_sb, 1)
                act.wait_ge(s_y_sb, 2 * tile + 3)
                act.dma_start(store, y_sb).then_inc(s_y_stored, 16)

            pick_biases(0)
            act.wait_ge(s_bias_in, 64)
            act.activation(bias_t[0:2 * E, :], bias_rows, ACT.Copy).then_inc(s_bias_hi, 1)
            act.wait_ge(s_bias_ok, 1)
            for q in range(4):
                weights_high(0, q, first=True)
            tokens_columns(0)
            with act.Fori(0, E - 1) as e:
                expert(e, y_dram[bass.ds(e * P, P), :], True)
            expert(E - 1, y_dram[P * (E - 1):P * E, :], False)
            act.wait_ge(s_route_ok, 1)
            extra = act.value_load(smi[0:1, 72:73], min_val=0, max_val=MAX_EXTRA)
            act.wait_ge(s_y_stored, 16 * (E + 1))
            act.wait_ge(s_xst_ready, 2 * E + 2)
            with act.If(extra > 0):
                for n in range(MAX_EXTRA):
                    act.dma_start(y_more[P * n:P * (n + 1), :], rows[:, 0, :]).then_inc(s_more_zero, 16)
                act.wait_ge(s_more_zero, 16 * MAX_EXTRA)
                with act.Fori(0, extra) as n:
                    pick_biases(act.value_load(smi[0:1, bass.ds(n + 56, 1)], min_val=0, max_val=E - 1))
                    for q in range(4):
                        weights_high(n + E, q)
                    expert(n + E, y_more[bass.ds(n * P, P), :], False)
                    act.wait_ge(s_y_stored, 16 * n + 16 * (E + 2))
                    act.wait_ge(s_xst_ready, 2 * n + 2 * E + 4)
            act.sem_inc(s_moe_done, 1)

            for k in range(2):
                column(p_cols[:, k, :])
            act.wait_ge(s_more_done, 1)
            squares()
            for k in range(KD):
                column(ca[:, k, :], vcol("norm_ple_w", k))
            for r in range(2):
                for q in range(2):
                    act.wait_ge(s_ct_ps, 2 * r + q + 1)
                    v = ps[q][:].rearrange("p (g h) -> p g h", h=GC)
                    for two in range(2):
                        pp = slice(NS * two, NS * (two + 1))
                        act.activation(s5c[r][pp, 32 * q:32 * (q + 1), :], v[pp, :, :], ACT.Copy,
                                       scale=(-1.0 if r or two else 1.0)).then_inc(s_ct_sb, 1)
            for r in range(2 * NT):
                act.wait_ge(s_pgate_ready, r + 1)
                act.activation(gate_sb[r], ps[r % 4][:], ACT.Sigmoid).then_inc(s_pgate_act, 1)
            act.wait_ge(s_pproj_taken, 2 * NT)
            squares()
            act.wait_ge(s_c_ready, 1)
            for q in range(G // 4):
                column(m_w[:, 4 * q:4 * q + 4, :].rearrange("p g m -> p (g m)"))
            for k in range(KD):
                column(xt[:, k, :].rearrange("p (s c) -> p s c", s=CH), None, lambda v: v.rearrange("p (c s) -> p s c", s=CH))
                act.wait_ge(s_cols_taken, COLS_XT - KD + k + 1)
                act.activation(ca[:, k, :], xt[:, k, :], ACT.Square).then_inc(s_sq2, 1)
            def high(n, k, hi):
                act.wait_ge(s_h_ready, KD * n + k + 1)
                act.activation(hi[:, k, :], ca[:, k, :], ACT.Copy).then_inc(s_h_hi, 1)

            def norm_shift(n, shift, hi=None):
                for k in range(KD):
                    act.wait_ge(s_hs_ready, KD * n + k + 1)
                    act.activation(ca[:, k, :], ca[:, k, :], ACT.Identity, bias=shift(k)).then_inc(s_h_ready, 1)
                    if hi is not None and k:
                        high(n, k - 1, hi)
                if hi is not None:
                    high(n, KD - 1, hi)

            norm_shift(0, lambda k: mods[:, 0, k:k + 1])
            act.wait_ge(s_k_ps, 1)
            for n in range(2):
                act.activation(k_sb[:, GP * n:GP * (n + 1), :], ps[n][:].rearrange("p (g h) -> p g h", g=GP), ACT.Copy).then_inc(s_k_sb, 1)

            act.wait_ge(s_rot_ready, 1)
            act.activation(rot_c, rot_c, ACT.Sin).then_inc(s_rot_done, 1)
            act.activation(rot_s, rot_s, ACT.Sin).then_inc(s_rot_done, 1)
            def s5_rows(k):
                act.wait_ge(s_yo_ps, k + 1)
                if k >= 2:
                    act.wait_ge(s_yt_ps, k - 1)
                for two in range(2):
                    dst = y_ch[k % 2].rearrange("c s (j g h) -> c j g s h", j=4, g=2)[:, :, two]
                    src = ps[2 * (k % 2) + two][0:NC, :].rearrange("c (j s h) -> c j s h", j=4, s=CH)
                    act.activation(dst, src, ACT.Copy).then_inc(s_yo_sb, 1)

            act.wait_ge(s_x_state, 1)
            for k in range(KD):
                s5_rows(k)
                if k >= 1:
                    act.wait_ge(s_gl_in, k)
                    act.activation(tmp2[:, 1024:1536], tmp2[:, 512:1024], ACT.Sigmoid, scale=GELU_S).then_inc(s_gl_s, 1)
            act.wait_ge(s_gl_in, KD)
            act.activation(tmp2[:, 1024:1536], tmp2[:, 512:1024], ACT.Sigmoid, scale=GELU_S).then_inc(s_gl_s, 1)

            def weights_high(n, i, b):
                parts, buf = linear[n][2], linear[n][4]
                act.wait_ge(s_lin_in[n % 4][b], 16 * len(parts) * i + lin_before[n] + 16 * len(parts))
                for v in range(len(parts)):
                    act.activation(split[n][0][b][:, v], buf[b][:, v], ACT.Copy).then_inc(s_w_hi, 1)

            def lin_sig(n, bank, func, after=None):
                def tile(i, b):
                    act.wait_ge(s_lin_ready, 2 * i + lin_base[n] + b + 1)
                    act.activation(sig_sb[b], ps[3 * b + bank][:], func).then_inc(s_lin_sig, 1)
                    if after:
                        after(i, b)

                pairs = linear[n][3] // 2
                with act.Fori(0, pairs - (n in split)) as i:
                    for b in range(2):
                        tile(i, b)
                        if n in split:
                            weights_high(n, i + 1, b)
                if n in split:
                    for b in range(2):
                        tile(pairs - 1, b)

            def square(m, n, i, b):
                act.wait_ge(s_lin_taken, 2 * i + lin_base[n] + b + 3)
                act.wait_ge(s_sq_used, 2 * i + KD * m + b + 1)
                act.activation(sq_t[b], flat(xt[:, bass.ds(2 * i + b, 1), :]), ACT.Square).then_inc(s_sqt, 1)

            def lin_squares(m, n):
                with act.Fori(0, KD // 2) as i:
                    for b in range(2):
                        square(m, n, i, b)

            def first_high(n):
                for b in range(2):
                    weights_high(n, 0, b)

            first_high(FIN0)
            lin_sig(GLU, 1, ACT.Sigmoid, lambda i, b: square(0, GLU, i, b))
            norm_shift(1, lambda k: mods[:, 0, 24 + k:25 + k], fin_h)
            lin_sig(FIN0, 0, ACT.Sigmoid)
            first_high(CIN)
            lin_squares(1, FOUT0)
            act.wait_ge(s_mods1, 1)
            norm_shift(2, lambda k: mods[:, 1, k:k + 1], cin_h)
            lin_sig(CIN, 1, ACT.Copy)
            first_high(FIN1)
            lin_squares(2, COUT)
            norm_shift(3, lambda k: mods[:, 1, 24 + k:25 + k], fin_h)
            lin_sig(FIN1, 0, ACT.Sigmoid)
            lin_squares(3, FOUT1)
            for i in range(2 * NT):
                column(nat3[:, i // 2, 512 * (i % 2):512 * (i % 2 + 1)])

        @block.vector
        def _(dve):
            step = Steps(dve, s_dve_step)
            tt, ts, stt = dve.tensor_tensor, dve.tensor_scalar, dve.scalar_tensor_tensor

            def rsqrt(y, v, t):
                yi, vi = y.bitcast(I32), v.bitcast(I32)
                step(ts(yi, vi, 1, None, ALU.logical_shift_right))
                step(ts(yi, yi, -1.0, float(RSQRT_SEED), ALU.mult, ALU.add))
                for _ in range(3):
                    step(tt(t, y, y, ALU.mult))
                    step(stt(t, t, -0.5, v, ALU.mult, ALU.mult))
                    step(stt(y, t, 1.5, y, ALU.add, ALU.mult))

            def row_rstd(eps):
                step(ts(sm[:, 8:12], sm[:, 0:4], 1.0 / D, eps, ALU.mult, ALU.add))
                rsqrt(sm[:, 4:8], sm[:, 8:12], sm[:, 12:16])

            def reduce_angle(r, x, n):
                step(ts(n, x, 0.5 / PI, MAGIC, ALU.mult, ALU.add))
                step(ts(n, n, MAGIC, None, ALU.subtract))
                step(stt(r, n, -TWO_PI[0], x, ALU.mult, ALU.add))
                step(stt(r, n, -TWO_PI[1], r, ALU.mult, ALU.add))
                step(stt(r, n, -TWO_PI[2], r, ALU.mult, ALU.add))
                step(ts(r, r, PI_IN, -PI_IN, ALU.min, ALU.max))

            def cosine_angle(r2, r, m):
                step(ts(r2, r, PI / 2, None, ALU.add))
                step(ts(m, r2, PI, -2 * PI, ALU.is_gt, ALU.mult))
                step(tt(r2, r2, m, ALU.add))
                step(ts(r2, r2, PI_IN, -PI_IN, ALU.min, ALU.max))

            dve.sem_inc(s_lin_taken, 2)
            dve.sem_inc(s_sq_used, 1)

            dve.wait_ge(s_sq, NT)
            row_rstd(EPS1)
            for i in range(NT):
                ts(nat3[:, i, :], rows[:, i, :], sm[:, 4 + i:5 + i], None, ALU.mult).then_inc(s_nat_ready, 1)

            dve.wait_ge(s_const_in, 16)
            dve.wait_ge(s_pos_in, 16)
            step(dve.tensor_copy(sm[:, 192:196], smi[:, 0:NT]))
            for i in range(NT):
                step(ts(trig[:, 0, i, :], freq, sm[:, 192 + i:193 + i], None, ALU.mult))
            reduce_angle(trig[:, 2], trig[:, 0], trig[:, 1])
            cosine_angle(trig[:, 3], trig[:, 2], trig[:, 1])
            dve.sem_inc(s_trig_ready, 1)

            dve.wait_ge(s_vec_ok, 3)
            c0 = VEC["c_2"][0]
            step(tt(cact[:], cact[:], vec[:, c0:c0 + 8], ALU.mult))

            def ada_tile(acc, w, k):
                if k == 0:
                    return ts(acc, w, cact[:, 0:1], None, ALU.mult)
                return stt(acc, w, cact[:, k:k + 1], acc, ALU.mult, ALU.add)

            def ada_chunk(c):
                for k in range(KD):
                    t = KD * c + k
                    dve.wait_ge(s_ada_in[t % 3], 16 * (t // 3 + 1))
                    if k == 0:
                        dve.wait_ge(s_ada_sum, c)
                    ada_tile(ada_acc, ada_w[t % 3], k).then_inc(s_ada_used, 1)
                    dve.wait_ge(s_ada_used, t + 1)

            def finish_mods(layer):
                step(tt(mods[:, layer, :], ps[7][:, 0:48], vec[:, NVEC + 48 * layer:NVEC + 48 * (layer + 1)], ALU.add))
                for h, name in enumerate(("norm1_g_2", "norm2_g_2")):
                    g0 = VEC[name][0] + 8 * layer
                    step(stt(scale1[:, layer, 8 * h:8 * (h + 1)], mods[:, layer, 24 * h + 8:24 * h + 16], 1.0,
                             vec[:, g0:g0 + 8], ALU.add, ALU.mult))

            q = [s5r[:, n, :] for n in range(32)]
            for c in range(4):
                ada_chunk(c)
            dve.wait_ge(s_s5_exp, 1)
            dt = s5r[:, 2, 1:2]
            step(ts(q[0], q[0], -1e-4, None, ALU.min))
            step(ts(q[3], q[0], dt, None, ALU.mult))
            step(ts(q[4], q[1], dt, None, ALU.mult))
            reduce_angle(q[5], q[4], q[6])
            step(ts(q[7], q[5], float(CH), None, ALU.mult))
            reduce_angle(q[25], q[7], q[6])
            cosine_angle(q[9], q[5], q[6])
            dve.sem_inc(s_s5_angle, 1)
            for c in range(4, ADA_C):
                ada_chunk(c)
            dve.wait_ge(s_ada_sum, ADA_C)
            finish_mods(0)
            dve.wait_ge(s_s5_fun, 4)
            step(tt(q[20], q[10], q[12], ALU.mult))
            step(tt(q[21], q[10], q[11], ALU.mult))
            step(tt(q[13], q[0], q[0], ALU.mult))
            step(tt(q[14], q[1], q[1], ALU.mult))
            step(tt(q[13], q[13], q[14], ALU.add))
            step(dve.reciprocal(q[13], q[13]))
            step(ts(q[14], q[20], -1.0, None, ALU.add))
            step(tt(q[15], q[14], q[0], ALU.mult))
            step(tt(q[16], q[21], q[1], ALU.mult))
            step(tt(q[15], q[15], q[16], ALU.add))
            step(tt(q[22], q[15], q[13], ALU.mult))
            step(tt(q[15], q[21], q[0], ALU.mult))
            step(tt(q[16], q[14], q[1], ALU.mult))
            step(tt(q[15], q[15], q[16], ALU.subtract))
            step(tt(q[23], q[15], q[13], ALU.mult))
            dve.sem_inc(s_s5_par, 1)
            dve.wait_ge(s_s5_tr, 1)
            step(dve.tensor_copy(par[:], ps[6][:, 0:6 * G].rearrange("p (v g) -> p v g", v=6)))
            dve.sem_inc(s_par_ok, 1)

            dve.wait_ge(s_proj_taken, 2 * NT)
            dve.wait_ge(s_trig_done, 1)
            for i in range(NT):
                x = proj[:, i, 0:2 * RET].rearrange("p (h two f) -> p h two f", h=2 * HEADS, two=2)
                sh = [P, 2 * HEADS, 32]
                sin, cos = [trig[:, v, i, :].unsqueeze(1).broadcast_to(sh) for v in (4, 5)]
                x1, x2 = x[:, :, 0, :], x[:, :, 1, :]
                t0, t1 = rope_t
                step(tt(t0, x1, cos, ALU.mult))
                step(tt(t1, x2, sin, ALU.mult))
                step(tt(qkr[:, i, :, 0, :], t0, t1, ALU.subtract))
                step(tt(t0, x2, cos, ALU.mult))
                step(tt(t1, x1, sin, ALU.mult))
                step(tt(qkr[:, i, :, 1, :], t0, t1, ALU.add))
                dve.sem_inc(s_rope_ready, 1)

            dve.wait_ge(s_ret_in, 48)
            for h in range(HEADS):
                for j in range(NT):
                    n = S - P * j
                    dve.wait_ge(s_score_ps, NT * h + j + 1)
                    if h >= 2 and j == 0:
                        dve.wait_ge(s_y_ps, h - 1)
                    tt(scr_s[h % 2][:, SCORE_AT[j]:SCORE_AT[j] + n], ps[4 + j][:, 0:n], decay[:, h, 0:n],
                       ALU.mult).then_inc(s_score_sb, 1)
            dve.wait_ge(s_sil, 1)
            step(tt(silu_g, silu_g, proj[:, :, 3 * RET:4 * RET], ALU.mult))
            dve.wait_ge(s_ret_y, NT)
            nh = NT * HEADS
            mu, var, rs, nt = [sm[:, 16 + nh * v:16 + nh * (v + 1)] for v in range(4)]
            wide = [P, nh, HD]
            step(dve.tensor_reduce(mu, ret_y, AXX, ALU.add))
            step(ts(mu, mu, 1.0 / HD, None, ALU.mult))
            step(tt(ret_y, ret_y, mu.unsqueeze(2).broadcast_to(wide), ALU.subtract))
            step(tt(ret_sq, ret_y, ret_y, ALU.mult))
            step(dve.tensor_reduce(var, ret_sq, AXX, ALU.add))
            step(ts(var, var, 1.0 / HD, EPS1, ALU.mult, ALU.add))
            rsqrt(rs, var, nt)
            step(tt(ret_y, ret_y, rs.unsqueeze(2).broadcast_to(wide), ALU.mult))
            step(tt(nat[:, 0:2048], nat[:, 0:2048], silu_g.rearrange("p k t -> p (k t)"), ALU.mult))
            dve.sem_inc(s_ret_ready, 1)

            for r in range(2 * NT):
                n, i = divmod(r, NT)
                dve.wait_ge(s_wout_ready, r + 1)
                v = rows[:, i, 512 * n:512 * (n + 1)]
                tt(v, v, ps[i][:], ALU.add).then_inc(s_wout_taken, 1)

            dve.wait_ge(s_sq, 2 * NT)
            row_rstd(EPS1)
            dve.wait_ge(s_norm_in, 64)
            for i in range(NT):
                stt(nat3[:, i, :], rows[:, i, :], sm[:, 4 + i:5 + i], norm_bc, ALU.mult, ALU.mult).then_inc(s_nat_ready, 1)

            at = [0]

            def scratch_of(*shape):
                n = 1
                for d in shape:
                    n *= d
                v = route[:, at[0]:at[0] + n]
                at[0] += n
                if len(shape) == 2:
                    v = v.rearrange("p (a b) -> p a b", a=shape[0])
                if len(shape) == 3:
                    v = v.rearrange("p (a b c) -> p a b c", a=shape[0], b=shape[1])
                return v

            logits, hot, prod = scratch_of(NT, E), scratch_of(NT, TOPK, E), scratch_of(NT, TOPK, E)
            mask, rank, over, tile, tmp = [scratch_of(NT, E) for _ in range(5)]
            count, need, total, base = [scratch_of(E) for _ in range(4)]
            ext = scratch_of(MAX_EXTRA + 1, E)
            ext_e, pick_t, pick_r, where = scratch_of(MAX_EXTRA + 1), scratch_of(16), scratch_of(16), scratch_of(16)
            assert at[0] <= 5120
            dve.wait_ge(s_log_ps, 1)
            step(tt(logits, ps[6][:, 0:NT * E].rearrange("p (i e) -> p i e", i=NT),
                    rb_bc.unsqueeze(1).broadcast_to([P, NT, E]), ALU.add))
            top = sm[:, 112:144].rearrange("p (i k) -> p i k", i=NT)
            idx = smi[:, 178:210].rearrange("p (i k) -> p i k", i=NT).bitcast(U32)
            gates = sm[:, 144:160].rearrange("p (i k) -> p i k", i=NT)
            idxf = sm[:, 192:208].rearrange("p (i k) -> p i k", i=NT)
            for i in range(NT):
                step(dve.max(top[:, i, :], logits[:, i, :]))
                step(dve.max_index(idx[:, i, :], top[:, i, :], logits[:, i, :]))
                step(ts(gates[:, i, :], top[:, i, 0:TOPK], top[:, i, 0:1], None, ALU.subtract))
            dve.sem_inc(s_gate_d, 1)
            step(dve.tensor_copy(idxf, idx[:, :, 0:TOPK]))
            for i in range(NT):
                for k in range(TOPK):
                    step(ts(hot[:, i, k, :], iota, idxf[:, i, k:k + 1], None, ALU.is_equal))
            step(dve.tensor_reduce(mask, hot.rearrange("p i k e -> p i e k"), AXX, ALU.add))
            dve.sem_inc(s_mask_ready, 1)
            dve.wait_ge(s_rank_ps, 1)
            step(dve.tensor_copy(rank, ps[7][:, 0:NT * E].rearrange("p (i e) -> p i e", i=NT)))
            step(dve.tensor_copy(count, ps[7][:, NT * E:NT * E + E]))

            def tiles_before(dst, v, limit):
                t = tmp if len(dst.shape) == 3 else base
                step(ts(dst, v, float(limit), None, ALU.is_ge))
                for m in (1, 2):
                    step(ts(t, v, float(P * m + limit), None, ALU.is_ge))
                    step(tt(dst, dst, t, ALU.add))

            tiles_before(need, count, P + 1)
            step(dve.tensor_tensor_scan(total, ones[:, 0:E], need, 0.0, ALU.mult, ALU.add))
            step(tt(base, total, need, ALU.subtract))
            tiles_before(over, rank, P)
            wide = [P, NT, E]
            iota_b = iota.unsqueeze(1).broadcast_to(wide)
            step(ts(base, base, float(E - 1), None, ALU.add))
            step(tt(tile, over, base.unsqueeze(1).broadcast_to(wide), ALU.add))
            step(tt(tile, tile, iota_b, ALU.subtract))
            step(ts(tmp, over, 0.0, None, ALU.is_gt))
            step(tt(tile, tile, tmp, ALU.mult))
            step(tt(tile, tile, iota_b, ALU.add))
            step(stt(rank, over, -float(P), rank, ALU.mult, ALU.add))
            for pick, v in ((pick_t, tile), (pick_r, rank)):
                step(tt(prod, hot, v.unsqueeze(2).broadcast_to([P, NT, TOPK, E]), ALU.mult))
                step(dve.tensor_reduce(pick.rearrange("p (i k) -> p i k", i=NT), prod, AXX, ALU.add))
            step(stt(where, pick_r, float(TILES), pick_t, ALU.mult, ALU.add))
            step(dve.tensor_copy(smi[:, 4:20], where))
            step(dve.tensor_copy(smi[:, 52:56], token))
            step(ts(ext_e, pick_t, float(E), None, ALU.is_ge))
            step(stt(where, pick_t, float(P), pick_r, ALU.mult, ALU.add))
            more, main = sm[:, 176:192], sm[:, 160:176]
            step(stt(prod[:, 0, 0, 0:16], where, -float(E * P), ext_e, ALU.add, ALU.mult))
            step(dve.tensor_copy(smi[:, 36:52], prod[:, 0, 0, 0:16]))
            step(ts(prod[:, 0, 1, 0:16], ext_e, -1.0, 1.0, ALU.mult, ALU.add))
            step(tt(where, where, prod[:, 0, 1, 0:16], ALU.mult))
            step(dve.tensor_copy(smi[:, 20:36], where))
            dve.wait_ge(s_gate_e, 1)
            step(dve.tensor_reduce(sm[:, 12:16], gates, AXX, ALU.add))
            step(dve.reciprocal(sm[:, 12:16], sm[:, 12:16]))
            step(tt(gates, gates, sm[:, 12:16].unsqueeze(2).broadcast_to([P, NT, TOPK]), ALU.mult))
            step(tt(more, sm[:, 144:160], ext_e, ALU.mult))
            step(tt(main, sm[:, 144:160], more, ALU.subtract))
            nx = MAX_EXTRA + 1
            step(tt(ext, total.unsqueeze(1).broadcast_to([P, nx, E]),
                    iota[:, 0:nx].unsqueeze(2).broadcast_to([P, nx, E]), ALU.is_le))
            step(dve.tensor_reduce(ext_e, ext, AXX, ALU.add))
            step(ts(ext_e, ext_e, float(E - 1), None, ALU.min))
            step(dve.tensor_copy(smi[:, 56:72], ext_e))
            step(dve.tensor_copy(smi[:, 72:73], total[:, E - 1:E]))
            dve.sem_inc(s_route_ok, 1)

            def swiglu(tile, h):
                dve.wait_ge(s_gu_ready, 2 * tile + h + 1)
                v = [ps[2 * h + n][:].rearrange("p (f two) -> p f two", two=2) for n in range(2)]
                g, u = [[t[:, 256 * n:256 * (n + 1)] for n in range(2)] for t in (t_g[h], t_u[h])]
                for n in range(2):
                    ts(g[n], v[n][:, :, 0], LIMIT, None, ALU.min).then_inc(s_g_ready, 1)
                for n in range(2):
                    step(ts(u[n], v[n][:, :, 1], LIMIT, -LIMIT, ALU.min, ALU.max))
                dve.wait_ge(s_g_ready, 4 * tile + 2 * h + 2)
                step(stt(t_u[h], t_u[h], 1.0, t_g[h], ALU.add, ALU.mult))
                dve.wait_ge(s_sig_ready, 2 * tile + h + 1)
                tt(act_n[h], t_u[h], t_s[h], ALU.mult).then_inc(s_act_ready, 1)

            def weights_low(tile, q):
                dve.wait_ge(s_gu_hi, 8 * tile + q + 1)
                tt(gu_lo[:, q], slot[q], whole(gu_hi[q % 4]), ALU.subtract).then_inc(s_gu_lo, 1)

            def tokens_low(tile):
                for r in range(2):
                    dve.wait_ge(s_xs_hi, 2 * tile + r + 1)
                    v = slice(4 * r, 4 * r + 4)
                    tt(xs_lo[:, v, :], ps[6 + r][:].rearrange("p (k t) -> p k t", k=4), whole(xs_hi[:, v, :]),
                       ALU.subtract).then_inc(s_xst_ready, 1)

            def expert(tile, ahead):
                for q in range(4, 8):
                    weights_low(tile, q)
                swiglu(tile, 0)
                if ahead:
                    weights_low(tile + 1, 0)
                    weights_low(tile + 1, 1)
                swiglu(tile, 1)
                tokens_low(tile + 1)
                if ahead:
                    weights_low(tile + 1, 2)
                    weights_low(tile + 1, 3)

            dve.wait_ge(s_bias_hi, 1)
            tt(bias_t[E:2 * E, :], bias_rows[E:2 * E, :], whole(bias_t[E:2 * E, :]), ALU.subtract).then_inc(s_bias_ok, 1)
            for q in range(4):
                weights_low(0, q)
            tokens_low(0)
            per = 2 * 3
            n0 = step.n
            with dve.Fori(0, E - 1) as e:
                step.n, step.off = n0, e * per
                expert(e, True)
                assert step.n == n0 + per
            step.n, step.off = n0, (E - 1) * per
            expert(E - 1, False)
            n0 += E * per
            extra = dve.value_load(smi[0:1, 72:73], min_val=0, max_val=MAX_EXTRA)
            with dve.If(extra > 0):
                main_step, step = step, Steps(dve, s_dve_more)
                with dve.Fori(0, extra) as n:
                    step.n, step.off = 0, n * per
                    for q in range(4):
                        weights_low(n + E, q)
                    expert(n + E, False)
                step = main_step
            step.n, step.off = n0, 0

            def combine(i, weights, done):
                for k in range(TOPK):
                    n = TOPK * i + k
                    ins = stt(rows[:, i, :], got[n], weights[:, n:n + 1], rows[:, i, :], ALU.mult, ALU.add)
                    if k < TOPK - 1:
                        step(ins)
                    else:
                        ins.then_inc(done, 1)

            for i in range(NT):
                dve.wait_ge(s_got_in[i], 16 * TOPK)
                combine(i, main, s_got_used)
            with dve.If(extra > 0):
                main_step, step = step, Steps(dve, s_dve_more2)
                dve.wait_ge(s_got_used, NT)
                dve.wait_ge(s_more_in, 16 * NT * TOPK)
                for i in range(NT):
                    combine(i, more, s_more_used)
                dve.wait_ge(s_more_used, NT)
                step = main_step
            dve.wait_ge(s_got_used, NT)
            dve.sem_inc(s_more_done, 1)

            dve.wait_ge(s_sq, 3 * NT)
            row_rstd(EPS1)
            for i in range(NT):
                ts(nat3[:, i, :], rows[:, i, :], sm[:, 4 + i:5 + i], None, ALU.mult).then_inc(s_nat_ready, 1)
            dve.wait_ge(s_ct_sb, 8)
            dve.wait_ge(s_power_ok, 1)
            for v in range(CH):
                ar, ai = [power[:, r, v, :].unsqueeze(2).broadcast_to([P, G, GC]) for r in range(2)]
                step(tt(s5_tb[0], s5c[0], ar, ALU.mult))
                step(tt(s5_tb[1], s5c[1], ai, ALU.mult))
                step(tt(m_c[:, :, v, :], s5_tb[0], s5_tb[1], ALU.add))
            dve.sem_inc(s_c_ready, 1)
            for r in range(2 * NT):
                n, i = divmod(r, NT)
                dve.wait_ge(s_pgate_act, r + 1)
                dve.wait_ge(s_pproj_ready, r + 1)
                step(tt(gate_sb[r], gate_sb[r], ps[4 + r % 4][:], ALU.mult))
                v = rows[:, i, 512 * n:512 * (n + 1)]
                tt(v, v, gate_sb[r], ALU.add).then_inc(s_pproj_taken, 1)
            dve.wait_ge(s_sq, 4 * NT)
            row_rstd(EPS1)
            for i in range(NT):
                stt(nat3[:, i, :], rows[:, i, :], sm[:, 4 + i:5 + i], fnorm_bc, ALU.mult, ALU.mult).then_inc(s_nat_ready, 1)

            def low(n, k, hi):
                dve.wait_ge(s_h_hi, KD * (n - 1) + k + 1)
                tt(h_lo[:, k, :], ca[:, k, :], whole(hi[:, k, :]), ALU.subtract).then_inc(s_h_lo, 1)

            def norm(n, scale, v, hi=None):
                dve.wait_ge(s_ss_ps, n + 1)
                step(ts(v, ps[6][:], 1.0 / D, EPS2, ALU.mult, ALU.add))
                rsqrt(n_y, v, n_t)
                for k in range(KD):
                    stt(ca[:, k, :], xt[:, k, :], scale(k), n_y, ALU.mult, ALU.mult).then_inc(s_hs_ready, 1)
                    if hi is not None and k >= 2:
                        low(n, k - 2, hi)
                if hi is not None:
                    low(n, KD - 2, hi)
                    low(n, KD - 1, hi)

            norm(0, lambda k: scale1[:, 0, k:k + 1], n_v[0])

            rot_c3, rot_s3 = [v.rearrange("p (j c) -> p j c", j=GP) for v in (rot_c, rot_s)]
            dve.wait_ge(s_nat_ready, 4 * NT)
            dve.wait_ge(s_b_ready, 1)
            half = [NS, GP, NC]
            for two in range(2):
                pp = slice(NS * two, NS * (two + 1))
                step(tt(rot_s3[pp], par[pp, 5, two:G:2].unsqueeze(2).broadcast_to(half),
                        chunk[pp].unsqueeze(1).broadcast_to(half), ALU.mult))
            reduce_angle(rot_s, rot_s, z_im)
            cosine_angle(rot_c, rot_s, z_im)
            dve.sem_inc(s_rot_ready, 1)
            mag3 = mag_sb.rearrange("p (j c) -> p j c", j=GP)
            dve.wait_ge(s_k_out, 16 * (CH + 1))
            for two in range(2):
                pp = slice(NS * two, NS * (two + 1))
                step(dve.tensor_copy(mag3[pp], par[pp, 4, two:G:2].unsqueeze(2).broadcast_to(half)))
            step(dve.memset(mag3[:, :, 0:1], 0.0))
            dve.wait_ge(s_rot_done, 2)
            t1, t2 = tmp1[:, 0:512], tmp1[:, 512:1024]
            for b in range(4):
                dve.wait_ge(s_ws_ps, b + 1)
                c, sn = rot_c[:, 512 * b:512 * (b + 1)], rot_s[:, 512 * b:512 * (b + 1)]
                wr, wi = ps[2 * b][:], ps[2 * b + 1][:]
                step(tt(t1, wr, c, ALU.mult))
                step(tt(t2, wi, sn, ALU.mult))
                step(tt(z_re[:, 512 * b:512 * (b + 1)], t1, t2, ALU.add))
                step(tt(t1, wi, c, ALU.mult))
                step(tt(t2, wr, sn, ALU.mult))
                step(tt(z_im[:, 512 * b:512 * (b + 1)], t1, t2, ALU.subtract))
            step(dve.tensor_tensor_scan(tmp1, mag_sb, z_re, 0.0, ALU.mult, ALU.add))
            step(dve.tensor_tensor_scan(tmp2, mag_sb, z_im, 0.0, ALU.mult, ALU.add))
            def later(r, op):
                zv, wv = [v.rearrange("p (j c) -> p j c", j=GP)[:, :, 0:NC - 1] for v in (z_re, z_im)]
                for two in range(2):
                    pp = slice(NS * two, NS * (two + 1))
                    step(tt(x_s[NS * r:NS * (r + 1), two:G:2, 1:NC], zv[pp], wv[pp], op))

            step(dve.memset(x_s[:, :, 0:1], 0.0))
            step(tt(z_re, tmp1, rot_c, ALU.mult))
            step(tt(z_im, tmp2, rot_s, ALU.mult))
            later(0, ALU.subtract)
            step(tt(z_re, tmp1, rot_s, ALU.mult))
            step(tt(z_im, tmp2, rot_c, ALU.mult))
            later(1, ALU.add)
            dve.sem_inc(s_x_state, 1)
            y_g, sq_g, sg = tmp2[:, 0:512], tmp2[:, 512:1024], tmp2[:, 1024:1536]
            for k in range(KD):
                dve.wait_ge(s_yt_ps, k + 1)
                dve.wait_ge(s_gelu_ready, k)
                ins = stt(y_g, ca[:, k, :], vcol("ssm_d_2", k), ps[4 + k % 2][:], ALU.mult, ALU.add)
                ins.then_inc(s_yt_used, 1)
                dve.wait_ge(s_yt_used, k + 1)
                step(tt(sq_g, y_g, y_g, ALU.mult))
                step(ts(sq_g, sq_g, GELU_C, 1.0, ALU.mult, ALU.add))
                tt(sq_g, sq_g, y_g, ALU.mult).then_inc(s_gl_in, 1)
                dve.wait_ge(s_gl_s, k + 1)
                tt(cb3[:, k, :], y_g, sg, ALU.mult).then_inc(s_gelu_ready, 1)

            def each_tile(n, per, body, extra=None):
                n0 = step.n
                pairs = linear[n][3] // 2

                def pair(i):
                    step.n, step.off = n0, i * per
                    if extra:
                        extra(i)
                    for b in range(2):
                        dve.wait_ge(s_lin_taken, 2 * i + b + lin_base[n] + 2)
                        body(i, b, 2 * i + b, bass.ds(2 * i + b, 1))
                        if n in split and not (isinstance(i, int) and i == pairs - 1):
                            weights_low(n, i + 1, b)
                    assert step.n == n0 + per

                with dve.Fori(0, pairs - (n in split)) as i:
                    pair(i)
                if n in split:
                    pair(pairs - 1)
                step.n, step.off = n0 + per * pairs, 0

            def weights_low(n, i, b):
                parts, buf = linear[n][2], linear[n][4]
                for v in range(len(parts)):
                    dve.wait_ge(s_w_hi, 2 * len(parts) * i + hi_before[n] + len(parts) * b + v + 1)
                    tt(split[n][1][b][:, v], buf[b][:, v], whole(split[n][0][b][:, v]), ALU.subtract).then_inc(s_w_lo, 1)

            def first_low(n):
                for b in range(2):
                    weights_low(n, 0, b)

            sig_n = {GLU: 0, FIN0: KD, CIN: KD + KF, FIN1: 2 * KD + KF}

            def clear_squares():
                step(dve.memset(sq_acc, 0.0))
                step(dve.memset(sq_t[1], 0.0))

            def add_square(m, i, b):
                dve.wait_ge(s_sqt, 2 * i + KD * m + b + 1)
                dve.wait_ge(s_sq_used, 2 * i + KD * m + b + 1)
                tt(sq_acc, sq_acc, sq_t[1 - b], ALU.add).then_inc(s_sq_used, 1)

            def glu(i, b, t, at):
                dve.wait_ge(s_lin_sig, t + sig_n[GLU] + 1)
                step(stt(lin_t[b], ps[3 * b][:], mods[:, 0, bass.ds(2 * i + 16 + b, 1)], sig_sb[b], ALU.mult, ALU.mult))
                x = flat(xt[:, at, :])
                tt(x, x, lin_t[b], ALU.add).then_inc(s_lin_taken, 1)
                add_square(0, i, b)

            def hidden(n):
                def body(i, b, t, at):
                    dve.wait_ge(s_lin_sig, t + sig_n[n] + 1)
                    step(tt(lin_t[b], ps[3 * b][:], sig_sb[b], ALU.mult))
                    tt(flat(f_act[:, at, :]), ps[3 * b + 1][:], lin_t[b], ALU.mult).then_inc(s_lin_taken, 1)
                return body

            def residual(m, n, layer, gate):
                def body(i, b, t, at):
                    dve.wait_ge(s_lin_ready, t + lin_base[n] + 1)
                    x = flat(xt[:, at, :])
                    stt(x, ps[3 * b][:], mods[:, layer, bass.ds(2 * i + gate + b, 1)], x, ALU.mult,
                        ALU.add).then_inc(s_lin_taken, 1)
                    add_square(m, i, b)
                return body

            def ada1_pair(i):
                for c in range(2):
                    for k in range(KD):
                        t = KD * c + k
                        before = sum(1 for u in range(t) if u % 3 == t % 3)
                        total = sum(1 for u in range(2 * KD) if u % 3 == t % 3)
                        dve.wait_ge(s_ada1_in[t % 3], 16 * total * i + 16 * (before + 1))
                        if k == 0:
                            dve.wait_ge(s_ada1_sum, 2 * i + c + 1)
                        ada_tile(ada_acc, ada_w[t % 3], k).then_inc(s_ada1_used, 1)
                        dve.wait_ge(s_ada1_used, 2 * KD * i + t + 1)

            cx = conv_x.rearrange("p s c -> p (s c)")

            def conv(i, b, t, at):
                def w(tap):
                    return vec[:, bass.ds(2 * i + VEC["conv_w_2"][0] + KD * tap + b, 1)]

                dve.wait_ge(s_lin_sig, t + sig_n[CIN] + 1)
                step(tt(cx[:, 2 * NC:], ps[3 * b + 2][:], sig_sb[b], ALU.mult))
                step(dve.tensor_copy(conv_x[:, 0:2, 1:NC], conv_x[:, CH:CH + 2, 0:NC - 1]))
                step(ts(lin_t[b], cx[:, 0:S], w(0), None, ALU.mult))
                step(stt(lin_t[b], cx[:, NC:NC + S], w(1), lin_t[b], ALU.mult, ALU.add))
                step(stt(lin_t[b], cx[:, 2 * NC:], w(2), lin_t[b], ALU.mult, ALU.add))
                tt(flat(cb3[:, at, :]), lin_t[b], ps[3 * b][:], ALU.mult).then_inc(s_lin_taken, 1)

            first_low(FIN0)
            clear_squares()
            each_tile(GLU, 2, glu)
            norm(1, lambda k: scale1[:, 0, 8 + k:9 + k], n_v[1], fin_h)
            each_tile(FIN0, 2, hidden(FIN0))
            first_low(CIN)
            clear_squares()
            each_tile(FOUT0, 0, residual(1, FOUT0, 0, 40), ada1_pair)
            dve.wait_ge(s_ada1_sum, ADA_C + 1)
            finish_mods(1)
            dve.sem_inc(s_mods1, 1)
            norm(2, lambda k: scale1[:, 1, k:k + 1], n_v[1], cin_h)
            step(dve.memset(conv_x[:, 0:2, 0:1], 0.0))
            each_tile(CIN, 10, conv)
            first_low(FIN1)
            clear_squares()
            each_tile(COUT, 0, residual(2, COUT, 1, 16))
            norm(3, lambda k: scale1[:, 1, 8 + k:9 + k], n_v[1], fin_h)
            each_tile(FIN1, 2, hidden(FIN1))
            clear_squares()
            each_tile(FOUT1, 0, residual(3, FOUT1, 1, 40))
            norm(4, lambda k: vcol("final_g_2", k), n_v[1])

        @block.tensor
        def _(pe):
            mm = pe.matmul
            pe.sem_inc(s_ada1_sum, 1)
            rounds = [0]

            def column(tiles):
                r = rounds[0]
                rounds[0] += 1
                if r >= 2:
                    pe.wait_ge(s_cols_taken, r - 1)
                at = 0
                for src in tiles:
                    n = src.shape[0]
                    m = src.free_size()
                    last = pe.transpose(ps[4 + r % 2][0:m, at:at + n], src, ident[0:n, 0:n])
                    at += n
                last.then_inc(s_cols_ready, 1)

            def columns_of(v, tiles=KD):
                for k in range(tiles):
                    column([v[:, i, P * k:P * (k + 1)] for i in range(NT)])

            pe.wait_ge(s_const_in, 16)
            pe.wait_ge(s_vec_in, 16 * (len(VEC) + 1))
            pe.transpose(ps[6][:, 0:NVEC], vec_rows[0:NVEC, :], ident[0:NVEC, 0:NVEC])
            pe.transpose(ps[6][:, P:P + NADA], ada_rows[0:NADA, :], ident[0:NADA, 0:NADA]).then_inc(s_vec_t, 1)
            pe.wait_ge(s_nat_ready, NT)
            columns_of(nat3)
            def ada_sum(layer, c, acc, done, wait):
                wait()
                for t in range(ADA_N // P):
                    last = mm(ps[7][:, c * (ADA_N // P) + t:c * (ADA_N // P) + t + 1], acc[:, P * t:P * (t + 1)],
                              ones[:, 0:1], start=True, stop=True)
                last.then_inc(done, 1)

            pe.wait_ge(s_cols_taken, KD)
            for r in range(5 * NT):
                n, i = divmod(r, NT)
                if i == 0:
                    pe.wait_ge(s_mix_in[n % 3], 16 * (n // 3 + 1))
                if r >= NT:
                    pe.wait_ge(s_proj_taken, r - NT + 1)
                for k in range(KD):
                    last = mm(ps[i][:], ca[:, k, P * i:P * (i + 1)], w_in_sb[n][:, k, :], start=(k == 0), stop=(k == KD - 1))
                last.then_inc(s_proj_ready, 1)
                c = r // 2 - 2
                if r % 2 == 0 and 0 <= c < ADA_C:
                    ada_sum(0, c, ada_acc, s_ada_sum, lambda: pe.wait_ge(s_ada_used, KD * (c + 1)))
            pe.wait_ge(s_s5_par, 1)
            pe.wait_ge(s_vec_ok, 2)
            for v in range(6):
                last = pe.transpose(ps[6][:, G * v:G * (v + 1)], s5r[:, 20 + v, :], ident[0:G, 0:G])
            last.then_inc(s_s5_tr, 1)
            pe.wait_ge(s_proj_taken, 5 * NT)
            pe.wait_ge(s_ret_in, 48)
            pe.wait_ge(s_par_ok, 1)
            for g in range(4):
                if g >= 1:
                    pe.wait_ge(s_pool_sb, g)
                for i in range(NT):
                    def u(j):
                        return proj[:, j, 4 * RET + P * g:4 * RET + P * (g + 1)]

                    dst = ps[6][:, P * i:P * (i + 1)]
                    last = mm(dst, u(i), band[:, g, min(i, 1), :], start=True, stop=(i == 0))
                    if i:
                        last = mm(dst, u(i - 1), band[:, g, 2, :], start=False, stop=True)
                last.then_inc(s_pool_ps, 1)
                pe.wait_ge(s_pool_sb, g + 1)
                if g >= 1:
                    pe.wait_ge(s_mix_sb, g)
                mm(ps[7][:], pool_w_sb[:, g, :], pooled[g % 2], start=True, stop=True).then_inc(s_mix_ps, 1)
            pe.wait_ge(s_rope_ready, NT)
            columns_of(nat3)
            pe.wait_ge(s_cols_taken, 2 * KD)
            pe.wait_ge(s_mix_sb, 4)

            def scores(h):
                pp = slice(HD * (h % 2), HD * (h % 2 + 1))
                for j in range(NT):
                    if h >= 1:
                        pe.wait_ge(s_score_sb, NT * (h - 1) + j + 1)
                    mm(ps[4 + j][:, 0:S - P * j], cb3[pp, 4 + h // 2, P * j:P * (j + 1)], cb3[pp, h // 2, P * j:S],
                       start=True, stop=True).then_inc(s_score_ps, 1)

            def values(h):
                pe.wait_ge(s_score_sb, NT * (h + 1))
                for i in range(NT):
                    for j in range(i + 1):
                        at = SCORE_AT[j] + P * (i - j)
                        last = mm(ps[i][:, HD * h:HD * (h + 1)], scr_s[h % 2][:, at:at + P],
                                  proj[:, j, 2 * RET + HD * h:2 * RET + HD * (h + 1)], start=(j == 0), stop=(j == i))
                last.then_inc(s_y_ps, 1)

            scores(0)
            for h in range(HEADS):
                if h + 1 < HEADS:
                    scores(h + 1)
                values(h)
            pe.wait_ge(s_ret_ready, 1)
            columns_of(nat[:].rearrange("p (two i d) -> p two i d", two=2, i=NT)[:, 0], 4)
            pe.wait_ge(s_cols_taken, 2 * KD + 4)
            for r in range(2 * NT):
                n, i = divmod(r, NT)
                if i == 0:
                    pe.wait_ge(s_mix_in[(n + 5) % 3], 16 * ((n + 5) // 3 + 1))
                if r >= NT:
                    pe.wait_ge(s_wout_taken, r - NT + 1)
                for k in range(KD):
                    last = mm(ps[i][:], ca[:, k, P * i:P * (i + 1)], w_out_sb[n][:, k, :], start=(k == 0), stop=(k == KD - 1))
                last.then_inc(s_wout_ready, 1)
            pe.wait_ge(s_nat_ready, 2 * NT)
            columns_of(nat3)
            pe.wait_ge(s_norm_in, 64)
            pe.wait_ge(s_cols_taken, 3 * KD + 4)
            for i in range(NT):
                for k in range(KD):
                    last = mm(ps[6][:, E * i:E * (i + 1)], ca[:, k, P * i:P * (i + 1)], rw_sb[:, k, :],
                              start=(k == 0), stop=(k == KD - 1))
            last.then_inc(s_log_ps, 1)
            pe.wait_ge(s_mask_ready, 1)
            mask = route[:, MASK_AT:MASK_AT + NT * E].rearrange("p (i e) -> p i e", i=NT)
            for i in range(NT):
                for j in range(i):
                    mm(ps[7][:, E * i:E * (i + 1)], ones, mask[:, j, :], start=(j == 0), stop=False)
                mm(ps[7][:, E * i:E * (i + 1)], tri, mask[:, i, :], start=(i == 0), stop=True)
            for j in range(NT):
                last = mm(ps[7][:, E * NT:E * (NT + 1)], ones, mask[:, j, :], start=(j == 0), stop=(j == NT - 1))
            last.then_inc(s_rank_ps, 1)
            pe.wait_ge(s_route_ok, 1)

            def tokens_columns(tile):
                pe.wait_ge(s_xs_in, 16 * tile + 16)
                for r in range(2):
                    for k in range(4):
                        last = pe.transpose(ps[6 + r][:, P * k:P * (k + 1)], xs[:, P * (4 * r + k):P * (4 * r + k + 1)], ident)
                    last.then_inc(s_xt_ready, 1)

            def hidden_columns(tile, h):
                pe.wait_ge(s_act_ready, 2 * tile + h + 1)
                for k in range(4):
                    last = pe.transpose(ps[2 * h][:, P * k:P * (k + 1)], act_n[h][:, P * k:P * (k + 1)], ident)
                last.then_inc(s_actt_ps, 1)

            def biases(at, bank):
                for n in range(2):
                    mm(ps[bank + n][:], pick[:], bias_t[0:2 * E, at + 512 * n:at + 512 * (n + 1)], start=True, stop=False)

            def up(tile, h):
                biases(D * h, 2 * h)
                for k in range(KD):
                    q = 4 * h + k // 2
                    if k % 2 == 0:
                        pe.wait_ge(s_gu_lo, 8 * tile + q + 1)
                    hi, lo = gu_hi[q % 4][:, k % 2], gu_lo[:, q, k % 2]
                    for x, w in ((xs_hi, hi), (xs_lo, hi), (xs_hi, lo)):
                        for n in range(2):
                            last = mm(ps[2 * h + n][:], x[:, k, :], w[:, 512 * n:512 * (n + 1)],
                                      start=False, stop=(k == KD - 1 and w is lo))
                    if k % 2 and k < KD - 1:
                        last.then_inc(s_slot_free, 1)
                last.then_inc(s_gu_ready, 1)

            def down(tile, h):
                pe.wait_ge(s_actt_ready, 2 * tile + h + 1)
                if h == 0:
                    pe.wait_ge(s_y_sb, 2 * tile + 1)
                    biases(2 * D, 4)
                for k in range(4):
                    q = 8 + 2 * h + k // 2
                    if k % 2 == 0:
                        pe.wait_ge(s_slot_in[q], 16 * tile + 16)
                    for n in range(2):
                        last = mm(ps[4 + n][:], act_t[h][:, k, :], slot[q][:, k % 2, 512 * n:512 * (n + 1)],
                                  start=False, stop=(h == 1 and k == 3))
                    if k % 2 and not (h and k == 3):
                        last.then_inc(s_slot_free, 1)
                if h:
                    last.then_inc(s_y_ready, 1)

            def expert(tile):
                pe.wait_ge(s_pick, tile + 1)
                pe.wait_ge(s_xst_ready, 2 * tile + 2)
                up(tile, 0)
                up(tile, 1)
                hidden_columns(tile, 0)
                tokens_columns(tile + 1)
                down(tile, 0)
                hidden_columns(tile, 1)
                down(tile, 1)

            tokens_columns(0)
            pe.wait_ge(s_bias_ok, 1)
            with pe.Fori(0, E) as e:
                expert(e)
            extra = pe.value_load(smi[0:1, 72:73], min_val=0, max_val=MAX_EXTRA)
            with pe.If(extra > 0):
                with pe.Fori(0, extra) as n:
                    expert(n + E)

            pe.wait_ge(s_ple_in, 64)
            pe.wait_ge(s_moe_done, 1)
            columns_of(p_rows, 2)
            pe.wait_ge(s_nat_ready, 3 * NT)
            columns_of(nat3)
            pe.wait_ge(s_c_in, 64)
            for r in range(2):
                for q in range(2):
                    if r:
                        pe.wait_ge(s_ct_sb, 2 * q + 2)
                    for t in range(4):
                        last = pe.transpose(ps[q][:, P * t:P * (t + 1)], c_rows[r][:, 4 * q + t].rearrange("p two n -> p (two n)"), ident)
                    last.then_inc(s_ct_ps, 1)
            pe.wait_ge(s_cols_taken, COLS_PLE)
            pe.wait_ge(s_ct_sb, 8)
            for r in range(2 * NT):
                n, i = divmod(r, NT)
                if r >= NT:
                    pe.wait_ge(s_pgate_act, r - NT + 1)
                for k in range(KD):
                    last = mm(ps[i][:], ca[:, k, P * i:P * (i + 1)], ple_w_sb[n][:, k, :], start=(k == 0), stop=(k == KD - 1))
                last.then_inc(s_pgate_ready, 1)
            for r in range(2 * NT):
                n, i = divmod(r, NT)
                if r >= NT:
                    pe.wait_ge(s_pproj_taken, r - NT + 1)
                for k in range(2):
                    last = mm(ps[4 + i][:], p_cols[:, k, P * i:P * (i + 1)], ple_p_sb[:, k, 512 * n:512 * (n + 1)],
                              start=(k == 0), stop=(k == 1))
                last.then_inc(s_pproj_ready, 1)
            pe.wait_ge(s_b_ready, 1)
            pe.wait_ge(s_pproj_taken, 2 * NT - 2)
            for q in range(G // 4):
                column([m_b[:, 4 * q + j].rearrange("p s h -> p (s h)") for j in range(4)])
            pe.wait_ge(s_nat_ready, 4 * NT)
            for k in range(KD + 1):
                if k < KD:
                    column([nat3[:, i, P * k:P * (k + 1)] for i in range(NT)])
                if k >= 1:
                    pe.wait_ge(s_sq2, k)
                    last = mm(ps[6][:], ones, ca[:, k - 1, :], start=(k == 1), stop=(k == KD))
            last.then_inc(s_ss_ps, 1)

            def norm_sums(n):
                pe.wait_ge(s_sq_used, KD * n + 1)
                mm(ps[6][:], ones, sq_acc, start=True, stop=False)
                pe.wait_ge(s_sqt, KD * n + 1)
                mm(ps[6][:], ones, sq_t[1], start=False, stop=True).then_inc(s_ss_ps, 1)

            pe.wait_ge(s_pgate_act, 2 * NT)
            for g in range(G):
                last = mm(ps[g // GP][:, GC * (g % GP):GC * (g % GP + 1)], m_b[:, g].rearrange("p s h -> p (s h)"),
                          s5c[0][:, g, :], start=True, stop=True)
            last.then_inc(s_k_ps, 1)
            pe.wait_ge(s_u_in, 16 * CH)
            pe.wait_ge(s_hs_ready, KD)
            pe.wait_ge(s_cols_taken, COLS_XT)
            pe.wait_ge(s_k_sb, 3)
            for b in range(4):
                for r in range(2):
                    for j in range(8 * b, 8 * b + 8):
                        for two in range(2):
                            pp = slice(NS * two, NS * (two + 1))
                            last = mm(ps[2 * b + r][pp, NC * (j % 8):NC * (j % 8 + 1)], m_w[:, 2 * j + two, NS * r:NS * (r + 1)], u_sb[:, 2 * j + two, :],
                                      start=True, stop=True)
                last.then_inc(s_ws_ps, 1)
            pe.wait_ge(s_x_state, 1)
            pe.wait_ge(s_t_in, 16 * CH)
            pe.wait_ge(s_c_ready, 1)

            def chunk_rows(k):
                if k >= 2:
                    pe.wait_ge(s_yo_sb, 2 * k - 2)
                for j in range(4 * k, 4 * k + 4):
                    for two in range(2):
                        dst = ps[2 * (k % 2) + two][0:NC, P * (j % 4):P * (j % 4 + 1)]
                        mm(dst, u_sb[:, 2 * j + two, :], m_t[:, 2 * j + two, :], start=True, stop=False)
                        last = mm(dst, x_s[:, 2 * j + two, :], m_c[:, 2 * j + two].rearrange("p s h -> p (s h)"), start=False, stop=True)
                last.then_inc(s_yo_ps, 1)

            def chunk_columns(k):
                pe.wait_ge(s_yo_sb, 2 * k + 2)
                if k >= 2:
                    pe.wait_ge(s_yt_used, k - 1)
                for v in range(CH):
                    last = pe.transpose(ps[4 + k % 2][:, NC * v:NC * (v + 1)], y_ch[k % 2][:, v, :], ident[0:NC, 0:NC])
                last.then_inc(s_yt_ps, 1)

            chunk_rows(0)
            for k in range(KD):
                if k + 1 < KD:
                    chunk_rows(k + 1)
                chunk_columns(k)

            def products(n, ready, before, extra=None):
                src, _, parts, tiles, buf = linear[n]
                depth = KF if src is f_act else KD

                def tile(i, b, first=False):
                    if n in split:
                        w_hi, w_lo, x_hi = split[n]
                        pe.wait_ge(s_w_lo, 2 * len(parts) * i + hi_before[n] + len(parts) * (b + 1))
                    else:
                        pe.wait_ge(s_lin_in[n % 4][b], 16 * len(parts) * i + lin_before[n] + 16 * len(parts))
                    pe.wait_ge(s_lin_taken, 2 * i + lin_base[n] + b + 1)
                    for v in range(len(parts)):
                        for k in range(depth):
                            if first and v == 0:
                                pe.wait_ge(ready, before + k + 1)
                            dst, a, z = ps[3 * b + v][:], k == 0, k == depth - 1
                            if n in split:
                                mm(dst, w_hi[b][:, v, k, :], x_hi[:, k, :], start=a, stop=False)
                                mm(dst, w_hi[b][:, v, k, :], h_lo[:, k, :], start=False, stop=False)
                                last = mm(dst, w_lo[b][:, v, k, :], x_hi[:, k, :], start=False, stop=z)
                            else:
                                last = mm(dst, buf[b][:, v, k, :], src[:, k, :], start=a, stop=z)
                    last.then_inc(s_lin_ready, 1)
                    if extra:
                        extra(i, b)

                tile(0, 0, first=True)
                tile(0, 1)
                with pe.Fori(1, tiles // 2) as i:
                    for b in range(2):
                        tile(i, b)

            def ada1_sum(i, b):
                pe.wait_ge(s_ada1_used, 2 * KD * i + KD * (b + 1))
                per = ADA_N // P
                for t in range(per):
                    last = mm(ps[7][:, bass.ds(2 * per * i + per * b + t, 1)], ada_acc[:, P * t:P * (t + 1)], ones[:, 0:1],
                              start=True, stop=True)
                last.then_inc(s_ada1_sum, 1)

            products(GLU, s_gelu_ready, 0)
            norm_sums(1)
            products(FIN0, s_h_lo, 0)
            products(FOUT0, s_lin_taken, lin_base[FIN0] + 2, ada1_sum)
            norm_sums(2)
            products(CIN, s_h_lo, KD)
            products(COUT, s_lin_taken, lin_base[CIN] + 2)
            norm_sums(3)
            products(FIN1, s_h_lo, 2 * KD)
            products(FOUT1, s_lin_taken, lin_base[FIN1] + 2)
            norm_sums(4)
            for i in range(NT):
                for h in range(2):
                    pe.wait_ge(s_hs_ready, 4 * KD + 4 * h + 4)
                    column([ca[:, 4 * h + k, P * i:P * (i + 1)] for k in range(4)])


def _constants():
    import numpy as np

    consts = np.zeros((P, NCONST), np.float32)

    def put(name, value):
        lo, hi = CONST[name]
        consts[:, lo:hi] = value

    t = np.arange(P)
    put("ident", np.eye(P))
    put("ones", 1.0)
    put("tri", t[:, None] < t[None, :])
    put("iota", np.arange(32)[None, :])
    put("freq", (10000.0 ** (-np.arange(32) / 32.0))[None, :])
    put("token", t[:, None] + P * np.arange(NT)[None, :])
    put("chunk", np.arange(NC)[None, :])
    put("pick", t[:, None] % E == np.arange(E)[None, :])
    gamma = np.log1p(-(2.0 ** (-5.0 - np.arange(HEADS))))
    lag = np.arange(S)[None, :] - t[:, None]
    decay = np.where(lag[:, None, :] >= 0, np.exp(np.maximum(lag, 0)[:, None, :] * gamma[None, :, None]), 0.0)
    decay = (decay * HD ** -0.5).astype(np.float32).reshape(P, HEADS * S)
    band = np.zeros((P, len(WINDOWS), 3, P), np.float32)
    for g, w in enumerate(WINDOWS):
        back = t[None, :] - t[:, None]
        inside = (back >= 0) & (back < w)
        band[:, g, 0] = inside / np.minimum(t + 1, w)[None, :] - np.eye(P)
        band[:, g, 1] = inside / w - np.eye(P)
        band[:, g, 2] = (back + P < w) / w
    return {"consts": consts, "decay": decay, "band": band.reshape(P, -1)}


_INS = ["x", "p", "positions", "w_in", "w_out", "ret_gn_w", "pool_w", "pool_scale", "norm_mix_w", "norm_moe_w",
        "router_w", "router_b", "expert_w_gate_up", "expert_b_gate_up", "expert_w_down", "expert_b_down",
        "norm_ple_w", "ple_gate_w", "ple_proj_w", "final_norm_w", "c_2", "norm1_g_2", "norm2_g_2", "w_ada_2",
        "b_ada_2", "ssm_a_re_2", "ssm_a_im_2", "ssm_log_step_2", "ssm_b_re_2", "ssm_b_im_2", "ssm_c_re_2",
        "ssm_c_im_2", "ssm_d_2", "ssm_w_out_2", "conv_w_in_2", "conv_w_2", "conv_w_out_2", "w_ffn_in_2",
        "w_ffn_out_2", "final_g_2"]


def kernel(**inputs):
    import numpy as np
    import concourse.bacc as bacc
    from concourse.bass_utils import run_bass_kernel_spmd

    nc = bacc.Bacc("TRN2", target_bir_lowering=False, num_devices=1)
    arrays = {name: np.ascontiguousarray(inputs[name]) for name in _INS}
    arrays.update(_constants())
    aps = {name: nc.dram_tensor(f"in_{name}", v.shape, mybir.dt.from_np(v.dtype), kind="ExternalInput").ap()
           for name, v in arrays.items()}
    out = nc.dram_tensor("out", (1, S, D), F32, kind="ExternalOutput").ap()
    program(nc, aps, out)
    got = run_bass_kernel_spmd(nc, [{f"in_{name}": v for name, v in arrays.items()}], core_ids=[0])
    return got.results[0]["out"]
```

```python
from contextlib import ExitStack

import concourse.bass as bass
from concourse import mybir

F32 = mybir.dt.float32
F32R = mybir.dt.float32r
I32 = mybir.dt.int32
U32 = mybir.dt.uint32
ALU = mybir.AluOpType
ACT = mybir.ActivationFunctionType
AXX = mybir.AxisListType.X

P = 128
S = 512
D = 1024
NT = S // P
KD = D // P
HEADS, HD = 8, 64
RET = HEADS * HD
NPROJ = 4 * RET + (D - RET)
WINDOWS = (2, 4, 8, 16)
E, TOPK = 32, 4
MAX_EXTRA = S * TOPK // P - 1
TILES = E + MAX_EXTRA + 1
G, GC, NS = 64, 16, 64
CH = P // GC
NC = S // CH
GP = G // 2
FF = 2816
KF = FF // P
EPS1, EPS2 = 1e-5, 1e-6
LIMIT, ALPHA = 7.0, 1.702
PI = 3.14159265358979
TWO_PI = (6.28125, 1.93500518798828125e-3, 3.019915981956753e-7)
MAGIC = 12582912.0
PI_IN = 3.1415925
RSQRT_SEED = 0x5F3759DF
GELU_C, GELU_S = 0.044715, 1.5957691216057308

VEC = {}
_at = 0
for _name, _rows in (("norm_mix_w", 8), ("ret_gn_w", 4), ("pool_scale", 4), ("norm_ple_w", 8),
                     ("norm1_g_2", 16), ("norm2_g_2", 16), ("ssm_d_2", 8), ("conv_w_2", 24),
                     ("final_g_2", 8), ("c_2", 8)):
    VEC[_name] = (_at, _rows)
    _at += _rows
NVEC = _at
NADA = 96
ADA_N = 768
ADA_C = 6 * D // ADA_N

CONST = {}
_at = 0
for _name, _cols in (("ident", P), ("ones", P), ("tri", P), ("iota", P), ("freq", 32), ("token", NT),
                     ("pick", E)):
    CONST[_name] = (_at, _at + _cols)
    _at += _cols
NCONST = _at


COLS_ROUTE = KD + KD + 4 + KD
COLS_PLE = COLS_ROUTE + 2 + KD
COLS_XT = COLS_PLE + G // 4 + KD
SCORE_AT = (0, 512, 896, 1152)
MASK_AT = NT * E + 2 * NT * TOPK * E
MIXED = (4, 5, 6, 7, 0, 1, 2, 3)
LINEAR = ("glu", "fin0", "fout0", "cin", "cout", "fin1", "fout1")


class Steps:

    def __init__(self, eng, sem):
        self.eng, self.sem, self.n, self.off = eng, sem, 0, 0

    def __call__(self, ins):
        ins.then_inc(self.sem, 1)
        self.n += 1
        self.eng.wait_ge(self.sem, self.n + self.off)


def program(nc, a, out):
    with ExitStack() as ctx:
        place = {}

        def sb(name, shape, dt=F32):
            place[name] = -(-nc.sbuf_base // 32) * 32
            return ctx.enter_context(nc.sbuf_tensor(name, shape, dt))

        def parts_at(name, region, first, cols):
            return nc.alloc_sbuf_tensor_at(name, [P, cols], F32R, offset=place[region] + 4 * first)

        def sem(name):
            return ctx.enter_context(nc.semaphore(name))

        ps = [ctx.enter_context(nc.psum_tensor(f"bank{i}", [P, 512], F32)) for i in range(8)]

        ring = sb("ring", [P, 24576])
        rows = sb("rows", [P, NT, D])
        nat = sb("nat", [P, 4096])
        ca = sb("ca", [P, KD, S])
        cb = sb("cb", [P, 4096])
        work = sb("work", [P, 10240])
        const = sb("const", [P, NCONST])
        vec = sb("vec", [P, NVEC + NADA])
        mods = sb("mods", [P, 2, 48])
        scale1 = sb("scale1", [P, 2, 16])
        cact = sb("cact", [P, 8])
        sm = sb("sm", [P, 208])
        smi = sb("smi", [P, 216], I32)
        ident, ones, tri, iota, freq, token, pick_e = (
            const[:, x:y] for x, y in CONST.values())

        def vcol(name, k):
            return vec[:, VEC[name][0] + k:VEC[name][0] + k + 1]

        nat3 = nat[:].rearrange("p (i d) -> p i d", i=NT)
        cb3 = cb[:].rearrange("p (k t) -> p k t", k=KD)
        ca_rows = ca[:].rearrange("p k t -> p (k t)").rearrange("p (i d) -> p i d", i=NT)

        w_in_sb = [ring[:, n * 4096:(n + 1) * 4096].rearrange("p (k n) -> p k n", k=KD) for n in (0, 1, 0, 1, 0)]
        w_in_lo, w_in_hi = [[parts_at(f"w_in_{name}{n}", "ring", first, 4096)[:].rearrange("p (k n) -> p k n", k=KD)
                             for n, first in enumerate(at)] for name, at in (("lo", (0, 4096)), ("hi", (8192, 20480)))]
        mix_hi = parts_at("mix_hi", "ring", 16384, KD * S)[:].rearrange("p (k t) -> p k t", k=KD)
        mix_lo = parts_at("mix_lo", "ca", 0, KD * S)[:].rearrange("p (k t) -> p k t", k=KD)
        w_out_sb = [ring[:, n * 4096:(n + 1) * 4096].rearrange("p (k n) -> p k n", k=KD) for n in (2, 0)]
        w_out_lo = [parts_at(f"w_out_lo{n}", "ring", first, 4096)[:].rearrange("p (k n) -> p k n", k=KD)
                    for n, first in enumerate((8192, 0))]
        w_out_hi = [parts_at(f"w_out_hi{n}", "ring", first, 4096)[:].rearrange("p (k n) -> p k n", k=KD)
                    for n, first in enumerate((12288, 4096))]
        mixed_lo = parts_at("mixed_lo", "ca", 0, KD * S)[:].rearrange("p (k t) -> p k t", k=KD)
        mixed_hi = [parts_at(f"mixed_hi{k}", "work", NPROJ * (k // 2) + S * (k % 2), S)[:] for k in range(KD)]
        pooled = [ring[:, 12288 + 512 * b:12288 + 512 * (b + 1)] for b in range(2)]
        decay = ring[:, 16384:20480].rearrange("p (h t) -> p h t", h=HEADS)
        band = ring[:, 20480:22016].rearrange("p (g v t) -> p g v t", g=4, v=3)
        scr_s = [ring[:, 22016 + 1280 * b:22016 + 1280 * (b + 1)] for b in range(2)]
        pool_w_sb = ring[:, 13312:13824].rearrange("p (g d) -> p g d", g=4)
        trig = ring[:, 13824:13824 + 1024].rearrange("p (v i f) -> p v i f", v=8, i=NT)
        proj = work[:].rearrange("p (i n) -> p i n", i=NT)
        ada_acc = [cb[:, 0:ADA_N], cb[:, 4 * ADA_N:5 * ADA_N]]
        ada_w = [cb[:, ADA_N * (b + 1):ADA_N * (b + 2)] for b in range(3)] + [ring[:, 12288:12288 + ADA_N]]
        vec_rows, ada_rows = ca[:, 0, 0:P], ca[:, 0, P:2 * P]
        qkr = nat[:].rearrange("p (i h two f) -> p i h two f", i=NT, h=2 * HEADS, two=2)
        s5r = nat[0:G, :].rearrange("p (v n) -> p v n", n=P)
        rope_t = [ring[:, 14848 + 512 * b:15360 + 512 * b].rearrange("p (h f) -> p h f", f=32) for b in range(2)]
        ret_y = nat[:, 0:2048].rearrange("p (n e) -> p n e", e=HD)
        ret_sq = nat[:, 2048:4096].rearrange("p (n e) -> p n e", e=HD)
        silu_g = ca[:, 0:4, :]
        route = work[:, 5120:10240]
        row_hot = work[:, 3072:5120].rearrange("p (n r) -> p n r", r=P)
        tile_token = cb[:, 1024:1024 + NT * TOPK * TILES].rearrange("p (n t) -> p n t", t=TILES)
        c_rows = [ring[:, 2048 + 1024 * r:3072 + 1024 * r].rearrange("p (t two n) -> p t two n", t=8, two=2) for r in range(2)]
        b_in = [ring[:, 1024 * r:1024 * (r + 1)].rearrange("p (g h) -> p g h", g=G) for r in range(2)]
        i_bbar = work[:, 0:1024].rearrange("p (g h) -> p g h", g=G)
        s5_ta = [work[:, 1024 * (r + 1):1024 * (r + 2)].rearrange("p (g h) -> p g h", g=G) for r in range(2)]
        s5_tb = [work[:, 5120 + 1024 * r:6144 + 1024 * r].rearrange("p (g h) -> p g h", g=G) for r in range(2)]
        k_sb = cb[:, 1024:2048].rearrange("p (g h) -> p g h", g=G)
        p_t = [sb(f"power_t{r}", [P, G])[:] for r in range(2)]
        k_zero = cb[0:GC, 2560:2560 + (CH - 1) * GC]

        slot = [ring[:, 2048 * s:2048 * (s + 1)].rearrange("p (k n) -> p k n", k=2) for s in range(12)]
        bias_rows = nat[0:2 * E, 0:3 * D]
        xs = work[:, 3072:4096]
        gu_lo = parts_at("gu_lo", "ring", 0, 8 * 2048)[:].rearrange("p (q k n) -> p q k n", q=8, k=2)
        gu_hi = [v for region in ("ca", "nat")
                 for v in [parts_at(f"gu_hi_{region}", region, 0, 4096)[:].rearrange("p (q k n) -> p q k n", q=2, k=2)]]
        gu_hi = [gu_hi[q // 2][:, q % 2] for q in range(4)]
        xs_hi = parts_at("xs_hi", "work", 4096, D)[:].rearrange("p (k t) -> p k t", k=KD)
        xs_lo = parts_at("xs_lo", "cb", 1024, D)[:].rearrange("p (k t) -> p k t", k=KD)
        bias_t = parts_at("bias_parts", "work", 0, 3 * D)
        pick = sb("pick", [2 * E, P], F32R)
        t_g = [work[:, 5120 + 512 * h:5632 + 512 * h] for h in range(2)]
        t_u = [work[:, 6144 + 512 * h:6656 + 512 * h] for h in range(2)]
        t_s = [work[:, 7168 + 512 * h:7680 + 512 * h] for h in range(2)]
        act_n = [work[:, 8192 + 512 * h:8704 + 512 * h] for h in range(2)]
        act_t = [work[:, 9216 + 512 * h:9728 + 512 * h].rearrange("p (k t) -> p k t", k=4) for h in range(2)]
        y_sb = cb[:, 0:1024]
        rw_sb = cb[:, 1024:1280].rearrange("p (k e) -> p k e", k=KD)
        norm_bc = cb[:, 2048:3072]
        fnorm_bc = cb[:, 3072:4096]
        rb_bc = cb[:, 1280:1312]
        got = [ring[:, 16384 + 1024 * n:16384 + 1024 * (n + 1)] for n in range(8)] + \
              [v[:, 1024 * n:1024 * (n + 1)] for v in (work, nat) for n in range(4)]

        ple_w_sb = [ring[:, 8192 + 4096 * n:12288 + 4096 * n].rearrange("p (k n) -> p k n", k=KD) for n in range(2)]
        ple_p_sb = work[:, 8192:10240].rearrange("p (k n) -> p k n", k=2)
        p_rows = ring[:, 4096:5120].rearrange("p (i d) -> p i d", i=NT)
        p_cols = cb[:, 1024:2048].rearrange("p (k t) -> p k t", k=2)
        gate_sb = [nat[:, 512 * b:512 * (b + 1)] for b in range(8)]

        m_c = ring[:, 0:8192].rearrange("p (g s h) -> p g s h", g=G, s=CH)
        m_w = ring[:, 8192:16384].rearrange("p (g m) -> p g m", g=G)
        m_b = ring[:, 16384:24576].rearrange("p (g s h) -> p g s h", g=G, s=CH)
        m_t = ring[:, 16384:24576].rearrange("p (g m) -> p g m", g=G)
        power = cb[:, 2048:3072].rearrange("p (r v g) -> p r v g", r=2, v=CH)
        xt = work[:, 0:4096].rearrange("p (k t) -> p k t", k=KD)
        flat_rows = rows[:].rearrange("p i d -> p (i d)")
        u_sb = flat_rows.rearrange("p (g c) -> p g c", g=G)
        mag_sb = work[:, 8192:10240]
        rot_s, rot_c, angle_t = work[:, 4096:6144], work[:, 6144:8192], work[:, 3072:4096]
        w_re, w_im, z_re, z_im = [cb[:, 2048 + 512 * v:2560 + 512 * v] for v in range(4)]
        rot_t = [nat[:, 1024 + 512 * v:1536 + 512 * v] for v in range(2)]
        y_g, sq_g = [[nat[:, first + 512 * b:first + 512 * (b + 1)] for b in range(2)] for first in (2048, 3072)]
        x_s = ring[:, 8192:12288].rearrange("p (g c) -> p g c", g=G)
        y_ch = [nat[NC * b:NC * (b + 1), 0:1024].rearrange("c (s h) -> c s h", s=CH) for b in range(2)]
        par = sb("par", [P, 6, G])
        s5c = [v.rearrange("p (g h) -> p g h", g=G) for v in (cb[:, 0:1024], work[:, 4096:5120])]

        places = {"ring": ring, "work": work, "rows": flat_rows, "nat": nat}

        def weights_at(v, depth, at):
            return [places[region][:, first:first + v * depth * P].rearrange("p (v k n) -> p v k n", v=v, k=depth)
                    for region, first in at]

        def parts(name, v, depth, at):
            return [parts_at(f"{name}{b}", region, first, v * depth * P)[:].rearrange("p (v k n) -> p v k n", v=v, k=depth)
                    for b, (region, first) in enumerate(at)]

        glu_at, cout_at = [("ring", 12288), ("ring", 14336)], [("ring", 16384), ("ring", 17408)]
        glu_sb, glu_lo = weights_at(2, KD, glu_at), parts("glu_lo", 2, KD, glu_at)
        cout_sb, cout_lo = weights_at(1, KD, cout_at), parts("cout_lo", 1, KD, cout_at)
        glu_hi = parts("glu_hi", 2, KD, [("work", 8192), ("work", 4096)])
        cout_hi = parts("cout_hi", 1, KD, [("ring", 4096), ("ring", 5120)])
        fin_at, cin_at, fout_at = ([("rows", 0), ("rows", 2048)], [("work", 4096), ("rows", 0)], [("work", 4096), ("rows", 0)])
        fin_sb, fin_lo = weights_at(2, KD, fin_at), parts("fin_lo", 2, KD, fin_at)
        cin_sb, cin_lo = weights_at(3, KD, cin_at), parts("cin_lo", 3, KD, cin_at)
        fout_sb, fout_lo = weights_at(1, KF, fout_at), parts("fout_lo", 1, KF, fout_at)
        fin_hi = parts("fin_hi", 2, KD, [("nat", 0), ("nat", 2048)])
        cin_hi = parts("cin_hi", 3, KD, [("work", 7168), ("nat", 0)])
        fout_hi = parts("fout_hi", 1, KF, [("work", 6912), ("nat", 0)])
        h_lo, h_hi, gelu_hi, gelu_lo, conv_hi, conv_lo = [
            parts_at(name, region, first, KD * S)[:].rearrange("p (k t) -> p k t", k=KD)
            for name, region, first in (("h_lo", "ca", 0), ("h_hi", "cb", 0), ("gelu_hi", "ca", 0),
                                        ("gelu_lo", "cb", 0), ("conv_hi", "ring", 0), ("conv_lo", "ring", 12288))]
        f_act = ring[:, 0:KF * S].rearrange("p (f t) -> p f t", f=KF)
        f_lo, f_hi = [parts_at(name, "ring", first, KF * S)[:].rearrange("p (f t) -> p f t", f=KF)
                      for name, first in (("f_lo", 0), ("f_hi", KF * S))]
        conv_y = ring[:, 12288:16384].rearrange("p (k t) -> p k t", k=KD)
        sig_sb = [ring[:, 22528 + 512 * b:23040 + 512 * b] for b in range(2)]
        lin_t = [ring[:, 23552 + 512 * b:24064 + 512 * b] for b in range(2)]
        conv_x = nat[:, 3072:3712].rearrange("p (s c) -> p s c", c=NC)
        n_scratch = {0: [nat[:, 512 * v:512 * (v + 1)] for v in range(3)],
                     2: [flat_rows[:, 3072:3584], flat_rows[:, 3584:4096], nat[:, 3072:3584]]}
        for n in (1, 3, 4):
            n_scratch[n] = [work[:, 4096 + 512 * v:4608 + 512 * v] for v in range(3)]
        square_sum = [[work[:, 6144 + 512 * v:6656 + 512 * v] for v in range(3)], [ca[:, v, :] for v in range(3)]]
        ada1_acc = work[:, 4096:4096 + ADA_N]
        ada1_w = [work[:, 4096 + ADA_N * (b + 1):4096 + ADA_N * (b + 2)] for b in range(3)]

        hn_dram = nc.dram_tensor("hn_dram", [S, D], F32).ap()
        y_dram = nc.dram_tensor("y_dram", [E * P, D], F32).ap()
        y_more = nc.dram_tensor("y_more", [MAX_EXTRA * P, D], F32).ap()
        k_dram = nc.dram_tensor("k_dram", [GC, G, 2 * CH, GC], F32).ap()
        u_dram = nc.dram_tensor("u_dram", [D, S], F32).ap()
        b_dram = nc.dram_tensor("b_dram", [2, NS, G, GC], F32).ap()

        s_const_in = sem("const_in")
        s_x_in = sem("x_in")
        s_vec_in = sem("vec_in")
        s_pos_in = sem("pos_in")
        s_mix_in = [sem(f"mix_in{i}") for i in range(3)]
        s_ret_in = sem("ret_in")
        s_cols_ready = sem("cols_ready")
        s_s5_in = sem("s5_in")
        s_proj_ready = sem("proj_ready")
        s_score_ps = sem("score_ps")
        s_norm_in = sem("norm_in")
        s_slot_in = [sem(f"slot_in{i}") for i in range(12)]
        s_bias_in = sem("bias_in")
        s_gu_ready = sem("gu_ready")
        s_y_ready = sem("y_ready")
        s_slot_free = sem("slot_free")
        s_y_sb = sem("y_sb")
        s_wout_ready = sem("wout_ready")
        s_route_ok = sem("route_ok")
        s_moe_done = sem("moe_done")
        s_ple_in = sem("ple_in")
        s_got_used = sem("got_used")
        s_b_in = sem("b_in")
        s_c_in = sem("c_in")
        s_k_sb = sem("k_sb")
        s_k_out = sem("k_out")
        s_t_in = sem("t_in")
        s_h_ready = sem("h_ready")
        s_u_in = sem("u_in")
        s_u_out = sem("u_out")
        s_power_ok = sem("power_ok")
        s_lin_in = [[sem(f"{name}_in{b}") for b in range(2)] for name in LINEAR[:4]]
        s_lin_ready = sem("lin_ready")
        s_ada1_used = sem("ada1_used")
        s_ada1_sum = sem("ada1_sum")
        s_ada_in = [sem(f"ada_in{i}") for i in range(3)]
        s_ada1_in = [sem(f"ada1_in{i}") for i in range(3)]
        s_ada_in.append(s_ada1_in[0])
        s_x_state = sem("x_state")
        s_yo_ps = sem("yo_ps")
        s_lin_taken = sem("lin_taken")
        s_cols_taken = sem("cols_taken")
        s_out_done = sem("out_done")
        s_ada_used = sem("ada_used")
        s_slot_hot = sem("slot_hot")
        s_ids_ps = sem("ids_ps")
        s_hn_stored = sem("hn_stored")
        s_ids_cur = sem("ids_cur")
        s_xs_in = sem("xs_in")
        s_xt_ready = sem("xt_ready")
        s_got_in = [sem(f"got_in{i}") for i in range(4)]
        s_more_in = sem("more_in")
        s_pool_step = sem("pool_step")
        s_more_done = sem("more_done")
        s_b_ready = sem("b_ready")
        s_pproj_ready = sem("pproj_ready")
        s_sq = sem("sq")
        s_vec_t = sem("vec_t")
        s_vec_ok = sem("vec_ok")
        s_proj_taken = sem("proj_taken")
        s_trig_ready = sem("trig_ready")
        s_trig_done = sem("trig_done")
        s_s5_exp = sem("s5_exp")
        s_s5_angle = sem("s5_angle")
        s_s5_fun = sem("s5_fun")
        s_pool_ps = sem("pool_ps")
        s_pool_sb = sem("pool_sb")
        s_mix_ps = sem("mix_ps")
        s_mix_sb = sem("mix_sb")
        s_sil = sem("sil")
        s_y_ps = sem("y_ps")
        s_ret_y = sem("ret_y")
        s_wout_taken = sem("wout_taken")
        s_nat_ready = sem("nat_ready")
        s_gate_d = sem("gate_d")
        s_gate_e = sem("gate_e")
        s_xst_ready = sem("xst_ready")
        s_g_ready = sem("g_ready")
        s_sig_ready = sem("sig_ready")
        s_actt_ps = sem("actt_ps")
        s_actt_ready = sem("actt_ready")
        s_y_stored = sem("y_stored")
        s_more_zero = sem("more_zero")
        s_ct_ps = sem("ct_ps")
        s_ct_sb = sem("ct_sb")
        s_pgate_ready = sem("pgate_ready")
        s_pgate_act = sem("pgate_act")
        s_pproj_taken = sem("pproj_taken")
        s_sq2 = sem("sq2")
        s_sqt = sem("sqt")
        s_gu_hi = sem("gu_hi")
        s_gu_lo = sem("gu_lo")
        s_xs_hi = sem("xs_hi")
        s_bias_hi = sem("bias_hi")
        s_pick = sem("pick")
        s_bias_ok = sem("bias_ok")
        s_h_hi = sem("h_hi")
        s_h_lo = sem("h_lo")
        s_w_hi = sem("w_hi")
        s_w_lo = sem("w_lo")
        s_sq_used = sem("sq_used")
        s_hs_ready = sem("hs_ready")
        s_k_ps = sem("k_ps")
        s_rot_ready = sem("rot_ready")
        s_rot_done = sem("rot_done")
        s_yt_ps = sem("yt_ps")
        s_yo_sb = sem("yo_sb")
        s_gl_in = sem("gl_in")
        s_gl_s = sem("gl_s")
        s_lin_sig = sem("lin_sig")
        s_mods1 = sem("mods1")
        s_dve_step = sem("dve_step")
        s_ada_sum = sem("ada_sum")
        s_s5_par = sem("s5_par")
        s_s5_tr = sem("s5_tr")
        s_par_ok = sem("par_ok")
        s_rope_ready = sem("rope_ready")
        s_score_sb = sem("score_sb")
        s_ret_ready = sem("ret_ready")
        s_log_ps = sem("log_ps")
        s_mask_ready = sem("mask_ready")
        s_rank_ps = sem("rank_ps")
        s_act_ready = sem("act_ready")
        s_dve_more = sem("dve_more")
        s_dve_more2 = sem("dve_more2")
        s_more_used = sem("more_used")
        s_c_ready = sem("c_ready")
        s_ss_ps = sem("ss_ps")
        s_ws_ps = sem("ws_ps")
        s_gelu_ready = sem("gelu_ready")
        s_yt_used = sem("yt_used")

        ctx.enter_context(nc.allow_non_contiguous_dma(reason="columns of weights"))

        x_v = a["x"][0].rearrange("(i p) d -> p i d", p=P)
        w_in_v = a["w_in"][0].rearrange("(k p) n -> p k n", p=P)
        w_out_v = a["w_out"][0].rearrange("(k p) n -> p k n", p=P)
        gu_v = a["expert_w_gate_up"][0].rearrange("e (k p) n -> p e k n", p=P)
        dn_v = a["expert_w_down"][0].rearrange("e (k p) n -> p e k n", p=P)
        ple_gate_v = a["ple_gate_w"][0].rearrange("(k p) n -> p k n", p=P)
        ple_proj_v = a["ple_proj_w"][0].rearrange("(k p) n -> p k n", p=P)
        ada_v = a["w_ada_2"].rearrange("l (k p) n -> p l k n", p=P)
        hn_v = hn_dram.rearrange("(i p) d -> p i d", p=P)

        def cols_view(w):
            return w.rearrange("(k p) n -> p k n", p=P)

        linear = [
            (cb3, cols_view(a["ssm_w_out_2"][0]), (0, D), KD, glu_sb),
            (ca, cols_view(a["w_ffn_in_2"][0]), (0, FF), KF, fin_sb),
            (f_act, cols_view(a["w_ffn_out_2"][0]), (0,), KD, fout_sb),
            (ca, cols_view(a["conv_w_in_2"][0]), (0, D, 2 * D), KD, cin_sb),
            (conv_y, cols_view(a["conv_w_out_2"][0]), (0,), KD, cout_sb),
            (ca, cols_view(a["w_ffn_in_2"][1]), (0, FF), KF, fin_sb),
            (f_act, cols_view(a["w_ffn_out_2"][1]), (0,), KD, fout_sb),
        ]
        GLU, FIN0, FOUT0, CIN, COUT, FIN1, FOUT1 = range(7)
        lin_before = [16 * len(linear[n - 4][2]) * (linear[n - 4][3] // 2) if n >= 4 else 0 for n in range(len(linear))]
        fin_parts, fout_parts = (fin_hi, fin_lo, h_hi, h_lo), (fout_hi, fout_lo, f_hi, f_lo)
        split = [(glu_hi, glu_lo, gelu_hi, gelu_lo), fin_parts, fout_parts, (cin_hi, cin_lo, h_hi, h_lo),
                 (cout_hi, cout_lo, conv_hi, conv_lo), fin_parts, fout_parts]
        depth = [KF if n in (FOUT0, FOUT1) else KD for n in range(len(linear))]
        src_before = [2 * KD + sum(depth[:n]) for n in range(len(linear))]
        hi_before = [7 * KD + sum(len(x[2]) * x[3] for x in linear[:n]) for n in range(len(linear))]
        lin_base = [sum(x[3] for x in linear[:n]) for n in range(len(linear) + 1)]

        def flat(v):
            return v.rearrange("p one t -> p (one t)")

        def gu_used(eng, tile, q):
            if q % 4 == 3:
                eng.wait_ge(s_gu_ready, 2 * tile + q // 4 + 1)
            else:
                eng.wait_ge(s_slot_free, 9 * tile + q - q // 4 + 1)

        def whole(v):
            return v.bitcast(F32)

        block = ctx.enter_context(nc.Block())

        @block.sync
        def _(sp):
            def load(dst, src, done):
                sp.dma_start(dst, src).then_inc(done, 16)

            load(const[:], a["consts"], s_const_in)
            load(rows[:], x_v, s_x_in)
            for name, (r0, n) in VEC.items():
                v = a[name]
                v = v.rearrange("(r c) -> r c", c=P) if len(v.shape) == 1 else \
                    v.rearrange("l (r c) -> (l r) c", c=P) if len(v.shape) == 2 else \
                    v.rearrange("l t (r c) -> (l t r) c", c=P)
                load(vec_rows[r0:r0 + n, :], v, s_vec_in)
            load(ada_rows[0:NADA, :], a["b_ada_2"].rearrange("l (r c) -> (l r) c", c=P), s_vec_in)
            load(smi[:, 0:NT], a["positions"][0].rearrange("(i p) -> p i", p=P), s_pos_in)
            for n in range(2):
                load(w_in_sb[n], w_in_v[:, :, 512 * n:512 * (n + 1)], s_mix_in[n % 3])
            load(pool_w_sb, a["pool_w"][0].rearrange("g c d -> c g d"), s_ret_in)
            sp.wait_ge(s_cols_ready, 8)
            for v, name in enumerate(("ssm_a_re_2", "ssm_a_im_2")):
                for half in range(2):
                    load(s5r[:, v, NS * half:NS * (half + 1)], a[name][0], s_s5_in)
            load(s5r[:, 2, 0:1], a["ssm_log_step_2"][0].rearrange("(g one) -> g one", one=1), s_s5_in)
            for n in (2, 3, 4):
                sp.wait_ge(s_proj_ready, NT * (n - 1))
                load(w_in_sb[n], w_in_v[:, :, 512 * n:512 * (n + 1)], s_mix_in[n % 3])
            sp.wait_ge(s_proj_ready, NT * 4)
            load(band, a["band"].rearrange("p (g v t) -> p g v t", g=4, v=3), s_ret_in)
            sp.wait_ge(s_proj_ready, NT * 5)
            load(decay, a["decay"].rearrange("p (h t) -> p h t", h=HEADS), s_s5_in)
            for n in range(2):
                load(w_out_sb[n], w_out_v[:, :, 512 * n:512 * (n + 1)], s_mix_in[(n + 5) % 3])
            for r, part in enumerate(("re", "im")):
                sp.dma_start(b_dram[r], a[f"ssm_b_{part}_2"][0].rearrange("g n h -> n g h")).then_inc(s_b_in, 16)
            sp.wait_ge(s_score_ps, HEADS * NT)
            load(rw_sb, a["router_w"][0].rearrange("(k p) e -> p k e", p=P), s_norm_in)
            load(rb_bc, a["router_b"][0].partition_broadcast(P), s_norm_in)
            load(norm_bc, a["norm_moe_w"][0].partition_broadcast(P), s_norm_in)
            load(fnorm_bc, a["final_norm_w"].partition_broadcast(P), s_norm_in)

            def load_slot(q, expert):
                e = bass.ds(expert, 1)
                if q < 8:
                    h, k = q // 4, 2 * (q % 4)
                    src = gu_v[:, e, k:k + 2, D * h:D * (h + 1)]
                else:
                    k = 2 * (q - 8)
                    src = dn_v[:, e, k:k + 2, :]
                load(slot[q], src.rearrange("p e k n -> p (e k) n"), s_slot_in[q])

            def stream(tile, expert):
                for q in range(12):
                    if q in (3, 7):
                        sp.wait_ge(s_gu_ready, 2 * tile - 1 + q // 4)
                    elif q == 11:
                        sp.wait_ge(s_y_ready, tile)
                    else:
                        sp.wait_ge(s_slot_free, 9 * tile - 8 + q - q // 4)
                    load_slot(q, expert)

            sp.wait_ge(s_wout_ready, 2 * NT)
            for q in range(8):
                load_slot(q, 0)
            sp.wait_ge(s_hn_stored, 16)
            sp.wait_ge(s_cols_ready, COLS_ROUTE)
            for half in range(2):
                pp = slice(E * half, E * (half + 1))
                load(bias_rows[pp, 0:2 * D], a["expert_b_gate_up"][0], s_bias_in)
                load(bias_rows[pp, 2 * D:], a["expert_b_down"][0], s_bias_in)
            for q in range(8, 12):
                load_slot(q, 0)
            with sp.Fori(1, E) as e:
                stream(e, e)
            sp.wait_ge(s_route_ok, 1)
            extra = sp.value_load(smi[0:1, 72:73], min_val=0, max_val=MAX_EXTRA)
            with sp.If(extra > 0):
                with sp.Fori(0, extra) as n:
                    expert = sp.value_load(smi[0:1, bass.ds(n + 56, 1)], min_val=0, max_val=E - 1)
                    stream(n + E, expert)

            sp.wait_ge(s_gu_ready, extra * 2 + 2 * E - 1)
            load(p_rows, a["p"][0, 0].rearrange("(i p) d -> p i d", p=P), s_c_in)
            sp.wait_ge(s_b_in, 32)
            for r in range(2):
                for d in range(2):
                    part = (r + d) % 2
                    load(c_rows[r][:, :, d, :], a[f"ssm_c_{('re', 'im')[part]}_2"][0].rearrange("(t g) h n -> (g h) t n", t=8), s_c_in)
                    load(b_in[r][NS * d:NS * (d + 1)], b_dram[part], s_b_in)
            sp.wait_ge(s_gu_ready, extra * 2 + 2 * E)
            load(ple_w_sb[0], ple_gate_v[:, :, 0:512], s_c_in)
            sp.wait_ge(s_got_in[NT - 1], 16 * TOPK)
            load(ple_w_sb[1], ple_gate_v[:, :, 512:], s_ple_in)
            load(ple_p_sb, ple_proj_v, s_ple_in)

            for k in range(KD):
                sp.wait_ge(s_h_ready, k + 1)
                sp.dma_start(u_dram[P * k:P * (k + 1), :], ca[:, k, :]).then_inc(s_u_out, 16)
            sp.wait_ge(s_u_out, 16 * KD)
            u_v = u_dram.rearrange("(g h) (s c) -> s h g c", h=GC, s=CH)
            for v in range(CH):
                load(u_sb[GC * v:GC * (v + 1), :, :], u_v[v], s_u_in)

            kd = k_dram.rearrange("h g v o -> h g (v o)")
            sp.wait_ge(s_k_sb, 3)
            for v in range(CH):
                sp.dma_start(k_dram[:, :, 2 * CH - 2 - v, :], k_sb[GC * v:GC * (v + 1), :, :]).then_inc(s_k_out, 16)
            sp.dma_start(kd[:, :, 0:(CH - 1) * GC],
                         k_zero.unsqueeze(1).broadcast_to([GC, G, (CH - 1) * GC])).then_inc(s_k_out, 16)
            sp.wait_ge(s_k_out, 16 * (CH + 1))
            for v in range(CH):
                load(m_t[GC * v:GC * (v + 1), :, :], kd[:, :, (CH - 1 - v) * GC:(2 * CH - 1 - v) * GC], s_t_in)

            def load_lin(n, b, at):
                _, w, parts, _, buf = linear[n]
                for v, col in enumerate(parts):
                    load(buf[b][:, v, :, :], w[:, :, bass.ds(at * P + col, P)], s_lin_in[n % 4][b])

            def first_lin(n):
                for b in range(2):
                    load_lin(n, b, b)

            def rest_lin(n):
                with sp.Fori(0, linear[n][3] // 2 - 1) as i:
                    for b in range(2):
                        sp.wait_ge(s_lin_ready, 2 * i + lin_base[n] + b + 1)
                        load_lin(n, b, 2 * i + 2 + b)

            def feed_forward(n):
                rest_lin(n)
                sp.wait_ge(s_ada1_sum, ADA_C + 1)
                load_lin(n + 1, 0, 0)
                sp.wait_ge(s_lin_ready, lin_base[n + 1])
                load_lin(n + 1, 1, 1)
                rest_lin(n + 1)

            sp.wait_ge(s_x_state, 4)
            first_lin(GLU)
            sp.wait_ge(s_yo_ps, KD)
            first_lin(FIN0)
            rest_lin(GLU)
            feed_forward(FIN0)
            for b in range(2):
                sp.wait_ge(s_lin_ready, lin_base[CIN] - 1 + b)
                load_lin(CIN, b, b)
            first_lin(COUT)
            rest_lin(CIN)
            sp.wait_ge(s_lin_taken, lin_base[COUT] + 2)
            first_lin(FIN1)
            rest_lin(COUT)
            feed_forward(FIN1)

            out_v = out[0].rearrange("(c s) d -> s c d", s=CH)
            for i in range(NT):
                sp.wait_ge(s_cols_taken, COLS_XT + 2 * i + 2)
                for d in range(2):
                    sp.dma_start(out_v[2 * i + d], nat3[NC * d:NC * (d + 1), i, :]).then_inc(s_out_done, 16)
            sp.wait_ge(s_out_done, 16 * 2 * NT)

        @block.gpsimd
        def _(pool):
            for t in range(ADA_C * KD):
                if t >= 4:
                    pool.wait_ge(s_ada_used, t - 3)
                c, k = divmod(t, KD)
                pool.dma_start(ada_w[t % 4], ada_v[:, 0, k, ADA_N * c:ADA_N * (c + 1)]).then_inc(s_ada_in[t % 4], 16)

            ptt = pool.tensor_tensor
            for n in range(2):
                for k in range(KD):
                    pool.wait_ge(s_w_hi, KD * (n + 5) + k + 1)
                    ptt(w_out_lo[n][:, k, :], w_out_sb[n][:, k, :], whole(w_out_hi[n][:, k, :]), ALU.subtract).then_inc(s_w_lo, 1)

            step = Steps(pool, s_pool_step)
            pool.wait_ge(s_route_ok, 1)
            pool.wait_ge(s_hn_stored, 16)

            def gather(tile):
                pool.tensor_copy(smi[:, 128:129], smi[:, bass.ds(tile + 80, 1)]).then_inc(s_ids_cur, 1)
                pool.wait_ge(s_ids_cur, tile + 1)
                pool.tensor_tensor(smi[:, 129:130], smi[:, 52:53], smi[:, 52:53], ALU.add)
                pool.indirect_dma_start(
                    out=xs, out_offset=None, in_=hn_dram,
                    in_offset=bass.IndirectOffsetOnAxis(ap=smi[:, 128:129].bitcast(U32), axis=0)).then_inc(s_xs_in, 16)

            def next_tile(tile):
                pool.wait_ge(s_xs_in, 16 * tile + 16)
                pool.wait_ge(s_xt_ready, 2 * tile + 2)
                gather(tile + 1)

            gather(0)
            for r in range(2):
                step(pool.tensor_copy(power[:, r, 0, :], par[:, r, :]))
            for v in range(1, CH):
                (xr, xi), (ar, ai) = [power[:, r, v - 1, :] for r in range(2)], [par[:, r, :] for r in range(2)]
                step(ptt(p_t[0], xr, ar, ALU.mult))
                step(ptt(p_t[1], xi, ai, ALU.mult))
                step(ptt(power[:, 0, v, :], p_t[0], p_t[1], ALU.subtract))
                step(ptt(p_t[0], xr, ai, ALU.mult))
                step(ptt(p_t[1], xi, ar, ALU.mult))
                step(ptt(power[:, 1, v, :], p_t[0], p_t[1], ALU.add))
            pool.sem_inc(s_power_ok, 1)
            with pool.Fori(0, E) as e:
                next_tile(e)
            extra = pool.value_load(smi[0:1, 72:73], min_val=0, max_val=MAX_EXTRA)
            with pool.If(extra > 0):
                with pool.Fori(0, extra) as n:
                    next_tile(n + E)

            def take(source, index, done):
                for n in range(NT * TOPK):
                    pool.indirect_dma_start(
                        out=got[n], out_offset=None, in_=source,
                        in_offset=bass.IndirectOffsetOnAxis(ap=smi[:, index + n:index + n + 1].bitcast(U32), axis=0),
                    ).then_inc(done[n // TOPK], 16)

            pool.wait_ge(s_moe_done, 1)
            take(y_dram, 20, s_got_in)
            with pool.If(extra > 0):
                pool.wait_ge(s_got_used, NT)
                take(y_more, 36, [s_more_in] * NT)
            def wide(v):
                return v.unsqueeze(2).broadcast_to([P, G, GC])

            def turned(dst, x, y, z, w, op):
                step(ptt(s5_ta[0], x, wide(z), ALU.mult))
                step(ptt(s5_ta[1], y, wide(w), ALU.mult))
                step(ptt(dst, s5_ta[0], s5_ta[1], op))

            pool.wait_ge(s_b_in, 96)
            step(pool.tensor_scalar(b_in[1][0:NS], b_in[1][0:NS], -1.0, None, ALU.mult))
            pool.wait_ge(s_more_done, 1)
            bbar = m_b[:, :, CH - 1, :]
            turned(bbar, b_in[0], b_in[1], par[:, 2, :], par[:, 3, :], ALU.add)
            turned(i_bbar, b_in[1], b_in[0], par[:, 2, :], par[:, 3, :], ALU.subtract)
            pool.sem_inc(s_b_ready, 1)
            for v in range(CH - 2, -1, -1):
                turned(m_b[:, :, v, :], bbar, i_bbar, power[:, 0, CH - 2 - v, :], power[:, 1, CH - 2 - v, :], ALU.add)
            pool.sem_inc(s_b_ready, 1)
            pool.wait_ge(s_pproj_ready, 2 * NT)
            pool.memset(k_zero, 0.0).then_inc(s_k_sb, 1)
            pool.wait_ge(s_hs_ready, 2 * KD)

            def last_use(k):
                return k - 2 if k >= 3 else max(t for t in range(KD) if t % 3 == k) + 1 - KD

            def ada1_load(i, first=False):
                for k in range(KD):
                    if not (first and k < 3):
                        pool.wait_ge(s_ada1_used, KD * i + last_use(k))
                    pool.dma_start(ada1_w[k % 3], ada_v[:, 1, k, bass.ds(ADA_N * i, ADA_N)]).then_inc(s_ada1_in[k % 3], 16)

            ada1_load(0, first=True)
            with pool.Fori(1, ADA_C) as i:
                ada1_load(i)

        @block.scalar
        def _(act):
            rounds = [0]

            def column(dst, scale=None, view=None):
                r = rounds[0]
                rounds[0] += 1
                act.wait_ge(s_cols_ready, r + 1)
                src = ps[4 + r % 2][:]
                src = src if view is None else view(src)
                if scale is None:
                    act.activation(dst, src, ACT.Copy).then_inc(s_cols_taken, 1)
                else:
                    act.activation(dst, src, ACT.Copy, scale=scale).then_inc(s_cols_taken, 1)

            def squares(scrap=nat3, ready=None, before=0):
                for i in range(NT):
                    if ready:
                        act.wait_ge(ready, before + i + 1)
                    act.activation(scrap[:, i, :], rows[:, i, :], ACT.Square, accum_out=sm[:, i:i + 1]).then_inc(s_sq, 1)

            act.sem_inc(s_sqt, 1)
            act.sem_inc(s_y_sb, 1)
            act.sem_inc(s_y_stored, 16)
            act.wait_ge(s_x_in, 16)
            squares()
            act.wait_ge(s_vec_t, 1)
            act.activation(vec[:, 0:NVEC], ps[6][:, 0:NVEC], ACT.Copy).then_inc(s_vec_ok, 1)
            act.activation(vec[:, NVEC:NVEC + NADA], ps[6][:, P:P + NADA], ACT.Copy).then_inc(s_vec_ok, 1)
            act.wait_ge(s_vec_ok, 2)
            c0 = VEC["c_2"][0]
            act.activation(cact[:], vec[:, c0:c0 + 8], ACT.Sigmoid).then_inc(s_vec_ok, 1)
            def w_in_high(n):
                act.wait_ge(s_mix_in[n % 3], 16 * (n // 3 + 1))
                for k in range(KD):
                    act.activation(w_in_hi[n % 2][:, k, :], w_in_sb[n][:, k, :], ACT.Copy).then_inc(s_w_hi, 1)

            for k in range(KD):
                column(ca[:, k, :], vcol("norm_mix_w", k))
                act.wait_ge(s_cols_taken, k + 1)
                act.activation(mix_hi[:, k, :], ca[:, k, :], ACT.Copy).then_inc(s_h_hi, 1)
                if k == 0:
                    w_in_high(0)
            w_in_high(1)
            for r in range(5 * NT):
                n, i = divmod(r, NT)
                act.wait_ge(s_proj_ready, r + 1)
                act.activation(proj[:, i, 512 * n:512 * (n + 1)], ps[i][:], ACT.Copy).then_inc(s_proj_taken, 1)
                if n >= 1 and n <= 3 and i == 1:
                    w_in_high(n + 1)
                if r == 4:
                    act.wait_ge(s_trig_ready, 1)
                    act.activation(trig[:, 4:6, :, :], trig[:, 2:4, :, :], ACT.Sin).then_inc(s_trig_done, 1)
                if r == 6:
                    act.wait_ge(s_s5_in, 80)
                    act.activation(s5r[:, 2, 1:2], s5r[:, 2, 0:1], ACT.Exp).then_inc(s_s5_exp, 1)
                if r == 14:
                    act.wait_ge(s_s5_angle, 1)
                    act.activation(s5r[:, 10, :], s5r[:, 3, :], ACT.Exp).then_inc(s_s5_fun, 1)
                    act.activation(s5r[:, 24, :], s5r[:, 3, :], ACT.Exp, scale=float(CH)).then_inc(s_s5_fun, 1)
                    act.activation(s5r[:, 11, :], s5r[:, 5, :], ACT.Sin).then_inc(s_s5_fun, 1)
                    act.activation(s5r[:, 12, :], s5r[:, 9, :], ACT.Sin).then_inc(s_s5_fun, 1)
            for g in range(4):
                act.wait_ge(s_pool_ps, g + 1)
                act.activation(pooled[g % 2], ps[6][:], ACT.Copy).then_inc(s_pool_sb, 1)
                act.wait_ge(s_mix_ps, g + 1)
                act.activation(ca[:, 4 + g, :], ps[7][:], ACT.Copy, scale=vcol("pool_scale", g)).then_inc(s_mix_sb, 1)
            for k in range(KD):
                column(cb3[:, k, :])
            act.activation(silu_g, proj[:, :, 3 * RET:4 * RET], ACT.Sigmoid).then_inc(s_sil, 1)

            def mixed_high(k):
                act.activation(mixed_hi[k], ca[:, k, :], ACT.Copy).then_inc(s_h_hi, 1)

            for k in range(4, KD):
                act.wait_ge(s_mix_sb, k - 3)
                mixed_high(k)
            for n in range(2):
                act.wait_ge(s_mix_in[(n + 5) % 3], 16 * ((n + 5) // 3 + 1))
                for k in range(KD):
                    act.activation(w_out_hi[n][:, k, :], w_out_sb[n][:, k, :], ACT.Copy).then_inc(s_w_hi, 1)
            act.wait_ge(s_y_ps, HEADS)
            for i in range(NT):
                act.activation(nat[:, 512 * i:512 * (i + 1)], ps[i][:], ACT.Copy).then_inc(s_ret_y, 1)
            for k in range(4):
                column(ca[:, k, :], vcol("ret_gn_w", k))
                act.wait_ge(s_cols_taken, 2 * KD + k + 1)
                mixed_high(k)
            squares(ready=s_wout_taken, before=NT)
            act.wait_ge(s_nat_ready, 2 * NT)
            act.dma_start(hn_v, nat3).then_inc(s_hn_stored, 16)
            for k in range(KD):
                column(ca[:, k, :])
            act.wait_ge(s_gate_d, 1)
            act.activation(sm[:, 144:160], sm[:, 144:160], ACT.Exp).then_inc(s_gate_e, 1)

            def tokens_columns(tile):
                for r in range(2):
                    act.wait_ge(s_xt_ready, 2 * tile + r + 1)
                    act.activation(xs_hi[:, 4 * r:4 * r + 4, :], ps[6 + r][:].rearrange("p (k t) -> p k t", k=4),
                                   ACT.Copy).then_inc(s_xs_hi, 1)

            def weights_high(tile, q, first=False):
                act.wait_ge(s_slot_in[q], 16 * tile + 16)
                if not first:
                    gu_used(act, tile - (q < 4), (q + 4) % 8)
                act.activation(gu_hi[q % 4], slot[q], ACT.Copy).then_inc(s_gu_hi, 1)

            def pick_biases(index):
                act.activation(pick[:], pick_e[0:2 * E, bass.ds(index, 1)].broadcast_to([2 * E, P]), ACT.Copy).then_inc(s_pick, 1)

            def expert(tile, store, ahead):
                def sigmoid(h):
                    act.wait_ge(s_g_ready, 4 * tile + 2 * h + 2)
                    act.activation(t_s[h], t_g[h], ACT.Sigmoid, scale=ALPHA).then_inc(s_sig_ready, 1)

                def hidden_columns(h):
                    act.wait_ge(s_actt_ps, 2 * tile + h + 1)
                    act.activation(act_t[h], ps[2 * h][:].rearrange("p (k t) -> p k t", k=4),
                                   ACT.Copy).then_inc(s_actt_ready, 1)

                for q in range(4, 8):
                    weights_high(tile, q)
                sigmoid(0)
                if ahead:
                    weights_high(tile + 1, 0)
                    weights_high(tile + 1, 1)
                hidden_columns(0)
                sigmoid(1)
                tokens_columns(tile + 1)
                if ahead:
                    weights_high(tile + 1, 2)
                    weights_high(tile + 1, 3)
                hidden_columns(1)
                if ahead:
                    pick_biases(tile + 1)
                act.wait_ge(s_y_ready, tile + 1)
                act.wait_ge(s_y_stored, 16 * tile + 16)
                for n in range(2):
                    act.activation(y_sb[:, 512 * n:512 * (n + 1)], ps[4 + n][:], ACT.Copy).then_inc(s_y_sb, 1)
                act.wait_ge(s_y_sb, 2 * tile + 3)
                act.dma_start(store, y_sb).then_inc(s_y_stored, 16)

            pick_biases(0)
            act.wait_ge(s_bias_in, 64)
            act.activation(bias_t[0:2 * E, :], bias_rows, ACT.Copy).then_inc(s_bias_hi, 1)
            act.wait_ge(s_bias_ok, 1)
            for q in range(4):
                weights_high(0, q, first=True)
            tokens_columns(0)
            with act.Fori(0, E - 1) as e:
                expert(e, y_dram[bass.ds(e * P, P), :], True)
            expert(E - 1, y_dram[P * (E - 1):P * E, :], False)
            act.wait_ge(s_route_ok, 1)
            extra = act.value_load(smi[0:1, 72:73], min_val=0, max_val=MAX_EXTRA)
            act.wait_ge(s_y_stored, 16 * (E + 1))
            act.wait_ge(s_xst_ready, 2 * E + 2)
            with act.If(extra > 0):
                for n in range(MAX_EXTRA):
                    act.dma_start(y_more[P * n:P * (n + 1), :], rows[:, 0, :]).then_inc(s_more_zero, 16)
                act.wait_ge(s_more_zero, 16 * MAX_EXTRA)
                with act.Fori(0, extra) as n:
                    pick_biases(act.value_load(smi[0:1, bass.ds(n + 56, 1)], min_val=0, max_val=E - 1))
                    for q in range(4):
                        weights_high(n + E, q)
                    expert(n + E, y_more[bass.ds(n * P, P), :], False)
                    act.wait_ge(s_y_stored, 16 * n + 16 * (E + 2))
                    act.wait_ge(s_xst_ready, 2 * n + 2 * E + 4)
            act.sem_inc(s_moe_done, 1)

            for k in range(2):
                column(p_cols[:, k, :])
            for r in range(2):
                for q in range(2):
                    act.wait_ge(s_ct_ps, 2 * r + q + 1)
                    v = ps[q][:].rearrange("p (g h) -> p g h", h=GC)
                    for two in range(2):
                        pp = slice(NS * two, NS * (two + 1))
                        act.activation(s5c[r][pp, 32 * q:32 * (q + 1), :], v[pp, :, :], ACT.Copy,
                                       scale=(-1.0 if r or two else 1.0)).then_inc(s_ct_sb, 1)
            with act.If(extra > 0):
                act.wait_ge(s_more_done, 1)
            squares(ca_rows, s_got_used)
            for k in range(KD):
                column(ca[:, k, :], vcol("norm_ple_w", k))
            for r in range(2 * NT):
                act.wait_ge(s_pgate_ready, r + 1)
                act.activation(gate_sb[r], ps[r % 4][:], ACT.Sigmoid).then_inc(s_pgate_act, 1)
            act.wait_ge(s_rot_ready, 1)
            act.activation(rot_c, rot_c, ACT.Sin).then_inc(s_rot_done, 1)
            act.activation(rot_s, rot_s, ACT.Sin).then_inc(s_rot_done, 1)
            squares(ready=s_pproj_taken, before=NT)
            act.wait_ge(s_c_ready, 1)
            for q in range(G // 4):
                column(m_w[:, 4 * q:4 * q + 4, :].rearrange("p g m -> p (g m)"))
            for k in range(KD):
                column(xt[:, k, :].rearrange("p (s c) -> p s c", s=CH), None, lambda v: v.rearrange("p (c s) -> p s c", s=CH))
                act.wait_ge(s_cols_taken, COLS_XT - KD + k + 1)
                act.activation(ca[:, k, :], xt[:, k, :], ACT.Square).then_inc(s_sq2, 1)
            def high(n, k, hi):
                act.wait_ge(s_h_ready, KD * n + k + 1)
                act.activation(hi[:, k, :], ca[:, k, :], ACT.Copy).then_inc(s_h_hi, 1)

            def norm_shift(n, shift, hi=None):
                for k in range(KD):
                    act.wait_ge(s_hs_ready, KD * n + k + 1)
                    act.activation(ca[:, k, :], ca[:, k, :], ACT.Identity, bias=shift(k)).then_inc(s_h_ready, 1)
                    if hi is not None and k:
                        high(n, k - 1, hi)
                if hi is not None:
                    high(n, KD - 1, hi)

            norm_shift(0, lambda k: mods[:, 0, k:k + 1])
            act.wait_ge(s_k_ps, 1)
            for n in range(2):
                act.activation(k_sb[:, GP * n:GP * (n + 1), :], ps[n][:].rearrange("p (g h) -> p g h", g=GP), ACT.Copy).then_inc(s_k_sb, 1)

            def s5_rows(k):
                act.wait_ge(s_yo_ps, k + 1)
                if k >= 2:
                    act.wait_ge(s_yt_ps, k - 1)
                half = slice(NC * (k % 2), NC * (k % 2 + 1))
                for two in range(2):
                    dst = y_ch[k % 2].rearrange("c s (j g h) -> c j g s h", j=4, g=2)[:, :, two]
                    src = ps[two][half, :].rearrange("c (j s h) -> c j s h", j=4, s=CH)
                    act.activation(dst, src, ACT.Copy).then_inc(s_yo_sb, 1)

            def gelu_sigmoid(k):
                act.wait_ge(s_gl_in, k + 1)
                act.activation(sq_g[k % 2], sq_g[k % 2], ACT.Sigmoid, scale=GELU_S * GELU_C).then_inc(s_gl_s, 1)

            def gelu_high(k):
                act.wait_ge(s_gelu_ready, k + 1)
                act.activation(gelu_hi[:, k, :], cb3[:, k, :], ACT.Copy).then_inc(s_h_hi, 1)

            def weights_high(n, i, b):
                parts, buf = linear[n][2], linear[n][4]
                act.wait_ge(s_lin_in[n % 4][b], 16 * len(parts) * i + lin_before[n] + 16 * len(parts))
                for v in range(len(parts)):
                    act.activation(split[n][0][b][:, v], buf[b][:, v], ACT.Copy).then_inc(s_w_hi, 1)

            def each_tile(n, first, last=None, early=(), late=()):
                pairs = linear[n][3] // 2
                with act.Fori(0, pairs - 1) as i:
                    for b in range(2):
                        first(i, b)
                        weights_high(n, i + 1, b)
                        if last:
                            last(i, b)
                for b in early:
                    weights_high(n + 1, 0, b)
                for b in range(2):
                    first(pairs - 1, b)
                    if last:
                        last(pairs - 1, b)
                    if b in late:
                        weights_high(n + 1, 0, b)

            for k in range(0, KD, 2):
                s5_rows(k)
                s5_rows(k + 1)
                if k == KD - 2:
                    weights_high(GLU, 0, 0)
                gelu_sigmoid(k)
                gelu_sigmoid(k + 1)
                gelu_high(k)
                gelu_high(k + 1)
            weights_high(GLU, 0, 1)

            def lin_sig(n, bank, func):
                def tile(i, b):
                    act.wait_ge(s_lin_ready, 2 * i + lin_base[n] + b + 1)
                    act.activation(sig_sb[b], ps[3 * b + bank][:], func).then_inc(s_lin_sig, 1)
                return tile

            def result_high(n):
                def tile(i, b):
                    act.wait_ge(s_lin_taken, 2 * i + lin_base[n] + b + 3)
                    at = bass.ds(2 * i + b, 1)
                    act.activation(split[n + 1][2][:, at, :], linear[n + 1][0][:, at, :], ACT.Copy).then_inc(s_h_hi, 1)
                return tile

            def square(m, n):
                def tile(i, b):
                    act.wait_ge(s_lin_taken, 2 * i + lin_base[n] + b + 3)
                    act.wait_ge(s_sq_used, 2 * i + KD * m + b + 1)
                    act.activation(square_sum[m > 0][1 + b], flat(xt[:, bass.ds(2 * i + b, 1), :]), ACT.Square).then_inc(s_sqt, 1)
                return tile

            each_tile(GLU, lin_sig(GLU, 1, ACT.Sigmoid), square(0, GLU), early=(0, 1))
            norm_shift(1, lambda k: mods[:, 0, 24 + k:25 + k], h_hi)
            each_tile(FIN0, lin_sig(FIN0, 0, ACT.Sigmoid), result_high(FIN0), early=(0,), late=(1,))
            each_tile(FOUT0, square(1, FOUT0), late=(0,))
            act.wait_ge(s_mods1, 1)
            norm_shift(2, lambda k: mods[:, 1, k:k + 1], h_hi)
            weights_high(CIN, 0, 1)
            each_tile(CIN, lin_sig(CIN, 1, ACT.Copy), result_high(CIN), early=(0, 1))
            each_tile(COUT, square(2, COUT), early=(0, 1))
            norm_shift(3, lambda k: mods[:, 1, 24 + k:25 + k], h_hi)
            each_tile(FIN1, lin_sig(FIN1, 0, ACT.Sigmoid), result_high(FIN1), early=(0,), late=(1,))
            each_tile(FOUT1, square(3, FOUT1))
            for i in range(2 * NT):
                column(nat3[:, i // 2, 512 * (i % 2):512 * (i % 2 + 1)])

        @block.vector
        def _(dve):
            step = Steps(dve, s_dve_step)
            tt, ts, stt = dve.tensor_tensor, dve.tensor_scalar, dve.scalar_tensor_tensor

            def rsqrt(y, v, t):
                yi, vi = y.bitcast(I32), v.bitcast(I32)
                step(ts(yi, vi, 1, None, ALU.logical_shift_right))
                step(ts(yi, yi, -1.0, float(RSQRT_SEED), ALU.mult, ALU.add))
                for _ in range(3):
                    step(tt(t, y, y, ALU.mult))
                    step(stt(t, t, -0.5, v, ALU.mult, ALU.mult))
                    step(stt(y, t, 1.5, y, ALU.add, ALU.mult))

            def row_rstd(eps):
                step(ts(sm[:, 8:12], sm[:, 0:4], 1.0 / D, eps, ALU.mult, ALU.add))
                rsqrt(sm[:, 4:8], sm[:, 8:12], sm[:, 12:16])

            def reduce_angle(r, x, n):
                step(ts(n, x, 0.5 / PI, MAGIC, ALU.mult, ALU.add))
                step(ts(n, n, MAGIC, None, ALU.subtract))
                step(stt(r, n, -TWO_PI[0], x, ALU.mult, ALU.add))
                step(stt(r, n, -TWO_PI[1], r, ALU.mult, ALU.add))
                step(stt(r, n, -TWO_PI[2], r, ALU.mult, ALU.add))
                step(ts(r, r, PI_IN, -PI_IN, ALU.min, ALU.max))

            def cosine_angle(r2, r, m):
                step(ts(r2, r, PI / 2, None, ALU.add))
                step(ts(m, r2, PI, -2 * PI, ALU.is_gt, ALU.mult))
                step(tt(r2, r2, m, ALU.add))
                step(ts(r2, r2, PI_IN, -PI_IN, ALU.min, ALU.max))

            dve.sem_inc(s_lin_taken, 2)
            dve.sem_inc(s_sq_used, 1)

            dve.wait_ge(s_sq, NT)
            row_rstd(EPS1)
            for i in range(NT):
                ts(nat3[:, i, :], rows[:, i, :], sm[:, 4 + i:5 + i], None, ALU.mult).then_inc(s_nat_ready, 1)

            dve.wait_ge(s_const_in, 16)
            dve.wait_ge(s_pos_in, 16)
            step(dve.tensor_copy(sm[:, 192:196], smi[:, 0:NT]))
            for i in range(NT):
                step(ts(trig[:, 0, i, :], freq, sm[:, 192 + i:193 + i], None, ALU.mult))
            reduce_angle(trig[:, 2], trig[:, 0], trig[:, 1])
            cosine_angle(trig[:, 3], trig[:, 2], trig[:, 1])
            dve.sem_inc(s_trig_ready, 1)

            dve.wait_ge(s_vec_ok, 3)
            c0 = VEC["c_2"][0]
            step(tt(cact[:], cact[:], vec[:, c0:c0 + 8], ALU.mult))

            def ada_tile(acc, w, k):
                if k == 0:
                    return ts(acc, w, cact[:, 0:1], None, ALU.mult)
                return stt(acc, w, cact[:, k:k + 1], acc, ALU.mult, ALU.add)

            def ada_chunk(c):
                for k in range(KD):
                    t = KD * c + k
                    dve.wait_ge(s_ada_in[t % 4], 16 * (t // 4 + 1))
                    if k == 0 and c >= 2:
                        dve.wait_ge(s_ada_sum, c - 1)
                    ada_tile(ada_acc[c % 2], ada_w[t % 4], k).then_inc(s_ada_used, 1)
                    dve.wait_ge(s_ada_used, t + 1)

            def finish_mods(layer):
                step(tt(mods[:, layer, :], ps[7][:, 0:48], vec[:, NVEC + 48 * layer:NVEC + 48 * (layer + 1)], ALU.add))
                for h, name in enumerate(("norm1_g_2", "norm2_g_2")):
                    g0 = VEC[name][0] + 8 * layer
                    step(stt(scale1[:, layer, 8 * h:8 * (h + 1)], mods[:, layer, 24 * h + 8:24 * h + 16], 1.0,
                             vec[:, g0:g0 + 8], ALU.add, ALU.mult))

            def w_in_low(n):
                for k in range(KD):
                    dve.wait_ge(s_w_hi, KD * n + k + 1)
                    tt(w_in_lo[n % 2][:, k, :], w_in_sb[n][:, k, :], whole(w_in_hi[n % 2][:, k, :]), ALU.subtract).then_inc(s_w_lo, 1)

            w_in_low(0)
            for k in range(KD):
                dve.wait_ge(s_h_hi, k + 1)
                tt(mix_lo[:, k, :], ca[:, k, :], whole(mix_hi[:, k, :]), ALU.subtract).then_inc(s_h_lo, 1)
            q = [s5r[:, n, :] for n in range(32)]
            ada_chunk(0)
            w_in_low(1)
            ada_chunk(1)
            ada_chunk(2)
            w_in_low(2)
            ada_chunk(3)
            dve.wait_ge(s_s5_exp, 1)
            dt = s5r[:, 2, 1:2]
            step(ts(q[0], q[0], -1e-4, None, ALU.min))
            step(ts(q[3], q[0], dt, None, ALU.mult))
            step(ts(q[4], q[1], dt, None, ALU.mult))
            reduce_angle(q[5], q[4], q[6])
            step(ts(q[7], q[5], float(CH), None, ALU.mult))
            reduce_angle(q[25], q[7], q[6])
            cosine_angle(q[9], q[5], q[6])
            dve.sem_inc(s_s5_angle, 1)
            w_in_low(3)
            ada_chunk(4)
            ada_chunk(5)
            w_in_low(4)
            ada_chunk(6)
            ada_chunk(7)
            dve.wait_ge(s_ada_sum, ADA_C)
            finish_mods(0)
            dve.wait_ge(s_s5_fun, 4)
            step(tt(q[20], q[10], q[12], ALU.mult))
            step(tt(q[21], q[10], q[11], ALU.mult))
            step(tt(q[13], q[0], q[0], ALU.mult))
            step(tt(q[14], q[1], q[1], ALU.mult))
            step(tt(q[13], q[13], q[14], ALU.add))
            step(dve.reciprocal(q[13], q[13]))
            step(ts(q[14], q[20], -1.0, None, ALU.add))
            step(tt(q[15], q[14], q[0], ALU.mult))
            step(tt(q[16], q[21], q[1], ALU.mult))
            step(tt(q[15], q[15], q[16], ALU.add))
            step(tt(q[22], q[15], q[13], ALU.mult))
            step(tt(q[15], q[21], q[0], ALU.mult))
            step(tt(q[16], q[14], q[1], ALU.mult))
            step(tt(q[15], q[15], q[16], ALU.subtract))
            step(tt(q[23], q[15], q[13], ALU.mult))
            dve.sem_inc(s_s5_par, 1)
            dve.wait_ge(s_s5_tr, 1)
            step(dve.tensor_copy(par[:], ps[6][:, 0:6 * G].rearrange("p (v g) -> p v g", v=6)))
            dve.sem_inc(s_par_ok, 1)

            dve.wait_ge(s_proj_taken, 2 * NT)
            dve.wait_ge(s_trig_done, 1)
            for i in range(NT):
                x = proj[:, i, 0:2 * RET].rearrange("p (h two f) -> p h two f", h=2 * HEADS, two=2)
                sh = [P, 2 * HEADS, 32]
                sin, cos = [trig[:, v, i, :].unsqueeze(1).broadcast_to(sh) for v in (4, 5)]
                x1, x2 = x[:, :, 0, :], x[:, :, 1, :]
                t0, t1 = rope_t
                step(tt(t0, x1, cos, ALU.mult))
                step(tt(t1, x2, sin, ALU.mult))
                step(tt(qkr[:, i, :, 0, :], t0, t1, ALU.subtract))
                step(tt(t0, x2, cos, ALU.mult))
                step(tt(t1, x1, sin, ALU.mult))
                step(tt(qkr[:, i, :, 1, :], t0, t1, ALU.add))
                dve.sem_inc(s_rope_ready, 1)

            def mixed_low(n):
                k = MIXED[n]
                dve.wait_ge(s_h_hi, KD + n + 1)
                tt(mixed_lo[:, k, :], ca[:, k, :], whole(mixed_hi[k]), ALU.subtract).then_inc(s_h_lo, 1)

            dve.wait_ge(s_s5_in, 96)
            for h in range(HEADS):
                for j in range(NT):
                    n = S - P * j
                    dve.wait_ge(s_score_ps, NT * h + j + 1)
                    if h >= 2 and j == 0:
                        dve.wait_ge(s_y_ps, h - 1)
                    tt(scr_s[h % 2][:, SCORE_AT[j]:SCORE_AT[j] + n], ps[4 + j][:, 0:n], decay[:, h, 0:n],
                       ALU.mult).then_inc(s_score_sb, 1)
                if h == 3:
                    for n in range(4):
                        mixed_low(n)
                if h == 5:
                    dve.wait_ge(s_sil, 1)
                    step(tt(silu_g, silu_g, proj[:, :, 3 * RET:4 * RET], ALU.mult))
            dve.wait_ge(s_ret_y, NT)
            nh = NT * HEADS
            mu, var, rs, nt = [sm[:, 16 + nh * v:16 + nh * (v + 1)] for v in range(4)]
            wide = [P, nh, HD]
            step(dve.tensor_reduce(mu, ret_y, AXX, ALU.add))
            step(ts(mu, mu, 1.0 / HD, None, ALU.mult))
            step(tt(ret_y, ret_y, mu.unsqueeze(2).broadcast_to(wide), ALU.subtract))
            step(tt(ret_sq, ret_y, ret_y, ALU.mult))
            step(dve.tensor_reduce(var, ret_sq, AXX, ALU.add))
            step(ts(var, var, 1.0 / HD, EPS1, ALU.mult, ALU.add))
            rsqrt(rs, var, nt)
            step(tt(ret_y, ret_y, rs.unsqueeze(2).broadcast_to(wide), ALU.mult))
            step(tt(nat[:, 0:2048], nat[:, 0:2048], silu_g.rearrange("p k t -> p (k t)"), ALU.mult))
            dve.sem_inc(s_ret_ready, 1)
            for n in range(4, KD):
                mixed_low(n)

            for r in range(2 * NT):
                n, i = divmod(r, NT)
                dve.wait_ge(s_wout_ready, r + 1)
                v = rows[:, i, 512 * n:512 * (n + 1)]
                tt(v, v, ps[i][:], ALU.add).then_inc(s_wout_taken, 1)

            dve.wait_ge(s_sq, 2 * NT)
            row_rstd(EPS1)
            dve.wait_ge(s_norm_in, 64)
            for i in range(NT):
                stt(nat3[:, i, :], rows[:, i, :], sm[:, 4 + i:5 + i], norm_bc, ALU.mult, ALU.mult).then_inc(s_nat_ready, 1)

            at = [0]

            def scratch_of(*shape):
                n = 1
                for d in shape:
                    n *= d
                v = route[:, at[0]:at[0] + n]
                at[0] += n
                if len(shape) == 2:
                    v = v.rearrange("p (a b) -> p a b", a=shape[0])
                if len(shape) == 3:
                    v = v.rearrange("p (a b c) -> p a b c", a=shape[0], b=shape[1])
                return v

            logits, hot, prod = scratch_of(NT, E), scratch_of(NT, TOPK, E), scratch_of(NT, TOPK, E)
            mask, rank, over, tile, tmp = [scratch_of(NT, E) for _ in range(5)]
            count, need, total, base = [scratch_of(E) for _ in range(4)]
            ext = scratch_of(MAX_EXTRA + 1, E)
            ext_e, pick_t, pick_r, where = scratch_of(MAX_EXTRA + 1), scratch_of(16), scratch_of(16), scratch_of(16)
            assert at[0] <= 5120
            dve.wait_ge(s_log_ps, 1)
            step(tt(logits, ps[6][:, 0:NT * E].rearrange("p (i e) -> p i e", i=NT),
                    rb_bc.unsqueeze(1).broadcast_to([P, NT, E]), ALU.add))
            top = sm[:, 112:144].rearrange("p (i k) -> p i k", i=NT)
            idx = smi[:, 178:210].rearrange("p (i k) -> p i k", i=NT).bitcast(U32)
            gates = sm[:, 144:160].rearrange("p (i k) -> p i k", i=NT)
            idxf = sm[:, 192:208].rearrange("p (i k) -> p i k", i=NT)
            for i in range(NT):
                step(dve.max(top[:, i, :], logits[:, i, :]))
                step(dve.max_index(idx[:, i, :], top[:, i, :], logits[:, i, :]))
                step(ts(gates[:, i, :], top[:, i, 0:TOPK], top[:, i, 0:1], None, ALU.subtract))
            dve.sem_inc(s_gate_d, 1)
            step(dve.tensor_copy(idxf, idx[:, :, 0:TOPK]))
            for i in range(NT):
                for k in range(TOPK):
                    step(ts(hot[:, i, k, :], iota[:, 0:E], idxf[:, i, k:k + 1], None, ALU.is_equal))
            step(dve.tensor_reduce(mask, hot.rearrange("p i k e -> p i e k"), AXX, ALU.add))
            dve.sem_inc(s_mask_ready, 1)
            dve.wait_ge(s_bias_hi, 1)
            tt(bias_t[E:2 * E, :], bias_rows[E:2 * E, :], whole(bias_t[E:2 * E, :]), ALU.subtract).then_inc(s_bias_ok, 1)
            dve.wait_ge(s_rank_ps, 1)
            step(dve.tensor_copy(rank, ps[7][:, 0:NT * E].rearrange("p (i e) -> p i e", i=NT)))
            step(dve.tensor_copy(count, ps[7][:, NT * E:NT * E + E]))

            def tiles_before(dst, v, limit):
                t = tmp if len(dst.shape) == 3 else base
                step(ts(dst, v, float(limit), None, ALU.is_ge))
                for m in (1, 2):
                    step(ts(t, v, float(P * m + limit), None, ALU.is_ge))
                    step(tt(dst, dst, t, ALU.add))

            tiles_before(need, count, P + 1)
            step(dve.tensor_tensor_scan(total, ones[:, 0:E], need, 0.0, ALU.mult, ALU.add))
            step(tt(base, total, need, ALU.subtract))
            tiles_before(over, rank, P)
            wide = [P, NT, E]
            iota_b = iota[:, 0:E].unsqueeze(1).broadcast_to(wide)
            step(ts(base, base, float(E - 1), None, ALU.add))
            step(tt(tile, over, base.unsqueeze(1).broadcast_to(wide), ALU.add))
            step(tt(tile, tile, iota_b, ALU.subtract))
            step(ts(tmp, over, 0.0, None, ALU.is_gt))
            step(tt(tile, tile, tmp, ALU.mult))
            step(tt(tile, tile, iota_b, ALU.add))
            step(stt(rank, over, -float(P), rank, ALU.mult, ALU.add))
            for pick, v in ((pick_t, tile), (pick_r, rank)):
                step(tt(prod, hot, v.unsqueeze(2).broadcast_to([P, NT, TOPK, E]), ALU.mult))
                step(dve.tensor_reduce(pick.rearrange("p (i k) -> p i k", i=NT), prod, AXX, ALU.add))
            for n in range(NT * TOPK):
                i = n // TOPK
                ts(row_hot[:, n, :], iota, pick_r[:, n:n + 1], None, ALU.is_equal).then_inc(s_slot_hot, 1)
                ts(tile_token[:, n, :], iota[:, 0:TILES], pick_t[:, n:n + 1], token[:, i:i + 1], ALU.is_equal,
                   ALU.mult).then_inc(s_slot_hot, 1)
            step(dve.tensor_copy(smi[:, 52:56], token))
            step(ts(ext_e, pick_t, float(E), None, ALU.is_ge))
            step(stt(where, pick_t, float(P), pick_r, ALU.mult, ALU.add))
            more, main = sm[:, 176:192], sm[:, 160:176]
            step(stt(prod[:, 0, 0, 0:16], where, -float(E * P), ext_e, ALU.add, ALU.mult))
            step(dve.tensor_copy(smi[:, 36:52], prod[:, 0, 0, 0:16]))
            step(ts(prod[:, 0, 1, 0:16], ext_e, -1.0, 1.0, ALU.mult, ALU.add))
            step(tt(where, where, prod[:, 0, 1, 0:16], ALU.mult))
            step(dve.tensor_copy(smi[:, 20:36], where))
            dve.wait_ge(s_gate_e, 1)
            step(dve.tensor_reduce(sm[:, 12:16], gates, AXX, ALU.add))
            step(dve.reciprocal(sm[:, 12:16], sm[:, 12:16]))
            step(tt(gates, gates, sm[:, 12:16].unsqueeze(2).broadcast_to([P, NT, TOPK]), ALU.mult))
            step(tt(more, sm[:, 144:160], ext_e, ALU.mult))
            step(tt(main, sm[:, 144:160], more, ALU.subtract))
            nx = MAX_EXTRA + 1
            step(tt(ext, total.unsqueeze(1).broadcast_to([P, nx, E]),
                    iota[:, 0:nx].unsqueeze(2).broadcast_to([P, nx, E]), ALU.is_le))
            step(dve.tensor_reduce(ext_e, ext, AXX, ALU.add))
            step(ts(ext_e, ext_e, float(E - 1), None, ALU.min))
            step(dve.tensor_copy(smi[:, 56:72], ext_e))
            step(dve.tensor_copy(smi[:, 72:73], total[:, E - 1:E]))
            dve.wait_ge(s_ids_ps, 1)
            step(dve.tensor_copy(smi[:, 80:80 + TILES], ps[6][:, 0:TILES]))
            dve.sem_inc(s_route_ok, 1)

            def swiglu(tile, h):
                dve.wait_ge(s_gu_ready, 2 * tile + h + 1)
                v = [ps[2 * h + n][:].rearrange("p (f two) -> p f two", two=2) for n in range(2)]
                g, u = [[t[:, 256 * n:256 * (n + 1)] for n in range(2)] for t in (t_g[h], t_u[h])]
                for n in range(2):
                    ts(g[n], v[n][:, :, 0], LIMIT, None, ALU.min).then_inc(s_g_ready, 1)
                for n in range(2):
                    step(ts(u[n], v[n][:, :, 1], LIMIT, -LIMIT, ALU.min, ALU.max))
                dve.wait_ge(s_g_ready, 4 * tile + 2 * h + 2)
                step(stt(t_u[h], t_u[h], 1.0, t_g[h], ALU.add, ALU.mult))
                dve.wait_ge(s_sig_ready, 2 * tile + h + 1)
                tt(act_n[h], t_u[h], t_s[h], ALU.mult).then_inc(s_act_ready, 1)

            def weights_low(tile, q):
                dve.wait_ge(s_gu_hi, 8 * tile + q + 1)
                tt(gu_lo[:, q], slot[q], whole(gu_hi[q % 4]), ALU.subtract).then_inc(s_gu_lo, 1)

            def tokens_low(tile):
                for r in range(2):
                    dve.wait_ge(s_xs_hi, 2 * tile + r + 1)
                    v = slice(4 * r, 4 * r + 4)
                    tt(xs_lo[:, v, :], ps[6 + r][:].rearrange("p (k t) -> p k t", k=4), whole(xs_hi[:, v, :]),
                       ALU.subtract).then_inc(s_xst_ready, 1)

            def expert(tile, ahead):
                for q in range(4, 8):
                    weights_low(tile, q)
                swiglu(tile, 0)
                if ahead:
                    weights_low(tile + 1, 0)
                    weights_low(tile + 1, 1)
                swiglu(tile, 1)
                tokens_low(tile + 1)
                if ahead:
                    weights_low(tile + 1, 2)
                    weights_low(tile + 1, 3)

            for q in range(3):
                weights_low(0, q)
            tokens_low(0)
            weights_low(0, 3)
            per = 2 * 3
            n0 = step.n
            with dve.Fori(0, E - 1) as e:
                step.n, step.off = n0, e * per
                expert(e, True)
                assert step.n == n0 + per
            step.n, step.off = n0, (E - 1) * per
            expert(E - 1, False)
            n0 += E * per
            extra = dve.value_load(smi[0:1, 72:73], min_val=0, max_val=MAX_EXTRA)
            with dve.If(extra > 0):
                main_step, step = step, Steps(dve, s_dve_more)
                with dve.Fori(0, extra) as n:
                    step.n, step.off = 0, n * per
                    for q in range(4):
                        weights_low(n + E, q)
                    expert(n + E, False)
                step = main_step
            step.n, step.off = n0, 0

            def combine(i, weights, done):
                for k in range(TOPK):
                    n = TOPK * i + k
                    ins = stt(rows[:, i, :], got[n], weights[:, n:n + 1], rows[:, i, :], ALU.mult, ALU.add)
                    if k < TOPK - 1:
                        step(ins)
                    else:
                        ins.then_inc(done, 1)

            for i in range(NT):
                dve.wait_ge(s_got_in[i], 16 * TOPK)
                combine(i, main, s_got_used)
            with dve.If(extra > 0):
                main_step, step = step, Steps(dve, s_dve_more2)
                dve.wait_ge(s_got_used, NT)
                dve.wait_ge(s_more_in, 16 * NT * TOPK)
                for i in range(NT):
                    combine(i, more, s_more_used)
                dve.wait_ge(s_more_used, NT)
                step = main_step
            dve.wait_ge(s_got_used, NT)
            dve.sem_inc(s_more_done, 1)

            dve.wait_ge(s_sq, 3 * NT)
            row_rstd(EPS1)
            for i in range(NT):
                ts(nat3[:, i, :], rows[:, i, :], sm[:, 4 + i:5 + i], None, ALU.mult).then_inc(s_nat_ready, 1)
            dve.wait_ge(s_ct_sb, 8)
            dve.wait_ge(s_power_ok, 1)
            dve.wait_ge(s_b_ready, 1)
            for v in range(CH):
                ar, ai = [power[:, r, v, :].unsqueeze(2).broadcast_to([P, G, GC]) for r in range(2)]
                step(tt(s5_tb[0], s5c[0], ar, ALU.mult))
                step(tt(s5_tb[1], s5c[1], ai, ALU.mult))
                step(tt(m_c[:, :, v, :], s5_tb[0], s5_tb[1], ALU.add))
            dve.sem_inc(s_c_ready, 1)
            rot_s3, mag3 = [v.rearrange("p (j c) -> p j c", j=GP) for v in (rot_s, mag_sb)]
            half = [NS, GP, NC]
            for two in range(2):
                pp = slice(NS * two, NS * (two + 1))
                step(tt(rot_s3[pp], par[pp, 5, two:G:2].unsqueeze(2).broadcast_to(half),
                        iota[pp, 0:NC].unsqueeze(1).broadcast_to(half), ALU.mult))
            for v in range(2):
                at = slice(1024 * v, 1024 * (v + 1))
                reduce_angle(rot_s[:, at], rot_s[:, at], angle_t)
                cosine_angle(rot_c[:, at], rot_s[:, at], angle_t)
            dve.sem_inc(s_rot_ready, 1)
            for r in range(2 * NT):
                n, i = divmod(r, NT)
                dve.wait_ge(s_pgate_act, r + 1)
                dve.wait_ge(s_pproj_ready, r + 1)
                step(tt(gate_sb[r], gate_sb[r], ps[4 + r % 4][:], ALU.mult))
                v = rows[:, i, 512 * n:512 * (n + 1)]
                tt(v, v, gate_sb[r], ALU.add).then_inc(s_pproj_taken, 1)
            dve.wait_ge(s_sq, 4 * NT)
            row_rstd(EPS1)
            for i in range(NT):
                stt(nat3[:, i, :], rows[:, i, :], sm[:, 4 + i:5 + i], fnorm_bc, ALU.mult, ALU.mult).then_inc(s_nat_ready, 1)

            for two in range(2):
                pp = slice(NS * two, NS * (two + 1))
                step(dve.tensor_copy(mag3[pp], par[pp, 4, two:G:2].unsqueeze(2).broadcast_to(half)))
            step(dve.memset(mag3[:, :, 0:1], 0.0))

            def low(n, k, hi):
                dve.wait_ge(s_h_hi, src_before[(None, FIN0, CIN, FIN1)[n]] + k + 1)
                tt(h_lo[:, k, :], ca[:, k, :], whole(hi[:, k, :]), ALU.subtract).then_inc(s_h_lo, 1)

            def norm(n, scale, hi=None):
                v, n_y, n_t = n_scratch[n]
                dve.wait_ge(s_ss_ps, n + 1)
                step(ts(v, ps[6][:], 1.0 / D, EPS2, ALU.mult, ALU.add))
                rsqrt(n_y, v, n_t)
                for k in range(KD):
                    stt(ca[:, k, :], xt[:, k, :], scale(k), n_y, ALU.mult, ALU.mult).then_inc(s_hs_ready, 1)
                if hi is not None:
                    for k in range(KD):
                        low(n, k, hi)

            norm(0, lambda k: scale1[:, 0, k:k + 1])

            def recurrence(b):
                dve.wait_ge(s_ws_ps, b + 1)
                at = slice(512 * b, 512 * (b + 1))
                c, sn, (t1, t2) = rot_c[:, at], rot_s[:, at], rot_t
                wr, wi = ps[2 * b][:], ps[2 * b + 1][:]
                step(tt(t1, wr, c, ALU.mult))
                step(tt(t2, wi, sn, ALU.mult))
                step(tt(z_re, t1, t2, ALU.add))
                step(tt(t1, wi, c, ALU.mult))
                step(tt(t2, wr, sn, ALU.mult))
                step(tt(z_im, t1, t2, ALU.subtract))
                if b == 0:
                    dve.wait_ge(s_k_out, 16 * (CH + 1))
                step(dve.tensor_tensor_scan(w_re, mag_sb[:, at], z_re, 0.0, ALU.mult, ALU.add))
                step(dve.tensor_tensor_scan(w_im, mag_sb[:, at], z_im, 0.0, ALU.mult, ALU.add))

                def later(r, op):
                    zv, wv = [v.rearrange("p (j c) -> p j c", c=NC)[:, :, 0:NC - 1] for v in (z_re, z_im)]
                    for two in range(2):
                        pp = slice(NS * two, NS * (two + 1))
                        step(tt(x_s[NS * r:NS * (r + 1), 16 * b + two:16 * (b + 1):2, 1:NC], zv[pp], wv[pp], op))

                step(dve.memset(x_s[:, 16 * b:16 * (b + 1), 0:1], 0.0))
                step(tt(z_re, w_re, c, ALU.mult))
                step(tt(z_im, w_im, sn, ALU.mult))
                later(0, ALU.subtract)
                step(tt(z_re, w_re, sn, ALU.mult))
                step(tt(z_im, w_im, c, ALU.mult))
                later(1, ALU.add)
                dve.sem_inc(s_x_state, 1)

            def gelu_low(k):
                dve.wait_ge(s_h_hi, src_before[GLU] + k + 1)
                tt(gelu_lo[:, k, :], cb3[:, k, :], whole(gelu_hi[:, k, :]), ALU.subtract).then_inc(s_h_lo, 1)

            def weights_low(n, i, b):
                parts, buf = linear[n][2], linear[n][4]
                for v in range(len(parts)):
                    dve.wait_ge(s_w_hi, 2 * len(parts) * i + hi_before[n] + len(parts) * b + v + 1)
                    tt(split[n][1][b][:, v], buf[b][:, v], whole(split[n][0][b][:, v]), ALU.subtract).then_inc(s_w_lo, 1)

            def gelu(first):
                tiles = [(k, y_g[k % 2], sq_g[k % 2]) for k in (first, first + 1)]
                for k, y, sq in tiles:
                    dve.wait_ge(s_yt_ps, k + 1)
                    if first:
                        dve.wait_ge(s_gelu_ready, k - 1)
                    stt(y, ca[:, k, :], vcol("ssm_d_2", k), ps[2 + k % 2][:], ALU.mult, ALU.add).then_inc(s_yt_used, 1)
                    dve.wait_ge(s_yt_used, k + 1)
                    step(tt(sq, y, y, ALU.mult))
                    stt(sq, sq, 1.0 / GELU_C, y, ALU.add, ALU.mult).then_inc(s_gl_in, 1)
                if first == KD - 2:
                    weights_low(GLU, 0, 0)
                for k, y, sq in tiles:
                    dve.wait_ge(s_gl_s, k + 1)
                    tt(cb3[:, k, :], y, sq, ALU.mult).then_inc(s_gelu_ready, 1)
                for k, _, _ in tiles:
                    gelu_low(k)

            dve.wait_ge(s_rot_done, 2)
            recurrence(0)
            for b in range(1, 4):
                recurrence(b)
                gelu(2 * b - 2)
            gelu(KD - 2)
            weights_low(GLU, 0, 1)

            def each_tile(n, per, body, last=None, extra=None, extras=0, early=(), late=()):
                n0 = step.n
                pairs = linear[n][3] // 2

                def pair(i, peeled=False, extra=None):
                    step.n, step.off = n0, i * per
                    for b in range(2):
                        dve.wait_ge(s_lin_taken, 2 * i + b + lin_base[n] + 2)
                        body(i, b, 2 * i + b, bass.ds(2 * i + b, 1))
                        if extra:
                            extra(i, b)
                        if not peeled:
                            weights_low(n, i + 1, b)
                        if last:
                            last(2 * i + b, bass.ds(2 * i + b, 1))
                        if peeled and b in late:
                            weights_low(n + 1, 0, b)
                    assert step.n == n0 + per

                if extra:
                    with dve.Fori(0, extras) as i:
                        pair(i, extra=extra)
                with dve.Fori(extras, pairs - 1) as i:
                    pair(i)
                for b in early:
                    weights_low(n + 1, 0, b)
                pair(pairs - 1, peeled=True)
                step.n, step.off = n0 + per * pairs, 0

            sig_n = {GLU: 0, FIN0: KD, CIN: KD + KF, FIN1: 2 * KD + KF}

            def clear_squares(m):
                step(dve.memset(square_sum[m > 0][0], 0.0))
                step(dve.memset(square_sum[m > 0][2], 0.0))

            def add_square(m, i, b):
                dve.wait_ge(s_sqt, 2 * i + KD * m + b + 1)
                dve.wait_ge(s_sq_used, 2 * i + KD * m + b + 1)
                acc = square_sum[m > 0][0]
                tt(acc, acc, square_sum[m > 0][2 - b], ALU.add).then_inc(s_sq_used, 1)

            def glu(i, b, t, at):
                dve.wait_ge(s_lin_sig, t + sig_n[GLU] + 1)
                step(stt(lin_t[b], ps[3 * b][:], mods[:, 0, bass.ds(2 * i + 16 + b, 1)], sig_sb[b], ALU.mult, ALU.mult))
                x = flat(xt[:, at, :])
                tt(x, x, lin_t[b], ALU.add).then_inc(s_lin_taken, 1)
                add_square(0, i, b)

            def hidden(n):
                def body(i, b, t, at):
                    dve.wait_ge(s_lin_sig, t + sig_n[n] + 1)
                    step(tt(lin_t[b], ps[3 * b][:], sig_sb[b], ALU.mult))
                    tt(flat(f_act[:, at, :]), ps[3 * b + 1][:], lin_t[b], ALU.mult).then_inc(s_lin_taken, 1)
                return body

            def result_low(n):
                hi, lo = split[n + 1][2:]

                def tile(t, at):
                    dve.wait_ge(s_h_hi, t + src_before[n + 1] + 1)
                    tt(flat(lo[:, at, :]), flat(linear[n + 1][0][:, at, :]), whole(flat(hi[:, at, :])),
                       ALU.subtract).then_inc(s_h_lo, 1)
                return tile

            def residual(m, n, layer, gate):
                def body(i, b, t, at):
                    dve.wait_ge(s_lin_ready, t + lin_base[n] + 1)
                    x = flat(xt[:, at, :])
                    stt(x, ps[3 * b][:], mods[:, layer, bass.ds(2 * i + gate + b, 1)], x, ALU.mult,
                        ALU.add).then_inc(s_lin_taken, 1)
                    add_square(m, i, b)
                return body

            def ada1_half(i, b):
                for k in range(KD // 2 * b, KD // 2 * (b + 1)):
                    total = sum(1 for u in range(KD) if u % 3 == k % 3)
                    before = 0 if k % 3 else 16 * (ADA_C * KD // 4)
                    dve.wait_ge(s_ada1_in[k % 3], 16 * total * i + before + 16 * (k // 3 + 1))
                    if k == 0:
                        dve.wait_ge(s_ada1_sum, i + 1)
                    ada_tile(ada1_acc, ada1_w[k % 3], k).then_inc(s_ada1_used, 1)
                    dve.wait_ge(s_ada1_used, KD * i + k + 1)

            cx = conv_x.rearrange("p s c -> p (s c)")

            def conv(i, b, t, at):
                def w(tap):
                    return vec[:, bass.ds(2 * i + VEC["conv_w_2"][0] + KD * tap + b, 1)]

                dve.wait_ge(s_lin_sig, t + sig_n[CIN] + 1)
                step(tt(cx[:, 2 * NC:], ps[3 * b + 2][:], sig_sb[b], ALU.mult))
                step(dve.tensor_copy(conv_x[:, 0:2, 1:NC], conv_x[:, CH:CH + 2, 0:NC - 1]))
                step(ts(lin_t[b], cx[:, 0:S], w(0), None, ALU.mult))
                step(stt(lin_t[b], cx[:, NC:NC + S], w(1), lin_t[b], ALU.mult, ALU.add))
                step(stt(lin_t[b], cx[:, 2 * NC:], w(2), lin_t[b], ALU.mult, ALU.add))
                tt(flat(conv_y[:, at, :]), lin_t[b], ps[3 * b][:], ALU.mult).then_inc(s_lin_taken, 1)

            clear_squares(0)
            each_tile(GLU, 2, glu, early=(0, 1))
            norm(1, lambda k: scale1[:, 0, 8 + k:9 + k], h_hi)
            each_tile(FIN0, 2, hidden(FIN0), result_low(FIN0), ada1_half, ADA_C, early=(0,), late=(1,))
            dve.wait_ge(s_ada1_sum, ADA_C + 1)
            finish_mods(1)
            dve.sem_inc(s_mods1, 1)
            clear_squares(1)
            each_tile(FOUT0, 0, residual(1, FOUT0, 0, 40), late=(0,))
            norm(2, lambda k: scale1[:, 1, k:k + 1], h_hi)
            weights_low(CIN, 0, 1)
            step(dve.memset(conv_x[:, 0:2, 0:1], 0.0))
            each_tile(CIN, 10, conv, result_low(CIN), early=(0, 1))
            clear_squares(2)
            each_tile(COUT, 0, residual(2, COUT, 1, 16), early=(0, 1))
            norm(3, lambda k: scale1[:, 1, 8 + k:9 + k], h_hi)
            each_tile(FIN1, 2, hidden(FIN1), result_low(FIN1), early=(0,), late=(1,))
            clear_squares(3)
            each_tile(FOUT1, 0, residual(3, FOUT1, 1, 40))
            norm(4, lambda k: vcol("final_g_2", k))

        @block.tensor
        def _(pe):
            mm = pe.matmul
            pe.sem_inc(s_ada1_sum, 1)
            rounds = [0]

            def column(tiles):
                r = rounds[0]
                rounds[0] += 1
                if r >= 2:
                    pe.wait_ge(s_cols_taken, r - 1)
                at = 0
                for src in tiles:
                    n = src.shape[0]
                    m = src.free_size()
                    last = pe.transpose(ps[4 + r % 2][0:m, at:at + n], src, ident[0:n, 0:n])
                    at += n
                last.then_inc(s_cols_ready, 1)

            def columns_of(v, tiles=KD):
                for k in range(tiles):
                    column([v[:, i, P * k:P * (k + 1)] for i in range(NT)])

            pe.wait_ge(s_const_in, 16)
            pe.wait_ge(s_vec_in, 16 * (len(VEC) + 1))
            pe.transpose(ps[6][:, 0:NVEC], vec_rows[0:NVEC, :], ident[0:NVEC, 0:NVEC])
            pe.transpose(ps[6][:, P:P + NADA], ada_rows[0:NADA, :], ident[0:NADA, 0:NADA]).then_inc(s_vec_t, 1)
            pe.wait_ge(s_nat_ready, NT)
            columns_of(nat3)
            def ada_sum(layer, c, acc, done, wait):
                wait()
                for t in range(ADA_N // P):
                    last = mm(ps[7][:, c * (ADA_N // P) + t:c * (ADA_N // P) + t + 1], acc[:, P * t:P * (t + 1)],
                              ones[:, 0:1], start=True, stop=True)
                last.then_inc(done, 1)

            pe.wait_ge(s_cols_taken, KD)
            for r in range(5 * NT):
                n, i = divmod(r, NT)
                if i == 0:
                    pe.wait_ge(s_w_lo, KD * (n + 1))
                if r >= NT:
                    pe.wait_ge(s_proj_taken, r - NT + 1)
                tokens, w_hi, w_lo = slice(P * i, P * (i + 1)), w_in_hi[n % 2], w_in_lo[n % 2]
                for k in range(KD):
                    if r == 0:
                        pe.wait_ge(s_h_lo, k + 1)
                    mm(ps[i][:], mix_hi[:, k, tokens], w_hi[:, k, :], start=(k == 0), stop=False)
                    mm(ps[i][:], mix_hi[:, k, tokens], w_lo[:, k, :], start=False, stop=False)
                    last = mm(ps[i][:], mix_lo[:, k, tokens], w_hi[:, k, :], start=False, stop=(k == KD - 1))
                last.then_inc(s_proj_ready, 1)
                c = r // 2 - 2
                if r % 2 == 0 and 0 <= c < ADA_C:
                    ada_sum(0, c, ada_acc[c % 2], s_ada_sum, lambda: pe.wait_ge(s_ada_used, KD * (c + 1)))
            pe.wait_ge(s_s5_par, 1)
            pe.wait_ge(s_vec_ok, 2)
            for v in range(6):
                last = pe.transpose(ps[6][:, G * v:G * (v + 1)], s5r[:, 20 + v, :], ident[0:G, 0:G])
            last.then_inc(s_s5_tr, 1)
            pe.wait_ge(s_proj_taken, 5 * NT)
            pe.wait_ge(s_ret_in, 32)
            pe.wait_ge(s_par_ok, 1)
            for g in range(4):
                if g >= 1:
                    pe.wait_ge(s_pool_sb, g)
                for i in range(NT):
                    def u(j):
                        return proj[:, j, 4 * RET + P * g:4 * RET + P * (g + 1)]

                    dst = ps[6][:, P * i:P * (i + 1)]
                    last = mm(dst, u(i), band[:, g, min(i, 1), :], start=True, stop=(i == 0))
                    if i:
                        last = mm(dst, u(i - 1), band[:, g, 2, :], start=False, stop=True)
                last.then_inc(s_pool_ps, 1)
                pe.wait_ge(s_pool_sb, g + 1)
                if g >= 1:
                    pe.wait_ge(s_mix_sb, g)
                mm(ps[7][:], pool_w_sb[:, g, :], pooled[g % 2], start=True, stop=True).then_inc(s_mix_ps, 1)
            pe.wait_ge(s_rope_ready, NT)
            columns_of(nat3)
            pe.wait_ge(s_cols_taken, 2 * KD)
            pe.wait_ge(s_mix_sb, 4)

            def scores(h):
                pp = slice(HD * (h % 2), HD * (h % 2 + 1))
                for j in range(NT):
                    if h >= 1:
                        pe.wait_ge(s_score_sb, NT * (h - 1) + j + 1)
                    mm(ps[4 + j][:, 0:S - P * j], cb3[pp, 4 + h // 2, P * j:P * (j + 1)], cb3[pp, h // 2, P * j:S],
                       start=True, stop=True).then_inc(s_score_ps, 1)

            def values(h):
                pe.wait_ge(s_score_sb, NT * (h + 1))
                for i in range(NT):
                    for j in range(i + 1):
                        at = SCORE_AT[j] + P * (i - j)
                        last = mm(ps[i][:, HD * h:HD * (h + 1)], scr_s[h % 2][:, at:at + P],
                                  proj[:, j, 2 * RET + HD * h:2 * RET + HD * (h + 1)], start=(j == 0), stop=(j == i))
                last.then_inc(s_y_ps, 1)

            scores(0)
            for h in range(HEADS):
                if h + 1 < HEADS:
                    scores(h + 1)
                values(h)
            def mixer_out(n, i, first, end):
                tokens = slice(P * i, P * (i + 1))
                for t in range(first, end):
                    k = MIXED[t]
                    if n == 0 and i == 0:
                        pe.wait_ge(s_h_lo, KD + t + 1)
                    mm(ps[i][:], mixed_hi[k][:, tokens], w_out_hi[n][:, k, :], start=(t == 0), stop=False)
                    mm(ps[i][:], mixed_hi[k][:, tokens], w_out_lo[n][:, k, :], start=False, stop=False)
                    last = mm(ps[i][:], mixed_lo[:, k, tokens], w_out_hi[n][:, k, :], start=False, stop=(t == KD - 1))
                return last

            pe.wait_ge(s_ret_y, NT)
            pe.wait_ge(s_w_lo, 7 * KD)
            for i in range(NT):
                mixer_out(0, i, 0, KD // 2)
            pe.wait_ge(s_ret_ready, 1)
            columns_of(nat[:].rearrange("p (two i d) -> p two i d", two=2, i=NT)[:, 0], 4)
            for i in range(NT):
                mixer_out(0, i, KD // 2, KD).then_inc(s_wout_ready, 1)
            for i in range(NT):
                pe.wait_ge(s_wout_taken, i + 1)
                mixer_out(1, i, 0, KD).then_inc(s_wout_ready, 1)
            pe.wait_ge(s_nat_ready, 2 * NT)
            columns_of(nat3)
            pe.wait_ge(s_norm_in, 64)
            pe.wait_ge(s_cols_taken, 3 * KD + 4)
            for i in range(NT):
                for k in range(KD):
                    last = mm(ps[6][:, E * i:E * (i + 1)], ca[:, k, P * i:P * (i + 1)], rw_sb[:, k, :],
                              start=(k == 0), stop=(k == KD - 1))
            last.then_inc(s_log_ps, 1)
            pe.wait_ge(s_mask_ready, 1)
            mask = route[:, MASK_AT:MASK_AT + NT * E].rearrange("p (i e) -> p i e", i=NT)
            for i in range(NT):
                for j in range(i):
                    mm(ps[7][:, E * i:E * (i + 1)], ones, mask[:, j, :], start=(j == 0), stop=False)
                mm(ps[7][:, E * i:E * (i + 1)], tri, mask[:, i, :], start=(i == 0), stop=True)
            for j in range(NT):
                last = mm(ps[7][:, E * NT:E * (NT + 1)], ones, mask[:, j, :], start=(j == 0), stop=(j == NT - 1))
            last.then_inc(s_rank_ps, 1)
            for n in range(NT * TOPK):
                pe.wait_ge(s_slot_hot, 2 * n + 2)
                last = mm(ps[6][:, 0:TILES], row_hot[:, n, :], tile_token[:, n, :], start=(n == 0), stop=(n == NT * TOPK - 1))
            last.then_inc(s_ids_ps, 1)
            pe.wait_ge(s_route_ok, 1)

            def tokens_columns(tile):
                pe.wait_ge(s_xs_in, 16 * tile + 16)
                for r in range(2):
                    for k in range(4):
                        last = pe.transpose(ps[6 + r][:, P * k:P * (k + 1)], xs[:, P * (4 * r + k):P * (4 * r + k + 1)], ident)
                    last.then_inc(s_xt_ready, 1)

            def hidden_columns(tile, h):
                pe.wait_ge(s_act_ready, 2 * tile + h + 1)
                for k in range(4):
                    last = pe.transpose(ps[2 * h][:, P * k:P * (k + 1)], act_n[h][:, P * k:P * (k + 1)], ident)
                last.then_inc(s_actt_ps, 1)

            def biases(at, bank):
                for n in range(2):
                    mm(ps[bank + n][:], pick[:], bias_t[0:2 * E, at + 512 * n:at + 512 * (n + 1)], start=True, stop=False)

            def up(tile, h):
                biases(D * h, 2 * h)
                for k in range(KD):
                    q = 4 * h + k // 2
                    if k % 2 == 0:
                        pe.wait_ge(s_gu_lo, 8 * tile + q + 1)
                    hi, lo = gu_hi[q % 4][:, k % 2], gu_lo[:, q, k % 2]
                    for x, w in ((xs_hi, hi), (xs_lo, hi), (xs_hi, lo)):
                        for n in range(2):
                            last = mm(ps[2 * h + n][:], x[:, k, :], w[:, 512 * n:512 * (n + 1)],
                                      start=False, stop=(k == KD - 1 and w is lo))
                    if k % 2 and k < KD - 1:
                        last.then_inc(s_slot_free, 1)
                last.then_inc(s_gu_ready, 1)

            def down(tile, h):
                pe.wait_ge(s_actt_ready, 2 * tile + h + 1)
                if h == 0:
                    pe.wait_ge(s_y_sb, 2 * tile + 1)
                    biases(2 * D, 4)
                for k in range(4):
                    q = 8 + 2 * h + k // 2
                    if k % 2 == 0:
                        pe.wait_ge(s_slot_in[q], 16 * tile + 16)
                    for n in range(2):
                        last = mm(ps[4 + n][:], act_t[h][:, k, :], slot[q][:, k % 2, 512 * n:512 * (n + 1)],
                                  start=False, stop=(h == 1 and k == 3))
                    if k % 2 and not (h and k == 3):
                        last.then_inc(s_slot_free, 1)
                if h:
                    last.then_inc(s_y_ready, 1)

            def expert(tile):
                pe.wait_ge(s_pick, tile + 1)
                pe.wait_ge(s_xst_ready, 2 * tile + 2)
                up(tile, 0)
                up(tile, 1)
                hidden_columns(tile, 0)
                tokens_columns(tile + 1)
                down(tile, 0)
                hidden_columns(tile, 1)
                down(tile, 1)

            tokens_columns(0)
            pe.wait_ge(s_bias_ok, 1)
            with pe.Fori(0, E) as e:
                expert(e)
            extra = pe.value_load(smi[0:1, 72:73], min_val=0, max_val=MAX_EXTRA)
            with pe.If(extra > 0):
                with pe.Fori(0, extra) as n:
                    expert(n + E)

            pe.wait_ge(s_c_in, 96)
            pe.wait_ge(s_moe_done, 1)
            columns_of(p_rows, 2)
            for r in range(2):
                for q in range(2):
                    if r:
                        pe.wait_ge(s_ct_sb, 2 * q + 2)
                    for t in range(4):
                        last = pe.transpose(ps[q][:, P * t:P * (t + 1)], c_rows[r][:, 4 * q + t].rearrange("p two n -> p (two n)"), ident)
                    last.then_inc(s_ct_ps, 1)
            pe.wait_ge(s_nat_ready, 3 * NT)
            columns_of(nat3)
            pe.wait_ge(s_cols_taken, COLS_PLE)
            pe.wait_ge(s_ct_sb, 8)
            for r in range(2 * NT):
                n, i = divmod(r, NT)
                if r >= NT:
                    pe.wait_ge(s_ple_in, 32)
                    pe.wait_ge(s_pgate_act, r - NT + 1)
                for k in range(KD):
                    last = mm(ps[i][:], ca[:, k, P * i:P * (i + 1)], ple_w_sb[n][:, k, :], start=(k == 0), stop=(k == KD - 1))
                last.then_inc(s_pgate_ready, 1)
            for r in range(2 * NT):
                n, i = divmod(r, NT)
                if r >= NT:
                    pe.wait_ge(s_pproj_taken, r - NT + 1)
                for k in range(2):
                    last = mm(ps[4 + i][:], p_cols[:, k, P * i:P * (i + 1)], ple_p_sb[:, k, 512 * n:512 * (n + 1)],
                              start=(k == 0), stop=(k == 1))
                last.then_inc(s_pproj_ready, 1)
            pe.wait_ge(s_b_ready, 2)
            pe.wait_ge(s_pproj_taken, 2 * NT - 2)
            for q in range(G // 4):
                column([m_b[:, 4 * q + j].rearrange("p s h -> p (s h)") for j in range(4)])
            pe.wait_ge(s_nat_ready, 4 * NT)
            for k in range(KD + 1):
                if k < KD:
                    column([nat3[:, i, P * k:P * (k + 1)] for i in range(NT)])
                if k >= 1:
                    pe.wait_ge(s_sq2, k)
                    last = mm(ps[6][:], ones, ca[:, k - 1, :], start=(k == 1), stop=(k == KD))
            last.then_inc(s_ss_ps, 1)

            def norm_sums(n):
                pe.wait_ge(s_sq_used, KD * n + 1)
                mm(ps[6][:], ones, square_sum[n > 1][0], start=True, stop=False)
                pe.wait_ge(s_sqt, KD * n + 1)
                mm(ps[6][:], ones, square_sum[n > 1][2], start=False, stop=True).then_inc(s_ss_ps, 1)

            pe.wait_ge(s_pgate_act, 2 * NT)
            for g in range(G):
                last = mm(ps[g // GP][:, GC * (g % GP):GC * (g % GP + 1)], m_b[:, g].rearrange("p s h -> p (s h)"),
                          s5c[0][:, g, :], start=True, stop=True)
            last.then_inc(s_k_ps, 1)
            pe.wait_ge(s_u_in, 16 * CH)
            pe.wait_ge(s_hs_ready, KD)
            pe.wait_ge(s_cols_taken, COLS_XT)
            pe.wait_ge(s_k_sb, 3)
            for b in range(4):
                for r in range(2):
                    for j in range(8 * b, 8 * b + 8):
                        for two in range(2):
                            pp = slice(NS * two, NS * (two + 1))
                            last = mm(ps[2 * b + r][pp, NC * (j % 8):NC * (j % 8 + 1)], m_w[:, 2 * j + two, NS * r:NS * (r + 1)], u_sb[:, 2 * j + two, :],
                                      start=True, stop=True)
                last.then_inc(s_ws_ps, 1)
            pe.wait_ge(s_t_in, 16 * CH)
            pe.wait_ge(s_c_ready, 1)

            def chunk_rows(k):
                pe.wait_ge(s_x_state, k // 2 + 1)
                if k >= 2:
                    pe.wait_ge(s_yo_sb, 2 * k - 2)
                half = slice(NC * (k % 2), NC * (k % 2 + 1))
                for j in range(4 * k, 4 * k + 4):
                    for two in range(2):
                        dst = ps[two][half, P * (j % 4):P * (j % 4 + 1)]
                        mm(dst, u_sb[:, 2 * j + two, :], m_t[:, 2 * j + two, :], start=True, stop=False)
                        last = mm(dst, x_s[:, 2 * j + two, :], m_c[:, 2 * j + two].rearrange("p s h -> p (s h)"), start=False, stop=True)
                last.then_inc(s_yo_ps, 1)

            def chunk_columns(k):
                pe.wait_ge(s_yo_sb, 2 * k + 2)
                if k == 0:
                    pe.wait_ge(s_x_state, 2)
                if k >= 2:
                    pe.wait_ge(s_yt_used, k - 1)
                half = slice(NC * (k % 2), NC * (k % 2 + 1))
                for v in range(CH):
                    last = pe.transpose(ps[2 + k % 2][:, NC * v:NC * (v + 1)], y_ch[k % 2][:, v, :], ident[half, half])
                last.then_inc(s_yt_ps, 1)

            for k in range(0, KD, 2):
                chunk_rows(k)
                chunk_rows(k + 1)
                chunk_columns(k)
                chunk_columns(k + 1)

            def products(n, extra=None, extras=0):
                _, _, parts, tiles, _ = linear[n]
                w_hi, w_lo, x_hi, x_lo = split[n]

                def tile(i, b, first=False):
                    pe.wait_ge(s_w_lo, 2 * len(parts) * i + hi_before[n] + len(parts) * (b + 1))
                    pe.wait_ge(s_lin_taken, 2 * i + lin_base[n] + b + 1)
                    for k in range(depth[n]):
                        if first:
                            pe.wait_ge(s_h_hi, src_before[n] + k + 1)
                        for v in range(len(parts)):
                            mm(ps[3 * b + v][:], w_hi[b][:, v, k, :], x_hi[:, k, :], start=(k == 0), stop=False)
                            mm(ps[3 * b + v][:], w_lo[b][:, v, k, :], x_hi[:, k, :], start=False, stop=False)
                    for k in range(depth[n]):
                        if first:
                            pe.wait_ge(s_h_lo, src_before[n] + k + 1)
                        for v in range(len(parts)):
                            last = mm(ps[3 * b + v][:], w_hi[b][:, v, k, :], x_lo[:, k, :], start=False, stop=(k == depth[n] - 1))
                    last.then_inc(s_lin_ready, 1)

                for b in range(2):
                    tile(0, b, first=(b == 0))
                if extra:
                    with pe.Fori(1, extras + 1) as i:
                        tile(i, 0)
                        extra(i - 1)
                        tile(i, 1)
                with pe.Fori(extras + 1, tiles // 2) as i:
                    for b in range(2):
                        tile(i, b)

            def ada1_sum(i):
                pe.wait_ge(s_ada1_used, KD * i + KD)
                per = ADA_N // P
                for t in range(per):
                    last = mm(ps[7][:, bass.ds(per * i + t, 1)], ada1_acc[:, P * t:P * (t + 1)], ones[:, 0:1],
                              start=True, stop=True)
                last.then_inc(s_ada1_sum, 1)

            products(GLU)
            norm_sums(1)
            products(FIN0, ada1_sum, ADA_C)
            products(FOUT0)
            norm_sums(2)
            products(CIN)
            products(COUT)
            norm_sums(3)
            products(FIN1)
            products(FOUT1)
            norm_sums(4)
            for i in range(NT):
                for h in range(2):
                    pe.wait_ge(s_hs_ready, 4 * KD + 4 * h + 4)
                    column([ca[:, 4 * h + k, P * i:P * (i + 1)] for k in range(4)])


def _constants():
    import numpy as np

    consts = np.zeros((P, NCONST), np.float32)

    def put(name, value):
        lo, hi = CONST[name]
        consts[:, lo:hi] = value

    t = np.arange(P)
    put("ident", np.eye(P))
    put("ones", 1.0)
    put("tri", t[:, None] < t[None, :])
    put("iota", t[None, :])
    put("freq", (10000.0 ** (-np.arange(32) / 32.0))[None, :])
    put("token", t[:, None] + P * np.arange(NT)[None, :])
    put("pick", t[:, None] % E == np.arange(E)[None, :])
    gamma = np.log1p(-(2.0 ** (-5.0 - np.arange(HEADS))))
    lag = np.arange(S)[None, :] - t[:, None]
    decay = np.where(lag[:, None, :] >= 0, np.exp(np.maximum(lag, 0)[:, None, :] * gamma[None, :, None]), 0.0)
    decay = (decay * HD ** -0.5).astype(np.float32).reshape(P, HEADS * S)
    band = np.zeros((P, len(WINDOWS), 3, P), np.float32)
    for g, w in enumerate(WINDOWS):
        back = t[None, :] - t[:, None]
        inside = (back >= 0) & (back < w)
        band[:, g, 0] = inside / np.minimum(t + 1, w)[None, :] - np.eye(P)
        band[:, g, 1] = inside / w - np.eye(P)
        band[:, g, 2] = (back + P < w) / w
    return {"consts": consts, "decay": decay, "band": band.reshape(P, -1)}


_INS = ["x", "p", "positions", "w_in", "w_out", "ret_gn_w", "pool_w", "pool_scale", "norm_mix_w", "norm_moe_w",
        "router_w", "router_b", "expert_w_gate_up", "expert_b_gate_up", "expert_w_down", "expert_b_down",
        "norm_ple_w", "ple_gate_w", "ple_proj_w", "final_norm_w", "c_2", "norm1_g_2", "norm2_g_2", "w_ada_2",
        "b_ada_2", "ssm_a_re_2", "ssm_a_im_2", "ssm_log_step_2", "ssm_b_re_2", "ssm_b_im_2", "ssm_c_re_2",
        "ssm_c_im_2", "ssm_d_2", "ssm_w_out_2", "conv_w_in_2", "conv_w_2", "conv_w_out_2", "w_ffn_in_2",
        "w_ffn_out_2", "final_g_2"]


def kernel(**inputs):
    import numpy as np
    import concourse.bacc as bacc
    from concourse.bass_utils import run_bass_kernel_spmd

    nc = bacc.Bacc("TRN2", target_bir_lowering=False, num_devices=1)
    arrays = {name: np.ascontiguousarray(inputs[name]) for name in _INS}
    arrays.update(_constants())
    aps = {name: nc.dram_tensor(f"in_{name}", v.shape, mybir.dt.from_np(v.dtype), kind="ExternalInput").ap()
           for name, v in arrays.items()}
    out = nc.dram_tensor("out", (1, S, D), F32, kind="ExternalOutput").ap()
    program(nc, aps, out)
    got = run_bass_kernel_spmd(nc, [{f"in_{name}": v for name, v in arrays.items()}], core_ids=[0])
    return got.results[0]["out"]
```
